# Optimizing a Trainium2 kernel written in Bass

```python
import jax, jax.numpy as jnp
from jax import lax
import numpy as np

D_MODEL = 1024
BATCH = 1
SEQ = 1024
DEPTH = 1

GRID_W = 64
N_MEM = 256
HEAD_DIM = 64
NA_HEADS = 8
NA_WIDTH = NA_HEADS * HEAD_DIM
NA_KH = 8
NA_KW = 16
RW_HEADS = 4
RW_WIDTH = RW_HEADS * HEAD_DIM
RW_LORA_W = 64
RW_LORA_A = 64
RW_LORA_G = 128
RW_PROJ = 3 * RW_WIDTH + 2 * RW_LORA_W + 2 * RW_LORA_A + RW_LORA_G
MEM_HEADS = 4
MEM_WIDTH = MEM_HEADS * HEAD_DIM
D_MIX = NA_WIDTH + RW_WIDTH + MEM_WIDTH
P_IN = 3 * NA_WIDTH + RW_PROJ + MEM_WIDTH
MOE_GROUPS = 4
MOE_EXPERTS_PER_GROUP = 4
MOE_EXPERTS = MOE_GROUPS * MOE_EXPERTS_PER_GROUP
MOE_TOP_K = 2
MOE_D_FF = 512
MOE_BLOCK = 128
RMS_EPS = 1e-6
RW_GN_EPS = 64e-5

kernel_name = 'hybrid_natten_rwkv7_hmoe_encoder'

def rms_norm(x, w):
    xf = x.astype(jnp.float32)
    y = xf * lax.rsqrt(jnp.mean(xf * xf, axis=-1, keepdims=True) + RMS_EPS)
    return (y * w.astype(jnp.float32)).astype(x.dtype)

def neighborhood_attention(q, k, v, rpb):
    B, S, H, dh = q.shape
    rows = S // GRID_W
    kh = min(NA_KH, rows)
    col = np.arange(GRID_W)
    col_start = np.clip(col - NA_KW // 2, 0, GRID_W - NA_KW)
    col_idx = col_start[:, None] + np.arange(NA_KW)[None, :]
    dc = col_idx - col[:, None]
    qg = q.reshape(B, rows, GRID_W, H, dh)
    kg = k.reshape(B, rows, GRID_W, H, dh)
    vg = v.reshape(B, rows, GRID_W, H, dh)
    scale = HEAD_DIM ** -0.5

    def one_row(r):
        rs = jnp.clip(r - kh // 2, 0, rows - kh)
        k_rows = lax.dynamic_slice_in_dim(kg, rs, kh, axis=1)
        v_rows = lax.dynamic_slice_in_dim(vg, rs, kh, axis=1)
        k_nb = k_rows[:, :, col_idx]
        v_nb = v_rows[:, :, col_idx]
        q_r = lax.dynamic_index_in_dim(qg, r, axis=1, keepdims=False)
        dr = rs + jnp.arange(kh) - r
        bias = rpb[:, dr[:, None, None] + NA_KH - 1, dc[None, :, :] + NA_KW - 1]
        s = jnp.einsum('bqhd,bnqmhd->bhqnm', q_r, k_nb).astype(jnp.float32) * scale
        s = s + jnp.transpose(bias, (0, 2, 1, 3)).astype(jnp.float32)[None]
        p = jax.nn.softmax(s.reshape(B, H, GRID_W, kh * NA_KW), axis=-1)
        p = p.reshape(B, H, GRID_W, kh, NA_KW).astype(v.dtype)
        return jnp.einsum('bhqnm,bnqmhd->bqhd', p, v_nb)

    out = lax.map(one_row, jnp.arange(rows))
    return jnp.transpose(out, (1, 0, 2, 3, 4)).reshape(B, S, H * dh)

def centred_shift(s, mu_prev, mu_next):
    prev = jnp.pad(s, ((0, 0), (1, 0), (0, 0)))[:, :-1]
    nxt = jnp.pad(s, ((0, 0), (0, 1), (0, 0)))[:, 1:]
    return s + mu_prev * (prev - s) + mu_next * (nxt - s)

def wkv7_scan(r, w, k, v, kk, a, reverse):
    B, S, H, N = r.shape

    def step(state, inp):
        r_t, w_t, k_t, v_t, kk_t, a_t = inp
        sa = jnp.einsum('bhvk,bhk->bhv', state, -kk_t)
        state = (state * w_t[:, :, None, :]
                 + sa[..., None] * (kk_t * a_t)[:, :, None, :]
                 + v_t[..., None] * k_t[:, :, None, :])
        return state, jnp.einsum('bhvk,bhk->bhv', state, r_t)

    xs = tuple(jnp.swapaxes(t, 0, 1) for t in (r, w, k, v, kk, a))
    state0 = jnp.zeros((B, H, N, N), jnp.float32)
    _, y = lax.scan(step, state0, xs, reverse=reverse)
    return jnp.swapaxes(y, 0, 1)

def rwkv7_bidirectional(rw, mu_prev, mu_next, w0, w2, a0, a2, g2, k_k, k_a, r_k, ln_w, ln_b):
    f32 = jnp.float32
    B, S, _ = rw.shape
    rw = centred_shift(rw.astype(f32), mu_prev.astype(f32), mu_next.astype(f32))
    splits = [RW_WIDTH, 2 * RW_WIDTH, 3 * RW_WIDTH,
              3 * RW_WIDTH + RW_LORA_W, 3 * RW_WIDTH + 2 * RW_LORA_W,
              3 * RW_WIDTH + 2 * RW_LORA_W + RW_LORA_A,
              3 * RW_WIDTH + 2 * RW_LORA_W + 2 * RW_LORA_A]
    r, k, v, lw_f, lw_b, la_f, la_b, lg = jnp.split(rw, splits, axis=-1)
    w0, w2, a0, a2, g2 = (t.astype(f32) for t in (w0, w2, a0, a2, g2))

    def heads(t):
        return t.reshape(B, S, RW_HEADS, HEAD_DIM)

    g = jax.nn.sigmoid(lg) @ g2
    kk = heads(k * k_k.astype(f32))
    kk = kk / jnp.maximum(jnp.sqrt(jnp.sum(kk * kk, axis=-1, keepdims=True)), 1e-12)
    rh, vh = heads(r), heads(v)
    ys = []
    kds = []
    for d, (lw, la, rev) in enumerate(((lw_f, la_f, False), (lw_b, la_b, True))):
        wl = -jax.nn.softplus(-(w0[d] + jnp.tanh(lw) @ w2[d])) - 0.5
        decay = jnp.exp(-jnp.exp(wl))
        a = jax.nn.sigmoid(a0[d] + la @ a2[d])
        kd = k * (1.0 + (a - 1.0) * k_a.astype(f32))
        ys.append(wkv7_scan(rh, heads(decay), heads(kd), vh, kk, heads(a), rev))
        kds.append(kd)
    y = ys[0] + ys[1]
    mu = jnp.mean(y, axis=-1, keepdims=True)
    var = jnp.mean((y - mu) ** 2, axis=-1, keepdims=True)
    yn = ((y - mu) * lax.rsqrt(var + RW_GN_EPS)).reshape(B, S, RW_WIDTH)
    yn = yn * ln_w.astype(f32) + ln_b.astype(f32)
    bonus = jnp.sum(rh * heads(kds[0] + kds[1]) * r_k.astype(f32), axis=-1, keepdims=True) * vh
    return (yn + bonus.reshape(B, S, RW_WIDTH)) * g

def memory_cross_attention(mq, mem_n, w_mem_kv, q_norm_w, k_norm_w):
    B, S, _ = mq.shape
    M = mem_n.shape[1]
    q = rms_norm(mq.reshape(B, S, MEM_HEADS, HEAD_DIM), q_norm_w)
    k, v = jnp.split(mem_n @ w_mem_kv, 2, axis=-1)
    k = rms_norm(k.reshape(B, M, MEM_HEADS, HEAD_DIM), k_norm_w)
    v = v.reshape(B, M, MEM_HEADS, HEAD_DIM)
    s = jnp.einsum('bshd,bmhd->bhsm', q, k).astype(jnp.float32) * (HEAD_DIM ** -0.5)
    p = jax.nn.softmax(s, axis=-1).astype(v.dtype)
    return jnp.einsum('bhsm,bmhd->bshd', p, v).reshape(B, S, MEM_WIDTH)

def hybrid_mixer(h, mem_n, w_in, na_q_norm_w, na_k_norm_w, na_rpb,
                 rw_mu_prev, rw_mu_next, rw_w0, rw_w2, rw_a0, rw_a2, rw_g2,
                 rw_k_k, rw_k_a, rw_r_k, rw_ln_w, rw_ln_b,
                 w_mem_kv, mem_q_norm_w, mem_k_norm_w, w_out):
    B, S, _ = h.shape
    proj = h @ w_in
    na_qkv, rw, mq = jnp.split(proj, [3 * NA_WIDTH, 3 * NA_WIDTH + RW_PROJ], axis=-1)
    q, k, v = [t.reshape(B, S, NA_HEADS, HEAD_DIM) for t in jnp.split(na_qkv, 3, axis=-1)]
    q = rms_norm(q, na_q_norm_w)
    k = rms_norm(k, na_k_norm_w)
    y_na = neighborhood_attention(q, k, v, na_rpb)
    y_rw = rwkv7_bidirectional(rw, rw_mu_prev, rw_mu_next, rw_w0, rw_w2, rw_a0, rw_a2, rw_g2,
                               rw_k_k, rw_k_a, rw_r_k, rw_ln_w, rw_ln_b).astype(h.dtype)
    y_mem = memory_cross_attention(mq, mem_n, w_mem_kv, mem_q_norm_w, mem_k_norm_w)
    return jnp.concatenate([y_na, y_rw, y_mem], axis=-1) @ w_out

def hierarchical_moe(h, w_group, b_group, w_expert, b_expert, w_gate, w_up, w_down):
    B, S, D = h.shape
    n = B * S
    h2 = h.reshape(n, D)
    f32 = jnp.float32
    glogits = (h2 @ w_group).astype(f32) + b_group.astype(f32)
    g_idx = jnp.argmax(glogits, axis=-1)
    g_w = jnp.take_along_axis(jax.nn.softmax(glogits, axis=-1), g_idx[:, None], axis=1)[:, 0]
    elogits = ((h2 @ w_expert).astype(f32) + b_expert.astype(f32)).reshape(n, MOE_GROUPS, MOE_EXPERTS_PER_GROUP)
    sel = jnp.take_along_axis(elogits, g_idx[:, None, None], axis=1)[:, 0]
    top_p, top_i = lax.top_k(jax.nn.softmax(sel, axis=-1), MOE_TOP_K)
    top_p = top_p / jnp.sum(top_p, axis=-1, keepdims=True)
    weights = g_w[:, None] * top_p
    expert = g_idx[:, None] * MOE_EXPERTS_PER_GROUP + top_i
    nk = n * MOE_TOP_K
    flat_e = expert.reshape(-1).astype(jnp.int32)
    flat_w = weights.reshape(-1)
    flat_t = jnp.repeat(jnp.arange(n, dtype=jnp.int32), MOE_TOP_K)
    order = jnp.argsort(flat_e)
    se, st, sw = flat_e[order], flat_t[order], flat_w[order]
    counts = jnp.bincount(flat_e, length=MOE_EXPERTS).astype(jnp.int32)
    starts = jnp.cumsum(counts) - counts
    padded = (counts + MOE_BLOCK - 1) // MOE_BLOCK * MOE_BLOCK
    pends = jnp.cumsum(padded)
    pstarts = pends - padded
    dest = pstarts[se] + jnp.arange(nk, dtype=jnp.int32) - starts[se]
    n_blocks = -(-nk // MOE_BLOCK) + MOE_EXPERTS
    cap = n_blocks * MOE_BLOCK
    tok_buf = jnp.zeros((cap,), jnp.int32).at[dest].set(st)
    w_buf = jnp.zeros((cap,), h2.dtype).at[dest].set(sw.astype(h2.dtype))
    block_start = jnp.arange(n_blocks, dtype=jnp.int32) * MOE_BLOCK
    block_e = jnp.clip(jnp.searchsorted(pends, block_start, side='right'), 0, MOE_EXPERTS - 1)

    def run_block(args):
        e, toks, wts = args
        xb = h2[toks]
        hid = jax.nn.silu(xb @ w_gate[e]) * (xb @ w_up[e])
        return (hid @ w_down[e]) * wts[:, None]

    out = lax.map(run_block, (block_e, tok_buf.reshape(n_blocks, MOE_BLOCK),
                              w_buf.reshape(n_blocks, MOE_BLOCK)))
    y = jnp.zeros((n, D), h2.dtype).at[tok_buf].add(out.reshape(cap, D))
    return y.reshape(B, S, D)

def setup_inputs(seed: int = 0) -> dict:
    key = jax.random.key(seed)
    ks = iter(jax.random.split(key, 48))
    L = DEPTH

    def nrm(shape, scale):
        return jax.random.normal(next(ks), shape, jnp.float32) * scale

    def gain(shape):
        return 1.0 + nrm(shape, 0.02)

    def unif(shape, lo, hi):
        return jax.random.uniform(next(ks), shape, jnp.float32, lo, hi)

    return {
        'x': nrm((BATCH, SEQ, D_MODEL), 1.0),
        'mem': nrm((BATCH, N_MEM, D_MODEL), 1.0),
        'attn_norm_w': gain((L, D_MODEL)),
        'w_in': nrm((L, D_MODEL, P_IN), D_MODEL ** -0.5),
        'na_q_norm_w': gain((L, HEAD_DIM)),
        'na_k_norm_w': gain((L, HEAD_DIM)),
        'na_rpb': nrm((L, NA_HEADS, 2 * NA_KH - 1, 2 * NA_KW - 1), 0.02),
        'rw_mu_prev': unif((L, RW_PROJ), 0.1, 0.5),
        'rw_mu_next': unif((L, RW_PROJ), 0.1, 0.5),
        'rw_w0': unif((L, 2, RW_WIDTH), -5.0, 0.5),
        'rw_w2': nrm((L, 2, RW_LORA_W, RW_WIDTH), 0.1 * RW_LORA_W ** -0.5),
        'rw_a0': nrm((L, 2, RW_WIDTH), 0.1),
        'rw_a2': nrm((L, 2, RW_LORA_A, RW_WIDTH), 0.5 * RW_LORA_A ** -0.5),
        'rw_g2': nrm((L, RW_LORA_G, RW_WIDTH), RW_LORA_G ** -0.5),
        'rw_k_k': 0.85 + nrm((L, RW_WIDTH), 0.02),
        'rw_k_a': 1.0 + nrm((L, RW_WIDTH), 0.02),
        'rw_r_k': nrm((L, RW_HEADS, HEAD_DIM), 0.1),
        'rw_ln_w': gain((L, RW_WIDTH)),
        'rw_ln_b': nrm((L, RW_WIDTH), 0.02),
        'mem_norm_w': gain((L, D_MODEL)),
        'w_mem_kv': nrm((L, D_MODEL, 2 * MEM_WIDTH), D_MODEL ** -0.5),
        'mem_q_norm_w': gain((L, HEAD_DIM)),
        'mem_k_norm_w': gain((L, HEAD_DIM)),
        'w_out': nrm((L, D_MIX, D_MODEL), D_MIX ** -0.5),
        'ffn_norm_w': gain((L, D_MODEL)),
        'moe_w_group': nrm((L, D_MODEL, MOE_GROUPS), D_MODEL ** -0.5),
        'moe_b_group': nrm((L, MOE_GROUPS), 0.01),
        'moe_w_expert': nrm((L, D_MODEL, MOE_EXPERTS), D_MODEL ** -0.5),
        'moe_b_expert': nrm((L, MOE_EXPERTS), 0.01),
        'moe_w_gate': nrm((L, MOE_EXPERTS, D_MODEL, MOE_D_FF), D_MODEL ** -0.5),
        'moe_w_up': nrm((L, MOE_EXPERTS, D_MODEL, MOE_D_FF), D_MODEL ** -0.5),
        'moe_w_down': nrm((L, MOE_EXPERTS, MOE_D_FF, D_MODEL), MOE_D_FF ** -0.5),
    }

def reference(x, mem, attn_norm_w, w_in, na_q_norm_w, na_k_norm_w, na_rpb,
              rw_mu_prev, rw_mu_next, rw_w0, rw_w2, rw_a0, rw_a2, rw_g2,
              rw_k_k, rw_k_a, rw_r_k, rw_ln_w, rw_ln_b,
              mem_norm_w, w_mem_kv, mem_q_norm_w, mem_k_norm_w, w_out,
              ffn_norm_w, moe_w_group, moe_b_group, moe_w_expert, moe_b_expert,
              moe_w_gate, moe_w_up, moe_w_down):
    for l in range(DEPTH):
        h = rms_norm(x, attn_norm_w[l])
        mem_n = rms_norm(mem, mem_norm_w[l])
        x = x + hybrid_mixer(h, mem_n, w_in[l], na_q_norm_w[l], na_k_norm_w[l], na_rpb[l],
                             rw_mu_prev[l], rw_mu_next[l], rw_w0[l], rw_w2[l], rw_a0[l], rw_a2[l],
                             rw_g2[l], rw_k_k[l], rw_k_a[l], rw_r_k[l], rw_ln_w[l], rw_ln_b[l],
                             w_mem_kv[l], mem_q_norm_w[l], mem_k_norm_w[l], w_out[l])
        x = x + hierarchical_moe(rms_norm(x, ffn_norm_w[l]), moe_w_group[l], moe_b_group[l],
                                 moe_w_expert[l], moe_b_expert[l], moe_w_gate[l],
                                 moe_w_up[l], moe_w_down[l])
    return x


_drawn_inputs = setup_inputs


def setup_inputs(seed=0):
    import zlib

    import numpy as np

    out = dict(_drawn_inputs(seed))
    spreads = {}
    factors = {'attn_norm_w': 3.142,
     'na_q_norm_w': 5.505,
     'na_k_norm_w': 6.752,
     'na_rpb': 37.776,
     'rw_w2': 26.699,
     'rw_a0': 2.881,
     'rw_k_k': 35.752,
     'rw_k_a': 3.648,
     'rw_ln_w': 31.616,
     'rw_ln_b': 34.904,
     'mem_norm_w': 8.0,
     'mem_q_norm_w': 8.0,
     'mem_k_norm_w': 8.0,
     'moe_b_group': 29.552,
     'moe_b_expert': 47.64,
     'ffn_norm_w': 8.0}
    for name, (base, spread) in spreads.items():
        noise = np.random.default_rng([zlib.crc32(name.encode()), seed]).standard_normal(out[name].shape)
        drawn = base * np.exp(spread * noise) if base else spread * noise
        out[name] = __import__('jax').numpy.asarray(drawn.astype(out[name].dtype))
    for name, factor in factors.items():
        out[name] = (out[name] * factor).astype(out[name].dtype)
    return out
```

```python
from contextlib import ExitStack
import math

import concourse.bass as bass
from concourse import mybir

F32 = mybir.dt.float32
I32 = mybir.dt.int32
ALU = mybir.AluOpType
ACT = mybir.ActivationFunctionType
AX = mybir.AxisListType
ds = bass.ds

P = 128
D = 1024
KD = D // P
SEQ = 1024
TT = SEQ // P
NMEM = 256
HD = 64
GRID_W = 64
ROWS = SEQ // GRID_W
KH, KW = 8, 16
NA_PAIRS = 4
RW_PAIRS = 2
MEM_PAIRS = 2
C_Q, C_K, C_V, C_RW, C_MQ, C_ALL = 0, 4, 8, 12, 21, 23
RWC = C_MQ - C_RW
CHUNK = 64
NCH = SEQ // CHUNK
NEG = -1.0e30
NG, NE, FF = 4, 16, 512
KF = FF // P
NBLK = 31
SURE = 2 * SEQ // P
RMS_EPS = 1e-6
GN_EPS = 64e-5
DECAY = math.exp(-0.5)

PCOLS = dict(attn_w=8, mem_w=8, naq_w=1, nak_w=1, mq_w=1, mk_w=1, mu_p=9, mu_n=9, w0=4, a0=4,
             k_k=2, k_a=2, r_k=2, ln_w=2, ln_b=2)
PCOL = {}
_n = 0
for _k, _w in PCOLS.items():
    PCOL[_k] = _n
    _n += _w
NPC = _n

CCOLS = dict(ident=128, pair_ones=128, ones=128, before=128, fold=64, eps=1, gn_eps=1,
             l_mask_f=512, l_mask_b=512, x_mask_f=384, x_mask_b=384, iota=32, blk128=8, token=8)
CCOL = {}
_n = 0
for _k, _w in CCOLS.items():
    CCOL[_k] = _n
    _n += _w
NCC = _n


class Shared:
    pass


ONE = 1


def counter(nc, stack, name):
    sem = stack.enter_context(nc.semaphore(name))
    nc.gpsimd.sem_inc(sem, ONE)
    return sem


def dma_counter(nc, stack, name):
    return stack.enter_context(nc.semaphore(name))


def window_start(r):
    return min(max(r - KH // 2, 0), ROWS - KH)


def norm_transpose(nc, s, src, tiles, dst, w_col, tag):
    with ExitStack() as c:
        xt = c.enter_context(nc.sbuf_tensor("nt_xt" + tag, [P, 2, D], F32))
        xn = c.enter_context(nc.sbuf_tensor("nt_xn" + tag, [P, 2, D], F32))
        sq = c.enter_context(nc.sbuf_tensor("nt_sq" + tag, [P, 2, D], F32))
        st = c.enter_context(nc.sbuf_tensor("nt_st" + tag, [P, 2, 4], F32))
        ps = c.enter_context(nc.psum_tensor("nt_ps" + tag, [P, 2, KD, P], F32))
        loaded = [counter(nc, c, f"nt_loaded{u}{tag}") for u in range(2)]
        std_ready = counter(nc, c, "nt_std" + tag)
        sum_ready = counter(nc, c, "nt_sum" + tag)
        inv_ready = counter(nc, c, "nt_inv" + tag)
        normed = counter(nc, c, "nt_normed" + tag)
        turned = counter(nc, c, "nt_turned" + tag)
        stored = counter(nc, c, "nt_stored" + tag)
        nc.all_engine_barrier()
        block = c.enter_context(nc.Block())

        @block.sync
        def _(sp):
            with sp.Fori(0, tiles // 2) as i:
                for u in range(2):
                    sp.wait_ge(normed, i * 2 + ONE)
                    sp.dma_start(xt[:, u, :], src[ds(i * 2 + u, 1)].rearrange("a p d -> p (a d)")).then_inc(loaded[u], 16)

        @block.scalar
        def _(act):
            with act.Fori(0, tiles // 2) as i:
                for u in range(2):
                    act.wait_ge(loaded[u], i * 16 + 16 + ONE)
                    act.wait_ge(inv_ready, i * 2 + ONE)
                    act.activation(sq[:, u, :], xt[:, u, :], ACT.Square, accum_out=st[:, u, 0:1]).then_inc(sum_ready, 1)
                for u in range(2):
                    act.wait_ge(sum_ready, i * 2 + u + 1 + ONE)
                    act.activation(st[:, u, 1:2], st[:, u, 0:1], ACT.Sqrt, bias=s.eps, scale=1.0 / D).then_inc(std_ready, 1)

        @block.vector
        def _(dve):
            with dve.Fori(0, tiles // 2) as i:
                for u in range(2):
                    dve.wait_ge(std_ready, i * 2 + u + 1 + ONE)
                    dve.reciprocal(st[:, u, 2:3], st[:, u, 1:2]).then_inc(inv_ready, 1)
                for u in range(2):
                    dve.wait_ge(inv_ready, i * 2 + u + 1 + ONE)
                    dve.wait_ge(turned, i * 2 + ONE)
                    dve.tensor_scalar(xn[:, u, :], xt[:, u, :], st[:, u, 2:3], None, ALU.mult).then_inc(normed, 1)
                for u in range(2):
                    dve.wait_ge(turned, i * 2 + u + 1 + ONE)
                    dve.tensor_tensor(dst[:, :, ds((i * 2 + u) * P, P)], ps[:, u, :, :],
                                      s.par(w_col, KD).unsqueeze(2).to_broadcast([P, KD, P]), ALU.mult).then_inc(stored, 1)

        @block.tensor
        def _(pe):
            with pe.Fori(0, tiles // 2) as i:
                for u in range(2):
                    pe.wait_ge(normed, i * 2 + u + 1 + ONE)
                    pe.wait_ge(stored, i * 2 + ONE)
                    for k in range(KD):
                        mm = pe.transpose(ps[:, u, k, :], xn[:, u, k * P:(k + 1) * P], s.ident)
                    mm.then_inc(turned, 1)


def memory_kv(nc, s):
    with ExitStack() as c:
        w = c.enter_context(nc.sbuf_tensor("kv_w", [P, KD, 512], F32))
        ps = c.enter_context(nc.psum_tensor("kv_ps", [P, 4, 512], F32))
        loaded = counter(nc, c, "kv_loaded")
        done = counter(nc, c, "kv_done")
        nc.all_engine_barrier()
        block = c.enter_context(nc.Block())

        @block.sync
        def _(sp):
            sp.dma_start(w[:, :, :], s.inp["w_mem_kv"].rearrange("(k p) n -> p k n", p=P)).then_inc(loaded, 16)

        @block.tensor
        def _(pe):
            pe.wait_ge(loaded, 16 + ONE)
            for j in range(2):
                for k in range(KD):
                    mm = pe.matmul(ps[:, j, 0:NMEM], w[:, k, j * P:(j + 1) * P], s.memT[:, k, :],
                                   start=(k == 0), stop=(k == KD - 1))
                mm.then_inc(done, 1)
            for m in range(2):
                for k in range(KD):
                    mm = pe.matmul(ps[:, 2 + m, 0:256], s.memT[:, k, m * P:(m + 1) * P], w[:, k, 256:512],
                                   start=(k == 0), stop=(k == KD - 1))
                mm.then_inc(done, 1)

        @block.vector
        def _(dve):
            for j in range(2):
                dve.wait_ge(done, j + 1 + ONE)
                dve.tensor_copy(s.mkT[:, j, :], ps[:, j, 0:NMEM])

        @block.scalar
        def _(act):
            for m in range(2):
                act.wait_ge(done, m + 3 + ONE)
                act.activation(s.mv[:, m, :], ps[:, 2 + m, 0:256], ACT.Copy)


def projection(nc, s):
    with ExitStack() as c:
        w = c.enter_context(nc.sbuf_tensor("pj_w", [P, 2, KD, P], F32))
        ps = c.enter_context(nc.psum_tensor("pj_ps", [P, 2, 2, 512], F32))
        loaded = [counter(nc, c, f"pj_loaded{u}") for u in range(2)]
        zero = c.enter_context(nc.sbuf_tensor("pj_zero", [P, D], F32))
        zeroed, filled = counter(nc, c, "pj_zeroed"), dma_counter(nc, c, "pj_filled")
        done = counter(nc, c, "pj_done")
        out0 = counter(nc, c, "pj_out_act")
        out1 = counter(nc, c, "pj_out_dve")
        nc.all_engine_barrier()
        block = c.enter_context(nc.Block())
        w_in = s.inp["w_in"].rearrange("(k p) n -> p k n", p=P)

        @block.gpsimd
        def _(pool):
            pool.memset(zero[:, :], 0.0).then_inc(zeroed, 1)
            pool.wait_ge(zeroed, 1 + ONE)
            for b in range(SURE, NBLK):
                pool.dma_start(s.y_dram[b * P:(b + 1) * P, :], zero[:, :]).then_inc(filled, 16)
            pool.wait_ge(filled, 16 * (NBLK - SURE))

        @block.sync
        def _(sp):
            def load(i, u):
                sp.wait_ge(done, i * 4 + ONE)
                sp.dma_start(w[:, u, :, :], w_in[:, :, ds((i * 2 + u) * P, P)]).then_inc(loaded[u], 16)
            with sp.Fori(0, C_ALL // 2) as i:
                load(i, 0)
                load(i, 1)
            load(C_ALL // 2, 0)

        @block.tensor
        def _(pe):
            def chunk(i, u):
                pe.wait_ge(loaded[u], i * 16 + 16 + ONE)
                pe.wait_ge(out0, i * 2 + ONE)
                pe.wait_ge(out1, i * 2 + ONE)
                for half in range(2):
                    for k in range(KD):
                        mm = pe.matmul(ps[:, u, half, :], w[:, u, k, :], s.hT[:, k, half * 512:(half + 1) * 512],
                                       start=(k == 0), stop=(k == KD - 1))
                    mm.then_inc(done, 1)
            with pe.Fori(0, C_ALL // 2) as i:
                chunk(i, 0)
                chunk(i, 1)
            chunk(C_ALL // 2, 0)

        @block.scalar
        def _(act):
            def out(i, u):
                act.wait_ge(done, i * 4 + 2 * u + 1 + ONE)
                act.activation(s.proj[:, ds(i * 2 + u, 1), 0:512], ps[:, u, 0:1, :], ACT.Copy).then_inc(out0, 1)
            with act.Fori(0, C_ALL // 2) as i:
                out(i, 0)
                out(i, 1)
            out(C_ALL // 2, 0)

        @block.vector
        def _(dve):
            def out(i, u):
                dve.wait_ge(done, i * 4 + 2 * u + 2 + ONE)
                dve.tensor_copy(s.proj[:, ds(i * 2 + u, 1), 512:1024], ps[:, u, 1:2, :]).then_inc(out1, 1)
            with dve.Fori(0, C_ALL // 2) as i:
                out(i, 0)
                out(i, 1)
            out(C_ALL // 2, 0)


def bias_table(nc, s):
    rpb = s.inp["na_rpb"]
    row = 15 * GRID_W
    H = 8
    with ExitStack() as c:
        filled = counter(nc, c, "bt_filled")
        placed = counter(nc, c, "bt_placed")
        nc.all_engine_barrier()
        block = c.enter_context(nc.Block())
        t = s.bias_dram

        def spot(h, start, dims):
            return bass.AP(t.tensor, h * GRID_W * row + start, dims)

        @block.sync
        def _(sp):
            for h in range(H):
                sp.dma_start(t[h], s.inp["neg_fill"]).then_inc(filled, 16)
            sp.wait_ge(filled, 16 * H + ONE)
            n = 0
            for h in range(H):
                src = bass.AP(rpb.tensor, h * 15 * 31 + KW - 1 - KW // 2, [[0, 49], [31, 15], [1, KW]])
                sp.dma_start(spot(h, 8 * row, [[row + 1, 49], [GRID_W, 15], [1, KW]]), src).then_inc(placed, 16)
                n += 1
            for qc in [*range(8), *range(57, 64)]:
                cs = min(max(qc - KW // 2, 0), GRID_W - KW)
                src = bass.AP(rpb.tensor, cs - qc + KW - 1, [[15 * 31, H], [31, 15], [1, KW]])
                sp.dma_start(spot(0, qc * row + cs, [[GRID_W * row, H], [GRID_W, 15], [1, KW]]), src).then_inc(placed, 16)
                n += 1
            sp.wait_ge(placed, 16 * n + ONE)


def attention(nc, s, memory):
    tag = "m" if memory else "n"
    nk = NMEM if memory else KH * GRID_W
    kt = nk // P
    klen = NMEM if memory else SEQ
    G = ROWS
    nv = 0 if memory else ROWS - 1
    vb = -(-nv // 4)
    with ExitStack() as c:
        def sb(name, shape):
            return c.enter_context(nc.sbuf_tensor(f"at{tag}_{name}", shape, F32))

        def sem(name):
            return counter(nc, c, f"at{tag}_{name}")

        sq = sb("sq", [P, 2, SEQ])
        std = sb("std", [P, 2, SEQ])
        inv = sb("inv", [P, 2, SEQ])
        kn = sb("kn", [P, klen])
        qbd = sb("qbd", [P, G, P])
        qn = sb("qn", [P, 1])
        tb = sb("tb", [P, 15 * GRID_W])
        vst = sb("vst", [P, SEQ])
        v64 = sb("v64", [P, 16, P])
        ssb = sb("ssb", [P, 2, nk])
        pr = sb("pr", [P, 2, nk])
        pn = sb("pn", [P, 2, nk])
        ptb = sb("ptb", [P, 2, nk])
        nm = sb("nm", [P, 2, 4])
        rs = sb("rs", [P, 2, 4])
        ps_s = c.enter_context(nc.psum_tensor(f"at{tag}_ps_s", [P, 2, 512], F32))
        ps_t = c.enter_context(nc.psum_tensor(f"at{tag}_ps_t", [P, 2, 512], F32))
        ps_o = c.enter_context(nc.psum_tensor(f"at{tag}_ps_o", [P, 2, 512], F32))
        ps_n = c.enter_context(nc.psum_tensor(f"at{tag}_ps_n", [P, 2, 512], F32))
        zeroed, sq_ready, sum_ready, std_ready, inv_ready = (sem(n) for n in ("zeroed", "sq", "sum", "std", "inv"))
        qk_ready, v_copied, v_turned, v_ready, bias_in = (sem(n) for n in ("qk", "vcopy", "vturn", "vready", "bias"))
        scored, biased, exped, inv_sum, normed = (sem(n) for n in ("scored", "biased", "exped", "invsum", "normed"))
        turned, pt_ready, summed, stored, qscaled = (sem(n) for n in ("turned", "pt", "summed", "stored", "qscaled"))
        nc.all_engine_barrier()
        block = c.enter_context(nc.Block())

        def pairs(eng, body):
            if memory:
                for j in range(MEM_PAIRS):
                    body(j)
            else:
                with eng.Fori(0, NA_PAIRS) as j:
                    body(j)

        def q_src(j, p0=0, p1=P):
            return s.proj[p0:p1, ds((C_MQ if memory else C_Q) + j, 1), :]

        def k_src(j):
            return s.mkT[:, ds(j, 1), :] if memory else s.proj[:, ds(C_K + j, 1), :]

        @block.sync
        def _(sp):
            if not memory:
                with sp.Fori(0, NA_PAIRS) as j:
                    sp.wait_ge(biased, j * G + ONE)
                    sp.dma_start(tb[:, :], s.bias_dram.rearrange("(j a) c d k -> j (a c) (d k)", a=2)[ds(j, 1)]
                                 .rearrange("o p r -> p (o r)")).then_inc(bias_in, 16)

        @block.scalar
        def _(act):
            def body(j):
                act.activation(sq[:, 0:1, :], q_src(j), ACT.Square).then_inc(sq_ready, 1)
                act.activation(sq[:, 1:2, 0:klen], k_src(j), ACT.Square).then_inc(sq_ready, 1)
                if not memory:
                    act.wait_ge(v_turned, j * vb + ONE)
                    act.activation(vst[:, :].unsqueeze(1), s.proj[:, ds(C_V + j, 1), :], ACT.Copy).then_inc(v_copied, 1)
                for n in range(2):
                    ln = SEQ if n == 0 else klen
                    act.wait_ge(sum_ready, j * 2 + n + 1 + ONE)
                    act.wait_ge(inv_ready, j * 2 + ONE)
                    act.activation(std[:, n, 0:ln], ps_n[:, :, :].rearrange("p a b -> p (a b)")[:, 0:ln], ACT.Sqrt,
                                   bias=s.eps, scale=1.0 / HD).then_inc(std_ready, 1)
                for b in range(vb):
                    m = min(4, nv - 4 * b)
                    act.wait_ge(v_turned, j * vb + b + 1 + ONE)
                    act.wait_ge(summed, j * G + ONE)
                    act.activation(v64[:, 4 * b:4 * b + m, :].rearrange("p a b -> p (a b)"), ps_t[:, b % 2, 0:m * P],
                                   ACT.Copy).then_inc(v_ready, 1)
                for r in range(G + 1):
                    if r < G:
                        act.wait_ge(biased, j * G + r + 1 + ONE)
                        act.wait_ge(normed, j * G + max(r - 1, 0) + ONE)
                        act.activation(pr[:, r % 2, :], ssb[:, r % 2, :], ACT.Exp, bias=nm[:, r % 2, 0:1], scale=-1.0,
                                       accum_out=rs[:, r % 2, 0:1]).then_inc(exped, 1)
                    if r >= 1:
                        act.wait_ge(turned, j * G + r + ONE)
                        act.wait_ge(summed, j * G + max(r - 2, 0) + ONE)
                        act.activation(ptb[:, (r - 1) % 2, :], ps_t[:, (r - 1) % 2, 0:nk], ACT.Copy).then_inc(pt_ready, 1)
            pairs(act, body)

        @block.vector
        def _(dve):
            dve.memset(qbd[:, :, :], 0.0).then_inc(zeroed, 1)
            if memory:
                dve.memset(tb[:, :], 0.0).then_inc(zeroed, 1)
            dve.tensor_scalar(qn[:, :], s.par("mq_w" if memory else "naq_w", 1), HD ** -0.5, None, ALU.mult).then_inc(qscaled, 1)
            dve.wait_ge(qscaled, 1 + ONE)
            dve.wait_ge(zeroed, 2 if memory else 1 + ONE)

            def body(j):
                for n in range(2):
                    ln = SEQ if n == 0 else klen
                    dve.wait_ge(std_ready, j * 2 + n + 1 + ONE)
                    dve.wait_ge(qk_ready, j * 3 + ONE)
                    dve.reciprocal(inv[:, n, 0:ln], std[:, n, 0:ln]).then_inc(inv_ready, 1)
                dve.wait_ge(inv_ready, j * 2 + 1 + ONE)
                dve.wait_ge(scored, j * G + ONE)
                for h in range(2):
                    p0, p1 = h * HD, (h + 1) * HD
                    dve.scalar_tensor_tensor(out=qbd[p0:p1, :, p0:p1],
                                             in0=q_src(j, p0, p1).rearrange("p o (r c) -> p (o r) c", c=HD),
                                             scalar=qn[p0:p1, 0:1],
                                             in1=inv[p0:p1, 0, :].rearrange("p (r c) -> p r c", c=HD),
                                             op0=ALU.mult, op1=ALU.mult).then_inc(qk_ready, 1)
                dve.wait_ge(inv_ready, j * 2 + 2 + ONE)
                dve.scalar_tensor_tensor(out=kn[:, :].unsqueeze(1), in0=k_src(j), scalar=s.par("mk_w" if memory else "nak_w", 1),
                                         in1=inv[:, 1:2, 0:klen], op0=ALU.mult, op1=ALU.mult).then_inc(qk_ready, 1)
                if not memory:
                    dve.wait_ge(bias_in, j * 16 + 16 + ONE)
                for r in range(G + 3):
                    if r < G:
                        t0 = 0 if memory else (window_start(r) - r + KH - 1) * GRID_W
                        dve.wait_ge(scored, j * G + r + 1 + ONE)
                        dve.wait_ge(exped, j * G + max(r - 1, 0) + ONE)
                        dve.memset(nm[:, r % 2, 1:2], 0.0)
                        dve.tensor_tensor_reduce(ssb[:, r % 2, :], ps_s[:, r % 2, 0:nk], tb[:, t0:t0 + nk], -1.0, 3.0e38,
                                                 ALU.add, ALU.min, nm[:, r % 2, 0:1]).then_inc(biased, 1)
                    if 1 <= r <= G:
                        q = r - 1
                        dve.wait_ge(exped, j * G + q + 1 + ONE)
                        dve.reciprocal(rs[:, q % 2, 1:2], rs[:, q % 2, 0:1]).then_inc(inv_sum, 1)
                        dve.wait_ge(inv_sum, j * G + q + 1 + ONE)
                        dve.wait_ge(turned, j * G + max(q - 1, 0) + ONE)
                        dve.tensor_scalar(pn[:, q % 2, :], pr[:, q % 2, :], rs[:, q % 2, 1:2], None, ALU.mult).then_inc(normed, 1)
                    if r >= 3:
                        q = r - 3
                        dve.wait_ge(summed, j * G + q + 1 + ONE)
                        for h in range(2):
                            p0, p1 = h * HD, (h + 1) * HD
                            o = dve.tensor_copy(s.mixT[p0:p1, ds((6 if memory else 0) + j, 1), q * HD:(q + 1) * HD],
                                                ps_o[p0:p1, q % 2, p0:p1].unsqueeze(1))
                        o.then_inc(stored, 1)
            pairs(dve, body)

        @block.tensor
        def _(pe):
            def body(j):
                for n in range(2):
                    pe.wait_ge(sq_ready, j * 2 + n + 1 + ONE)
                    pe.wait_ge(std_ready, j * 2 + n + ONE)
                    for half in range(2 if (n == 0 or not memory) else 1):
                        ln = min(512, klen) if n else 512
                        mm = pe.matmul(ps_n[:, half, 0:ln], s.pair_ones, sq[:, n, half * 512:half * 512 + ln], start=True, stop=True)
                    mm.then_inc(sum_ready, 1)
                if not memory:
                    pe.wait_ge(v_copied, j + 1 + ONE)
                    for b in range(vb):
                        pe.wait_ge(v_ready, j * vb + max(b - 1, 0) + ONE)
                        pe.wait_ge(pt_ready, j * G + ONE)
                        for m in range(4 * b, min(4 * b + 4, nv)):
                            mm = pe.transpose(ps_t[:, b % 2, (m % 4) * P:(m % 4 + 1) * P], vst[:, m * HD:m * HD + P], s.ident)
                        mm.then_inc(v_turned, 1)
                pe.wait_ge(qk_ready, j * 3 + 3 + ONE)
                for r in range(G + 2):
                    ks = 0 if memory else window_start(min(r, G - 1)) * GRID_W
                    if r < G:
                        pe.wait_ge(biased, j * G + max(r - 1, 0) + ONE)
                        pe.matmul(ps_s[:, r % 2, 0:nk], qbd[:, r, :], kn[:, ks:ks + nk], start=True, stop=True).then_inc(scored, 1)
                    if r == 1 and not memory:
                        pe.wait_ge(v_ready, j * vb + vb + ONE)
                    if 1 <= r <= G:
                        q = r - 1
                        pe.wait_ge(normed, j * G + q + 1 + ONE)
                        pe.wait_ge(pt_ready, j * G + max(q - 1, 0) + ONE)
                        for a in range(kt):
                            mm = pe.transpose(ps_t[:, q % 2, a * P:(a + 1) * P], pn[:, q % 2, a * P:(a + 1) * P], s.ident)
                        mm.then_inc(turned, 1)
                    if r >= 2:
                        q = r - 2
                        pe.wait_ge(pt_ready, j * G + q + 1 + ONE)
                        pe.wait_ge(stored, j * G + max(q - 1, 0) + ONE)
                        for a in range(kt):
                            v = s.mv[:, a, j * P:(j + 1) * P] if memory else v64[:, window_start(q) + 2 * a, :]
                            mm = pe.matmul(ps_o[:, q % 2, 0:P], v, ptb[:, q % 2, a * P:(a + 1) * P],
                                           start=(a == 0), stop=(a == kt - 1))
                        mm.then_inc(summed, 1)
            pairs(pe, body)


def shift(nc, s):
    with ExitStack() as c:
        keep = c.enter_context(nc.sbuf_tensor("sh_keep", [P, RWC], F32))
        summed, kept, scaled, mixed = (counter(nc, c, "sh_" + n) for n in ("sum", "keep", "scaled", "mixed"))
        nc.all_engine_barrier()
        block = c.enter_context(nc.Block())

        @block.vector
        def _(dve):
            dve.tensor_tensor(keep[:, :], s.par("mu_p", RWC), s.par("mu_n", RWC), ALU.add).then_inc(summed, 1)
            dve.wait_ge(summed, 1 + ONE)
            dve.tensor_scalar(keep[:, :], keep[:, :], -1.0, 1.0, ALU.mult, ALU.add).then_inc(kept, 1)
            for j in range(RWC):
                src, dst = s.proj[:, C_RW + j, :], s.proj[:, j, :]
                dve.wait_ge(scaled, j + 1 + ONE)
                dve.scalar_tensor_tensor(out=dst[:, 1:], in0=src[:, :-1], scalar=s.par("mu_p", RWC)[:, j:j + 1], in1=dst[:, 1:],
                                         op0=ALU.mult, op1=ALU.add).then_inc(mixed, 1)
                dve.wait_ge(mixed, 2 * j + 1 + ONE)
                dve.scalar_tensor_tensor(out=dst[:, :-1], in0=src[:, 1:], scalar=s.par("mu_n", RWC)[:, j:j + 1], in1=dst[:, :-1],
                                         op0=ALU.mult, op1=ALU.add).then_inc(mixed, 1)

        @block.scalar
        def _(act):
            act.wait_ge(kept, 1 + ONE)
            for j in range(RWC):
                act.activation(s.proj[:, j, :], s.proj[:, C_RW + j, :], ACT.Copy, scale=keep[:, j:j + 1]).then_inc(scaled, 1)


S_R, S_K, S_V, S_LW, S_LA, S_LG, S_PROD, S_BONUS = 0, 2, 4, 6, 7, 8, 9, 21
UNITS = [(d, p) for d in range(2) for p in range(RW_PAIRS)]


def prod(s, n):
    return s.proj[:, S_PROD + 4 * n:S_PROD + 4 * n + 4, :] if n < 3 else s.extra[:, 0:4, :]


def gates(nc, s):
    with ExitStack() as c:
        def sem(name):
            return counter(nc, c, "ga_" + name)
        tmp = c.enter_context(nc.sbuf_tensor("ga_tmp", [P, 12, SEQ], F32))
        go = s.mixT[:, 4, :]
        w2, a2, g2 = (s.mixT[:, 5, n * 256:(n + 1) * 256] for n in range(3))
        ps = c.enter_context(nc.psum_tensor("ga_ps", [P, 4, SEQ], F32))
        loaded, kk_scaled, act_in, grouped, taken = (sem(n) for n in ("loaded", "kk_scaled", "act_in", "grouped", "taken"))
        kk_steps, kd_steps, b_ready, go_ready, cum_steps = (sem(n) for n in ("kk_steps", "kd_steps", "b_ready", "go_ready", "cum"))
        exps, scaled_v, scaled_g, bonus_steps = (sem(n) for n in ("exps", "scaled_v", "scaled_g", "bonus"))
        nc.all_engine_barrier()
        block = c.enter_context(nc.Block())
        tanh_lw, sig_lg = s.proj[:, S_LW, :], s.proj[:, S_LG, :]

        def lw(n):
            return tmp[:, n, :]

        def a(n):
            return tmp[:, 4 + n, :]

        def kk(p):
            return tmp[:, 8 + p, :]

        def sq(p):
            return tmp[:, 10 + p, :]

        def cum(n):
            return s.proj[:, S_LG if n % 2 else S_LW, :]

        @block.sync
        def _(sp):
            sp.dma_start(w2[:, :], s.inp["rw_w2"].rearrange("d k n -> (d k) n")).then_inc(loaded, 16)
            sp.dma_start(a2[:, :], s.inp["rw_a2"].rearrange("d k n -> (d k) n")).then_inc(loaded, 16)
            sp.dma_start(g2[:, :], s.inp["rw_g2"]).then_inc(loaded, 16)

        @block.tensor
        def _(pe):
            def group(n, lhsT, rhs):
                if n >= 4:
                    pe.wait_ge(taken, n - 3 + ONE)
                for half in range(2):
                    mm = pe.matmul(ps[:, n % 4, half * 512:(half + 1) * 512], lhsT, rhs[:, half * 512:(half + 1) * 512],
                                   start=True, stop=True)
                mm.then_inc(grouped, 1)
            pe.wait_ge(loaded, 48 + ONE)
            pe.wait_ge(act_in, 1 + ONE)
            for n, (d, p) in enumerate(UNITS):
                group(n, w2[d * HD:(d + 1) * HD, p * P:(p + 1) * P], tanh_lw[d * HD:(d + 1) * HD, :])
            for n, (d, p) in enumerate(UNITS):
                group(4 + n, a2[d * HD:(d + 1) * HD, p * P:(p + 1) * P], s.proj[d * HD:(d + 1) * HD, S_LA, :])
            pe.wait_ge(act_in, 2 + ONE)
            for p in range(RW_PAIRS):
                group(8 + p, g2[:, p * P:(p + 1) * P], sig_lg)
            for p in range(RW_PAIRS):
                pe.wait_ge(act_in, 3 + p + ONE)
                group(10 + p, s.pair_ones, sq(p))

        @block.scalar
        def _(act):
            act.activation(tanh_lw, s.proj[:, S_LW, :], ACT.Tanh).then_inc(act_in, 1)
            act.activation(sig_lg, s.proj[:, S_LG, :], ACT.Sigmoid).then_inc(act_in, 1)
            for p in range(RW_PAIRS):
                act.wait_ge(kk_scaled, p + 1 + ONE)
                act.activation(sq(p), kk(p), ACT.Square).then_inc(act_in, 1)
            for n in range(4):
                act.wait_ge(grouped, n + 1 + ONE)
                act.activation(lw(n), ps[:, n % 4, :], ACT.Sigmoid, bias=s.par("w0", 4)[:, n:n + 1]).then_inc(taken, 1)
            for n in range(4):
                act.wait_ge(grouped, n + 5 + ONE)
                act.activation(a(n), ps[:, n % 4, :], ACT.Sigmoid, bias=s.par("a0", 4)[:, n:n + 1]).then_inc(taken, 1)
            for p in range(RW_PAIRS):
                act.wait_ge(grouped, p + 9 + ONE)
                act.activation(s.extra[:, 4 + p, :], ps[:, (8 + p) % 4, :], ACT.Copy).then_inc(taken, 1)
            for p in range(RW_PAIRS):
                act.wait_ge(grouped, p + 11 + ONE)
                act.activation(sq(p), ps[:, (10 + p) % 4, :], ACT.Sqrt).then_inc(taken, 1)
            for n in range(4):
                pr = prod(s, n)
                act.wait_ge(cum_steps, 3 * n + 3 + ONE)
                act.wait_ge(b_ready, 4 + ONE)
                incl = cum(n) if n < 2 else lw(n)
                act.activation(pr[:, 0, :], pr[:, 0, :], ACT.Exp, scale=-DECAY).then_inc(exps, 1)
                act.activation(pr[:, 1, :], incl, ACT.Exp, scale=-DECAY).then_inc(exps, 1)
                act.activation(a(n), incl, ACT.Exp, scale=DECAY).then_inc(exps, 1)
                act.activation(s.ec[:, n, :], cum(n).rearrange("p (c t) -> p c t", t=CHUNK)[:, :, CHUNK - 1], ACT.Exp,
                               scale=-DECAY).then_inc(exps, 1)

        @block.vector
        def _(dve):
            dve.memset(go, 1.0).then_inc(go_ready, 1)
            dve.wait_ge(go_ready, 1 + ONE)
            dve.memset(go.rearrange("p (c t) -> p c t", t=CHUNK)[:, :, 0:1], 0.0).then_inc(go_ready, 1)
            for p in range(RW_PAIRS):
                dve.tensor_scalar(kk(p), s.proj[:, S_K + p, :], s.par("k_k", 2)[:, p:p + 1], None, ALU.mult).then_inc(kk_scaled, 1)
            for n, (d, p) in enumerate(UNITS):
                dve.wait_ge(taken, n + 5 + ONE)
                dve.tensor_scalar(prod(s, n)[:, 3, :], a(n), 1.0, s.par("k_a", 2)[:, p:p + 1], ALU.subtract, ALU.mult).then_inc(kd_steps, 1)
                dve.wait_ge(kd_steps, 2 * n + 1 + ONE)
                dve.scalar_tensor_tensor(out=prod(s, n)[:, 3, :], in0=prod(s, n)[:, 3, :], scalar=1.0, in1=s.proj[:, S_K + p, :],
                                         op0=ALU.add, op1=ALU.mult).then_inc(kd_steps, 1)
            for p in range(RW_PAIRS):
                dve.wait_ge(kd_steps, 2 * (p + 2) + 2 + ONE)
                dve.tensor_tensor(s.proj[:, S_BONUS + p, :], prod(s, p)[:, 3, :], prod(s, p + 2)[:, 3, :], ALU.add).then_inc(bonus_steps, 1)
                dve.wait_ge(bonus_steps, 2 * p + 1 + ONE)
                dve.scalar_tensor_tensor(out=s.proj[:, S_BONUS + p, :], in0=s.proj[:, S_BONUS + p, :], scalar=s.par("r_k", 2)[:, p:p + 1],
                                         in1=s.proj[:, S_R + p, :], op0=ALU.mult, op1=ALU.mult).then_inc(bonus_steps, 1)
            for p in range(RW_PAIRS):
                dve.wait_ge(taken, 11 + p + ONE)
                dve.tensor_scalar(sq(p), sq(p), 1e-12, None, ALU.max).then_inc(kk_steps, 1)
                dve.wait_ge(kk_steps, 3 * p + 1 + ONE)
                dve.reciprocal(sq(p), sq(p)).then_inc(kk_steps, 1)
                dve.wait_ge(kk_steps, 3 * p + 2 + ONE)
                dve.tensor_tensor(kk(p), kk(p), sq(p), ALU.mult).then_inc(kk_steps, 1)
            dve.wait_ge(go_ready, 2 + ONE)

            def scale(n):
                d, p = UNITS[n]
                dve.wait_ge(exps, 4 * n + 4 + ONE)
                dve.tensor_tensor(prod(s, n)[:, 0, :], prod(s, n)[:, 0, :], kk(p), ALU.mult).then_inc(scaled_v, 1)
                dve.tensor_tensor(prod(s, n)[:, 1, :], prod(s, n)[:, 1, :], s.proj[:, S_R + p, :], ALU.mult).then_inc(scaled_v, 1)
            dve.wait_ge(kk_steps, 6 + ONE)
            for n, (d, p) in enumerate(UNITS):
                if n >= 2:
                    scale(n - 2)
                dve.tensor_tensor_scan(cum(n), go, lw(n), 0.0, ALU.mult, ALU.add).then_inc(cum_steps, 1)
                dve.wait_ge(cum_steps, 3 * n + 1 + ONE)
                if d == 0:
                    dve.tensor_tensor(prod(s, n)[:, 0, :], cum(n), lw(n), ALU.subtract).then_inc(cum_steps, 2)
                else:
                    total = cum(n).rearrange("p (c t) -> p c t", t=CHUNK)[:, :, CHUNK - 1:CHUNK].to_broadcast([P, NCH, CHUNK])
                    dve.tensor_tensor(prod(s, n)[:, 0, :].rearrange("p (c t) -> p c t", t=CHUNK), total,
                                      cum(n).rearrange("p (c t) -> p c t", t=CHUNK), ALU.subtract).then_inc(cum_steps, 1)
                    dve.wait_ge(cum_steps, 3 * n + 2 + ONE)
                    dve.tensor_tensor(lw(n), prod(s, n)[:, 0, :], lw(n), ALU.add).then_inc(cum_steps, 1)
            scale(2)
            scale(3)

        @block.gpsimd
        def _(pool):
            pool.wait_ge(kk_steps, 6 + ONE)
            pool.wait_ge(taken, 8 + ONE)
            for n, (d, p) in enumerate(UNITS):
                pool.tensor_tensor(prod(s, n)[:, 2, :], kk(p), a(n), ALU.mult).then_inc(b_ready, 1)
            pool.wait_ge(bonus_steps, 4 + ONE)
            pool.wait_ge(b_ready, 4 + ONE)
            for n in range(4):
                pool.wait_ge(exps, 4 * n + 3 + ONE)
                for j in (2, 3):
                    pool.tensor_tensor(prod(s, n)[:, j, :], prod(s, n)[:, j, :], a(n), ALU.mult).then_inc(scaled_g, 1)


def scan(nc, s):
    NU = len(UNITS)
    with ExitStack() as c:
        def sb(name, shape):
            return c.enter_context(nc.sbuf_tensor("sc_" + name, shape, F32))

        def sem(name):
            return counter(nc, c, "sc_" + name)
        bd = sb("bd", [P, NU, 5, P])
        lm = sb("lm", [P, NU, 512])
        xm = sb("xm", [P, NU, 3 * P])
        qq = sb("qq", [P, NU, 2, P])
        mm2 = sb("mm2", [P, NU, 2, 2, P])
        y1 = sb("y1", [P, NU, P])
        btv = sb("btv", [P, NU, 320])
        wu = sb("wu", [P, NU, 2, HD])
        st = sb("st", [P, NU, HD])
        ps = c.enter_context(nc.psum_tensor("sc_ps", [P, NU, 2, 512], F32))
        zeroed, packed, unpacked, seeded = (sem(n) for n in ("zeroed", "packed", "unpacked", "seeded"))
        prods, masked, sides = (sem(n) for n in ("products", "masked", "sides"))
        powed, pow_out, improved, inverse = (sem(n) for n in ("powed", "pow_out", "improved", "inverse"))
        crossed, cross_out = sem("crossed"), sem("cross_out")
        w_sum, w_out, u_sum, u_out, y_sum, y_out, s_out = (sem(n) for n in ("w_sum", "w_out", "u_sum", "u_out", "y_sum", "y_out", "s_out"))
        nc.all_engine_barrier()
        block = c.enter_context(nc.Block())
        yb = s.proj[:, 0:4, :].rearrange("p n (c v) -> p n c v", v=HD)

        def chunk_of(i, n):
            return i if UNITS[n][0] == 0 else i * -1 + (NCH - 1)

        @block.gpsimd
        def _(pool):
            pool.memset(bd[:, :, :, :], 0.0).then_inc(zeroed, 1)
            pool.wait_ge(zeroed, 1 + ONE)
            with pool.Fori(0, NCH) as i:
                pool.wait_ge(seeded, i * NU * 2 + ONE)
                for n, (d, p) in enumerate(UNITS):
                    tok = chunk_of(i, n) * CHUNK
                    pool.wait_ge(y_sum, i * NU + ONE)
                    for h in range(2):
                        p0, p1 = h * HD, (h + 1) * HD
                        pool.tensor_copy(bd[p0:p1, n, 0:4, p0:p1], prod(s, n)[p0:p1, :, ds(tok, CHUNK)]).then_inc(packed, 1)
                        pool.tensor_copy(bd[p0:p1, n, 4, p0:p1], s.proj[p0:p1, S_V + p, ds(tok, CHUNK)]).then_inc(packed, 1)
                pool.wait_ge(packed, i * NU * 4 + NU * 4 + ONE)
                for n in range(NU):
                    pool.wait_ge(masked, (i * NU + n) * 2 + 2 + ONE)
                    pool.tensor_tensor(qq[:, n, 0, :], lm[:, n, 0:P], s.ident, ALU.add).then_inc(seeded, 1)
                    pool.tensor_tensor(qq[:, n, 1, :], xm[:, n, 0:P], s.ident, ALU.add).then_inc(seeded, 1)

        @block.tensor
        def _(pe):
            with pe.Fori(0, NCH) as i:
                def at(n, per=1):
                    return (i * NU + n) * per
                for n in range(NU):
                    b = bd[:, n, :, :]
                    pe.wait_ge(packed, at(n, 4) + 4 + ONE)
                    pe.wait_ge(y_out, at(0) + ONE)
                    pe.wait_ge(s_out, at(0) + 1 + ONE)
                    kr = b[:, 0:2, :].rearrange("p a b -> p (a b)")
                    pe.matmul(ps[:, n, 0, 0:256], b[:, 2, :], kr, start=True, stop=True)
                    pe.matmul(ps[:, n, 0, 256:512], b[:, 3, :], kr, start=True, stop=True)
                    pe.matmul(ps[:, n, 1, 0:P], b[:, 0, :], b[:, 2, :], start=True, stop=True)
                    pe.transpose(ps[:, n, 1, P:2 * P], b[:, 2, :], s.ident)
                    pe.transpose(ps[:, n, 1, 2 * P:3 * P], b[:, 3, :], s.ident)
                    pe.matmul(ps[:, n, 1, 3 * P:3 * P + HD], b[:, 4, :], s.fold, start=True, stop=True).then_inc(prods, 1)
                for n in range(NU):
                    pe.wait_ge(masked, at(n, 2) + 2 + ONE)
                    pe.matmul(ps[:, n, 0, 0:P], lm[:, n, 0:P], xm[:, n, 0:P], start=True, stop=True)
                    pe.matmul(ps[:, n, 0, P:2 * P], xm[:, n, 0:P], lm[:, n, 0:P], start=True, stop=True).then_inc(powed, 1)
                for step in range(3):
                    for n in range(NU):
                        m = mm2[:, n, step % 2, :, :]
                        pe.wait_ge(pow_out, (i * NU * 3) + NU * step + n + 1 + ONE)
                        if step == 0:
                            pe.wait_ge(seeded, at(n, 2) + 2 + ONE)
                            pe.wait_ge(sides, at(n) + 1 + ONE)
                        else:
                            pe.wait_ge(improved, (i * NU * 4) + NU * (step - 1) + n + 1 + ONE)
                        pe.matmul(ps[:, n, 1, 0:P], m[:, 0, :], qq[:, n, 0, :], start=True, stop=True)
                        mm = pe.matmul(ps[:, n, 1, P:2 * P], m[:, 1, :], qq[:, n, 1, :], start=True, stop=True)
                        if step < 2:
                            pe.matmul(ps[:, n, 0, 0:P], m[:, 1, :], m[:, 0, :], start=True, stop=True)
                            mm = pe.matmul(ps[:, n, 0, P:2 * P], m[:, 0, :], m[:, 1, :], start=True, stop=True)
                        mm.then_inc(powed, 1)
                for level in range(2):
                    for n in range(NU):
                        pe.wait_ge(improved, (i * NU * 4) + NU * (2 + level) + n + 1 + ONE)
                        pe.matmul(ps[:, n, 0, 0:P], xm[:, n, (level + 1) * P:(level + 2) * P], qq[:, n, 0, :],
                                  start=True, stop=True).then_inc(crossed, 1)
                    for n in range(NU):
                        pe.wait_ge(cross_out, (i * NU * 2) + NU * level + n + 1 + ONE)
                        mm = pe.matmul(ps[:, n, 1, 0:P], qq[:, n, 1, :], y1[:, n, :], start=True, stop=True)
                        if level == 0:
                            mm = pe.matmul(ps[:, n, 1, P:2 * P], y1[:, n, :], qq[:, n, 1, :], start=True, stop=True)
                        mm.then_inc(crossed, 1)
                for n in range(NU):
                    pe.matmul(ps[:, n, 0, 0:HD], bd[:, n, 0, :], st[:, n, :], start=True, stop=False)
                    pe.matmul(ps[:, n, 0, 0:HD], lm[:, n, 256:384], btv[:, n, 256:320], start=False, stop=True).then_inc(w_sum, 1)
                for n in range(NU):
                    pe.wait_ge(w_out, at(n) + 1 + ONE)
                    pe.wait_ge(inverse, at(n) + 1 + ONE)
                    pe.matmul(ps[:, n, 0, HD:2 * HD], qq[:, n, 0, :], wu[:, n, 0, :], start=True, stop=True).then_inc(u_sum, 1)
                for n in range(NU):
                    pe.wait_ge(u_out, at(n) + 1 + ONE)
                    pe.matmul(ps[:, n, 0, 2 * HD:3 * HD], s.ident, st[:, n, :], start=True, stop=False)
                    pe.matmul(ps[:, n, 0, 2 * HD:3 * HD], btv[:, n, 0:P], wu[:, n, 1, :], start=False, stop=False)
                    pe.matmul(ps[:, n, 0, 2 * HD:3 * HD], btv[:, n, P:2 * P], btv[:, n, 256:320], start=False, stop=True)
                    pe.matmul(ps[:, n, 1, 0:HD], bd[:, n, 1, :], st[:, n, :], start=True, stop=False)
                    pe.matmul(ps[:, n, 1, 0:HD], lm[:, n, P:2 * P], wu[:, n, 1, :], start=False, stop=False)
                    pe.matmul(ps[:, n, 1, 0:HD], lm[:, n, 384:512], btv[:, n, 256:320], start=False, stop=True).then_inc(y_sum, 1)

        @block.vector
        def _(dve):
            dve.memset(st[:, :, :], 0.0).then_inc(s_out, 1)
            with dve.Fori(0, NCH) as i:
                def at(n, per=1):
                    return (i * NU + n) * per
                for n, (d, p) in enumerate(UNITS):
                    dve.wait_ge(prods, at(n) + 1 + ONE)
                    dve.wait_ge(u_out, at(0) + ONE)
                    dve.tensor_tensor(xm[:, n, :].rearrange("p (a b) -> p a b", a=3),
                                      ps[:, n, 1:2, 0:P].to_broadcast([P, 3, P]),
                                      s.x_mask[d].rearrange("p (a b) -> p a b", a=3), ALU.mult).then_inc(masked, 1)
                    dve.tensor_tensor(lm[:, n, :], ps[:, n, 0, :], s.l_mask[d], ALU.mult).then_inc(masked, 1)
                for step in range(3):
                    for n in range(NU):
                        dve.wait_ge(powed, (i * NU * 4) + NU * (step + 1) + n + 1 + ONE)
                        dve.tensor_tensor(qq[:, n, :, :], ps[:, n, 1, 0:256].rearrange("p (a b) -> p a b", a=2), qq[:, n, :, :],
                                          ALU.add).then_inc(improved, 1)
                for level in range(2):
                    for n in range(NU):
                        dve.wait_ge(crossed, (i * NU * 4) + NU * (2 * level + 1) + n + 1 + ONE)
                        if level == 0:
                            dve.tensor_tensor(qq[:, n, :, :], ps[:, n, 1, 0:256].rearrange("p (a b) -> p a b", a=2), qq[:, n, :, :],
                                              ALU.add).then_inc(improved, 1)
                        else:
                            dve.tensor_tensor(qq[:, n, 0, :], ps[:, n, 1, 0:P], qq[:, n, 0, :], ALU.add).then_inc(inverse, 1)
                for n in range(NU):
                    ch = chunk_of(i, n)
                    dve.wait_ge(y_sum, at(n) + 1 + ONE)
                    dve.tensor_tensor(st[:, n, :], ps[:, n, 0, 2 * HD:3 * HD],
                                      s.ec[:, n, ds(ch, 1)].to_broadcast([P, HD]), ALU.mult).then_inc(s_out, 1)
                    dve.tensor_copy(yb[:, n, ds(ch, 1), :], ps[:, n, 1:2, 0:HD]).then_inc(y_out, 1)

        @block.scalar
        def _(act):
            with act.Fori(0, NCH) as i:
                def at(n, per=1):
                    return (i * NU + n) * per
                for n in range(NU):
                    act.wait_ge(masked, at(n, 2) + 1 + ONE)
                    act.activation(btv[:, n, :], ps[:, n, 1, P:P + 320], ACT.Copy).then_inc(sides, 1)
                for step in range(3):
                    for n in range(NU):
                        act.wait_ge(powed, (i * NU * 4) + NU * step + n + 1 + ONE)
                        act.activation(mm2[:, n, step % 2, :, :].rearrange("p a b -> p (a b)"), ps[:, n, 0, 0:256],
                                       ACT.Copy).then_inc(pow_out, 1)
                for level in range(2):
                    for n in range(NU):
                        act.wait_ge(crossed, (i * NU * 4) + NU * 2 * level + n + 1 + ONE)
                        act.activation(y1[:, n, :], ps[:, n, 0, 0:P], ACT.Copy).then_inc(cross_out, 1)
                for n in range(NU):
                    act.wait_ge(w_sum, at(n) + 1 + ONE)
                    act.activation(wu[:, n, 0, :], ps[:, n, 0, 0:HD], ACT.Copy).then_inc(w_out, 1)
                for n in range(NU):
                    act.wait_ge(u_sum, at(n) + 1 + ONE)
                    act.activation(wu[:, n, 1, :], ps[:, n, 0, HD:2 * HD], ACT.Copy, scale=-1.0).then_inc(u_out, 1)


def rwkv_out(nc, s):
    with ExitStack() as c:
        def sem(name):
            return counter(nc, c, "ro_" + name)
        ybd = c.enter_context(nc.sbuf_tensor("ro_ybd", [P, RW_PAIRS, P], F32))
        yt = c.enter_context(nc.sbuf_tensor("ro_yt", [P, RW_PAIRS, SEQ], F32))
        ps = c.enter_context(nc.psum_tensor("ro_ps", [P, RW_PAIRS, 512], F32))
        pn = c.enter_context(nc.psum_tensor("ro_pn", [P, SEQ], F32))
        pb = c.enter_context(nc.psum_tensor("ro_pb", [P, SEQ], F32))
        zeroed, packed, turned, stored = (sem(n) for n in ("zeroed", "packed", "turned", "stored"))
        meaned, centred, squared, spread, rooted, bonus, steps = (sem(n) for n in ("mean", "centred", "sq", "var", "root", "bonus", "steps"))
        nc.all_engine_barrier()
        block = c.enter_context(nc.Block())
        yb = s.proj[:, 0:4, :].rearrange("p n (c v) -> p n c v", v=HD)
        root = s.proj[:, 9:11, :]
        sq = s.proj[:, 11:13, :]

        @block.gpsimd
        def _(pool):
            pool.memset(ybd[:, :, :], 0.0).then_inc(zeroed, 1)
            pool.wait_ge(zeroed, 1 + ONE)
            with pool.Fori(0, NCH) as i:
                for p in range(RW_PAIRS):
                    pool.wait_ge(turned, i * RW_PAIRS + ONE)
                    for h in range(2):
                        p0, p1 = h * HD, (h + 1) * HD
                        pool.tensor_tensor(ybd[p0:p1, p:p + 1, p0:p1], yb[p0:p1, p, ds(i, 1), :], yb[p0:p1, p + 2, ds(i, 1), :],
                                           ALU.add).then_inc(packed, 1)

        @block.tensor
        def _(pe):
            with pe.Fori(0, NCH) as i:
                for p in range(RW_PAIRS):
                    pe.wait_ge(packed, (i * RW_PAIRS + p) * 2 + 2 + ONE)
                    pe.wait_ge(stored, i * RW_PAIRS + ONE)
                    pe.matmul(ps[:, p, 0:HD], ybd[:, p, :], s.fold, start=True, stop=True).then_inc(turned, 1)
            for p in range(RW_PAIRS):
                pe.wait_ge(stored, NCH * RW_PAIRS + ONE)
                if p:
                    pe.wait_ge(rooted, p + ONE)
                    pe.wait_ge(steps, 4 * p + ONE)
                for half in range(2):
                    mm = pe.matmul(pn[:, half * 512:(half + 1) * 512], s.pair_ones, yt[:, p, half * 512:(half + 1) * 512], start=True, stop=True)
                mm.then_inc(meaned, 1)
                for half in range(2):
                    mm = pe.matmul(pb[:, half * 512:(half + 1) * 512], s.pair_ones,
                                   s.proj[:, S_BONUS + p, half * 512:(half + 1) * 512], start=True, stop=True)
                mm.then_inc(bonus, 1)
                pe.wait_ge(squared, p + 1 + ONE)
                for half in range(2):
                    mm = pe.matmul(pn[:, half * 512:(half + 1) * 512], s.pair_ones, sq[:, p, half * 512:(half + 1) * 512], start=True, stop=True)
                mm.then_inc(spread, 1)

        @block.scalar
        def _(act):
            with act.Fori(0, NCH) as i:
                for p in range(RW_PAIRS):
                    act.wait_ge(turned, i * RW_PAIRS + p + 1 + ONE)
                    act.activation(yt[:, p, ds(i * CHUNK, CHUNK)], ps[:, p, 0:HD], ACT.Copy).then_inc(stored, 1)
            for p in range(RW_PAIRS):
                act.wait_ge(centred, p + 1 + ONE)
                act.activation(sq[:, p, :], yt[:, p, :], ACT.Square).then_inc(squared, 1)
                act.wait_ge(spread, p + 1 + ONE)
                act.activation(root[:, p, :], pn[:, :], ACT.Sqrt, bias=s.gn_eps, scale=1.0 / HD).then_inc(rooted, 1)

        @block.vector
        def _(dve):
            for p in range(RW_PAIRS):
                dve.wait_ge(meaned, p + 1 + ONE)
                dve.wait_ge(stored, NCH * RW_PAIRS + ONE)
                dve.scalar_tensor_tensor(out=yt[:, p, :], in0=pn[:, :], scalar=-1.0 / HD, in1=yt[:, p, :], op0=ALU.mult, op1=ALU.add)\
                   .then_inc(centred, 1)
                dve.wait_ge(bonus, p + 1 + ONE)
                v = s.proj[:, S_V + p, :]
                dve.tensor_tensor(v, pb[:, :], v, ALU.mult).then_inc(steps, 1)
                dve.wait_ge(rooted, p + 1 + ONE)
                dve.reciprocal(root[:, p, :], root[:, p, :]).then_inc(steps, 1)
                dve.wait_ge(steps, 4 * p + 2 + ONE)
                dve.scalar_tensor_tensor(out=yt[:, p, :], in0=yt[:, p, :], scalar=s.par("ln_w", 2)[:, p:p + 1], in1=root[:, p, :],
                                         op0=ALU.mult, op1=ALU.mult).then_inc(steps, 1)
                dve.wait_ge(steps, 4 * p + 3 + ONE)
                dve.scalar_tensor_tensor(out=yt[:, p, :], in0=yt[:, p, :], scalar=s.par("ln_b", 2)[:, p:p + 1], in1=v,
                                         op0=ALU.add, op1=ALU.add).then_inc(steps, 1)
                dve.wait_ge(steps, 4 * p + 4 + ONE)
                dve.tensor_tensor(s.mixT[:, 4 + p, :], yt[:, p, :], s.extra[:, 4 + p, :], ALU.mult)


def out_projection(nc, s):
    with ExitStack() as c:
        w = c.enter_context(nc.sbuf_tensor("op_w", [P, KD, D], F32))
        ps = c.enter_context(nc.psum_tensor("op_ps", [P, 4, 512], F32))
        loaded, x_in, done, added = (counter(nc, c, "op_" + n) for n in ("loaded", "x_in", "done", "added"))
        nc.all_engine_barrier()
        block = c.enter_context(nc.Block())

        @block.sync
        def _(sp):
            sp.dma_start(w[:, :, :], s.inp["w_out"].rearrange("(k p) n -> p k n", p=P)).then_inc(loaded, 16)
            sp.dma_start(s.x1[:, :, :], s.inp["x"].rearrange("(t p) n -> p t n", p=P)).then_inc(x_in, 16)

        @block.tensor
        def _(pe):
            pe.wait_ge(loaded, 16 + ONE)
            with pe.Fori(0, 2) as half:
                for t in range(TT):
                    pe.wait_ge(added, half * TT + max(t - 3, 0) + ONE)
                    for k in range(KD):
                        mm = pe.matmul(ps[:, t % 4, :], s.mixT[:, k, t * P:(t + 1) * P], w[:, k, ds(half * 512, 512)],
                                       start=(k == 0), stop=(k == KD - 1))
                    mm.then_inc(done, 1)

        @block.vector
        def _(dve):
            dve.wait_ge(x_in, 16 + ONE)
            with dve.Fori(0, 2) as half:
                for t in range(TT):
                    dve.wait_ge(done, half * TT + t + 1 + ONE)
                    x = s.x1[:, t, ds(half * 512, 512)]
                    dve.tensor_tensor(x, ps[:, t % 4, :], x, ALU.add).then_inc(added, 1)


def ffn_norm_router(nc, s):
    with ExitStack() as c:
        def sb(name, shape):
            return c.enter_context(nc.sbuf_tensor("fr_" + name, shape, F32))

        def sem(name):
            return counter(nc, c, "fr_" + name)
        sq = sb("sq", [P, D])
        h = sb("h", [P, 2, D])
        hT = sb("hT", [P, 2, KD, P])
        wf = sb("wf", [P, D])
        wr = sb("wr", [P, KD, NG + NE])
        br = sb("br", [P, NG + NE])
        st = sb("st", [P, 2, 4])
        ps = c.enter_context(nc.psum_tensor("fr_ps", [P, 2, KD, P], F32))
        pl = c.enter_context(nc.psum_tensor("fr_pl", [P, 2, 512], F32))
        loaded, sums, roots, invs, normed, turned, copied, logits, biased = (
            sem(n) for n in ("loaded", "sums", "roots", "invs", "normed", "turned", "copied", "logits", "biased"))
        rows_out = [sem("rows_out0"), sem("rows_out1")]
        nc.all_engine_barrier()
        block = c.enter_context(nc.Block())
        h_rows = s.h_dram.rearrange("(t p) n -> t p n", p=P)

        @block.sync
        def _(sp):
            sp.dma_start(wf[:, :], s.inp["ffn_norm_w"].to_broadcast([P, D])).then_inc(loaded, 16)
            sp.dma_start(wr[:, :, 0:NG], s.inp["moe_w_group"].rearrange("(k p) n -> p k n", p=P)).then_inc(loaded, 16)
            sp.dma_start(wr[:, :, NG:], s.inp["moe_w_expert"].rearrange("(k p) n -> p k n", p=P)).then_inc(loaded, 16)
            sp.dma_start(br[:, 0:NG], s.inp["moe_b_group"].to_broadcast([P, NG])).then_inc(loaded, 16)
            sp.dma_start(br[:, NG:], s.inp["moe_b_expert"].to_broadcast([P, NE])).then_inc(loaded, 16)
            with sp.Fori(0, TT // 2) as i:
                for u in range(2):
                    sp.wait_ge(normed, i * 2 + u + 1 + ONE)
                    sp.dma_start(h_rows[ds(i * 2 + u, 1)].rearrange("o p n -> p (o n)"), h[:, u, :]).then_inc(rows_out[u], 16)
            sp.wait_ge(rows_out[0], 16 * TT // 2 + ONE)
            sp.wait_ge(rows_out[1], 16 * TT // 2 + ONE)

        @block.scalar
        def _(act):
            with act.Fori(0, TT // 2) as i:
                for u in range(2):
                    act.wait_ge(invs, i * 2 + ONE)
                    act.wait_ge(sums, i * 2 + u + ONE)
                    act.activation(sq[:, :].unsqueeze(1), s.x1[:, ds(i * 2 + u, 1), :], ACT.Square, accum_out=st[:, u, 0:1]).then_inc(sums, 1)
                for u in range(2):
                    act.wait_ge(sums, i * 2 + u + 1 + ONE)
                    act.activation(st[:, u, 1:2], st[:, u, 0:1], ACT.Sqrt, bias=s.eps, scale=1.0 / D).then_inc(roots, 1)
                for u in range(2):
                    act.wait_ge(turned, i * 2 + u + 1 + ONE)
                    act.wait_ge(logits, i * 2 + ONE)
                    act.activation(hT[:, u, :, :], ps[:, u, :, :], ACT.Copy).then_inc(copied, 1)

        @block.vector
        def _(dve):
            dve.wait_ge(loaded, 80 + ONE)
            with dve.Fori(0, TT // 2) as i:
                for u in range(2):
                    dve.wait_ge(roots, i * 2 + u + 1 + ONE)
                    dve.reciprocal(st[:, u, 2:3], st[:, u, 1:2]).then_inc(invs, 1)
                for u in range(2):
                    dve.wait_ge(invs, i * 2 + u + 1 + ONE)
                    dve.wait_ge(turned, i * 2 + ONE)
                    dve.wait_ge(rows_out[u], i * 16 + ONE)
                    dve.scalar_tensor_tensor(out=h[:, u:u + 1, :], in0=s.x1[:, ds(i * 2 + u, 1), :], scalar=st[:, u, 2:3],
                                             in1=wf[:, :].unsqueeze(1), op0=ALU.mult, op1=ALU.mult).then_inc(normed, 1)
                for u in range(2):
                    dve.wait_ge(logits, i * 2 + u + 1 + ONE)
                    dve.tensor_tensor(s.logits[:, ds(i * 2 + u, 1), :], pl[:, u:u + 1, 0:NG + NE], br[:, :].unsqueeze(1), ALU.add)\
                       .then_inc(biased, 1)

        @block.tensor
        def _(pe):
            pe.wait_ge(loaded, 80 + ONE)
            with pe.Fori(0, TT // 2) as i:
                for u in range(2):
                    pe.wait_ge(normed, i * 2 + u + 1 + ONE)
                    pe.wait_ge(copied, i * 2 + ONE)
                    for k in range(KD):
                        mm = pe.transpose(ps[:, u, k, :], h[:, u, k * P:(k + 1) * P], s.ident)
                    mm.then_inc(turned, 1)
                for u in range(2):
                    pe.wait_ge(copied, i * 2 + u + 1 + ONE)
                    pe.wait_ge(biased, i * 2 + ONE)
                    for k in range(KD):
                        mm = pe.matmul(pl[:, u, 0:NG + NE], hT[:, u, k, :], wr[:, k, :], start=(k == 0), stop=(k == KD - 1))
                    mm.then_inc(logits, 1)


def routing(nc, s):
    with ExitStack() as c:
        def sb(name, shape, dt=F32):
            return c.enter_context(nc.sbuf_tensor("rt_" + name, shape, dt))

        def sem(name):
            return counter(nc, c, "rt_" + name)
        gmax, gmin, den, m1, m2, e2v = (sb(n, [P, TT]) for n in ("gmax", "gmin", "den", "m1", "m2", "e2"))
        t4, t4b, goh, sel = (sb(n, [P, TT, 4]) for n in ("t4", "t4b", "goh", "sel"))
        t44 = sb("t44", [P, TT, 4, 4])
        eoh = sb("eoh", [P, 2, TT, 4])
        oh = sb("oh", [P, 2, TT, NE])
        both = sb("both", [P, TT, NE])
        off = sb("off", [P, TT + 1, NE])
        rank = sb("rank", [P, TT, NE])
        t16 = sb("t16", [P, 2, TT, NE])
        cnt8 = sb("cnt8", [P, NE, 8])
        nb, ends, starts = (sb(n, [P, NE]) for n in ("nb", "ends", "starts"))
        b32 = sb("b32", [P, 32, NE])
        be = sb("be", [P, 32])
        bei = s.blk
        slotf = sb("slotf", [P, 2, TT])
        zeros = sb("zeros", [P, 32], I32)
        toki = sb("toki", [P, TT], I32)
        ps = c.enter_context(nc.psum_tensor("rt_ps", [P, 2, 512], F32))
        step, expd, stacked, ranked, zeroed, cleared, tok_ready = (
            sem(n) for n in ("step", "exp", "stacked", "ranked", "zeroed", "cleared", "tok"))
        scattered = dma_counter(nc, c, "rt_scattered")
        nc.all_engine_barrier()
        block = c.enter_context(nc.Block())
        gl, el = s.logits[:, :, 0:NG], s.logits[:, :, NG:]
        iota4 = s.iota[:, 0:4]

        def b3(ap, shape):
            return ap.to_broadcast(shape)

        @block.vector
        def _(dve):
            n = 0

            def link(ins):
                nonlocal n
                n += 1
                ins.then_inc(step, 1)
                dve.wait_ge(step, n + ONE)

            def first_max(vals, peak, onehot):
                link(dve.tensor_reduce(peak, vals, AX.X, ALU.max))
                link(dve.tensor_tensor(t4[:, :, :], vals, b3(peak.unsqueeze(2), [P, TT, 4]), ALU.is_equal))
                link(dve.tensor_scalar(t4[:, :, :], t4[:, :, :], -4.0, 4.0, ALU.mult, ALU.add))
                link(dve.tensor_tensor(t4[:, :, :], t4[:, :, :], b3(iota4.unsqueeze(1), [P, TT, 4]), ALU.add))
                link(dve.tensor_reduce(gmin[:, :], t4[:, :, :], AX.X, ALU.min))
                link(dve.tensor_tensor(onehot, b3(gmin[:, :].unsqueeze(2), [P, TT, 4]), b3(iota4.unsqueeze(1), [P, TT, 4]), ALU.is_equal))

            dve.memset(zeros[:, :], 0).then_inc(zeroed, 1)
            dve.tensor_copy(toki[:, :], s.token).then_inc(tok_ready, 1)
            first_max(gl, gmax[:, :], goh[:, :, :])
            link(dve.tensor_tensor(t4b[:, :, :], gl, b3(gmax[:, :].unsqueeze(2), [P, TT, 4]), ALU.subtract))
            dve.wait_ge(expd, 1 + ONE)
            link(dve.tensor_reduce(den[:, :], t4b[:, :, :], AX.X, ALU.add))
            link(dve.tensor_tensor(t44[:, :, :, :], el.rearrange("p t (g e) -> p t e g", g=4),
                                   b3(goh[:, :, :].unsqueeze(2), [P, TT, 4, 4]), ALU.mult))
            link(dve.tensor_reduce(sel[:, :, :], t44[:, :, :, :], AX.X, ALU.add))
            first_max(sel[:, :, :], m1[:, :], eoh[:, 0, :, :])
            link(dve.scalar_tensor_tensor(out=sel[:, :, :], in0=eoh[:, 0, :, :], scalar=NEG, in1=sel[:, :, :], op0=ALU.mult, op1=ALU.add))
            first_max(sel[:, :, :], m2[:, :], eoh[:, 1, :, :])
            link(dve.tensor_tensor(e2v[:, :], m2[:, :], m1[:, :], ALU.subtract))
            dve.wait_ge(expd, 2 + ONE)
            link(dve.tensor_scalar(m1[:, :], e2v[:, :], 1.0, None, ALU.add))
            link(dve.tensor_tensor(m1[:, :], m1[:, :], den[:, :], ALU.mult))
            link(dve.reciprocal(s.wt[:, 0, :], m1[:, :]))
            link(dve.tensor_tensor(s.wt[:, 1, :], s.wt[:, 0, :], e2v[:, :], ALU.mult))
            for k in range(2):
                link(dve.tensor_tensor(oh[:, k, :, :].rearrange("p t (g e) -> p t g e", g=4),
                                       b3(goh[:, :, :].unsqueeze(3), [P, TT, 4, 4]),
                                       b3(eoh[:, k, :, :].unsqueeze(2), [P, TT, 4, 4]), ALU.mult))
            link(dve.tensor_tensor(both[:, :, :], oh[:, 0, :, :], oh[:, 1, :, :], ALU.add))
            dve.sem_inc(stacked, 1)
            link(dve.memset(off[:, 0, :], 0.0))
            dve.wait_ge(ranked, 1 + ONE)
            for t in range(TT):
                link(dve.tensor_tensor(off[:, t + 1, :], ps[:, 1, t * NE:(t + 1) * NE], off[:, t, :], ALU.add))
            link(dve.tensor_tensor(cnt8[:, :, :], b3(off[:, TT, :].unsqueeze(2), [P, NE, 8]), b3(s.blk128.unsqueeze(1), [P, NE, 8]), ALU.is_gt))
            link(dve.tensor_reduce(nb[:, :], cnt8[:, :, :], AX.X, ALU.add))
            link(dve.tensor_tensor_scan(ends[:, :], s.ones[:, 0:NE], nb[:, :], 0.0, ALU.mult, ALU.add))
            link(dve.tensor_tensor(starts[:, :], ends[:, :], nb[:, :], ALU.subtract))
            link(dve.tensor_tensor(b32[:, :, :], b3(ends[:, :].unsqueeze(1), [P, 32, NE]), b3(s.iota.unsqueeze(2), [P, 32, NE]), ALU.is_le))
            link(dve.tensor_reduce(be[:, :], b32[:, :, :], AX.X, ALU.add))
            link(dve.tensor_scalar(bei[:, :], be[:, :], float(NE - 1), None, ALU.min))
            link(dve.tensor_copy(bei[:, 31:32], ends[:, NE - 1:NE]))
            link(dve.tensor_tensor(rank[:, :, :], ps[:, 0, 0:TT * NE].rearrange("p (t e) -> p t e", e=NE), off[:, 0:TT, :], ALU.add))
            link(dve.scalar_tensor_tensor(out=rank[:, :, :], in0=b3(starts[:, :].unsqueeze(1), [P, TT, NE]), scalar=float(P),
                                          in1=rank[:, :, :], op0=ALU.mult, op1=ALU.add))
            link(dve.tensor_tensor(t16[:, :, :, :], oh[:, :, :, :], b3(rank[:, :, :].unsqueeze(1), [P, 2, TT, NE]), ALU.mult))
            link(dve.tensor_reduce(slotf[:, :, :], t16[:, :, :, :], AX.X, ALU.add))
            link(dve.tensor_copy(s.slot[:, :, :], slotf[:, :, :]))
            dve.sem_inc(stacked, 1)

        @block.scalar
        def _(act):
            act.wait_ge(step, 7 + ONE)
            act.activation(t4b[:, :, :], t4b[:, :, :], ACT.Exp).then_inc(expd, 1)
            act.wait_ge(step, 24 + ONE)
            act.activation(e2v[:, :], e2v[:, :], ACT.Exp).then_inc(expd, 1)

        @block.tensor
        def _(pe):
            pe.wait_ge(stacked, 1 + ONE)
            flat = both[:, :, :].rearrange("p t e -> p (t e)")
            pe.matmul(ps[:, 0, 0:TT * NE], s.before, flat, start=True, stop=True)
            pe.matmul(ps[:, 1, 0:TT * NE], s.ones, flat, start=True, stop=True).then_inc(ranked, 1)

        @block.sync
        def _(sp):
            sp.wait_ge(zeroed, 1 + ONE)
            sp.dma_start(s.tok_dram.rearrange("(p n) o -> p (n o)", p=P), zeros[:, :]).then_inc(cleared, 16)
            sp.wait_ge(cleared, 16 + ONE)

        @block.gpsimd
        def _(pool):
            pool.wait_ge(cleared, 16 + ONE)
            pool.wait_ge(tok_ready, 1 + ONE)
            pool.wait_ge(stacked, 2 + ONE)
            for k in range(2):
                for t in range(TT):
                    pool.indirect_dma_start(out=s.tok_dram, out_offset=bass.IndirectOffsetOnAxis(ap=s.slot[:, k, t:t + 1], axis=0),
                                            in_=toki[:, t:t + 1], in_offset=None).then_inc(scattered, 16)
            pool.wait_ge(scattered, 16 * 2 * TT)


def experts(nc, s):
    with ExitStack() as c:
        def sb(name, shape, dt=F32):
            return c.enter_context(nc.sbuf_tensor("ex_" + name, shape, dt))

        def sem(name):
            return counter(nc, c, "ex_" + name)
        wg = sb("wg", [P, 2, KD, FF])
        wu = sb("wu", [P, 2, KD, FF])
        wd = sb("wd", [P, 2, KF, D])
        idx = sb("idx", [P, 2], I32)
        x = sb("x", [P, 2, D])
        xT = sb("xT", [P, 2, KD, P])
        sg = sb("sg", [P, FF])
        hid = sb("hid", [P, FF])
        hT = sb("hT", [P, KF, P])
        y = sb("y", [P, D])
        spare = sb("spare", [P, 1])
        act_spare = sb("act_spare", [P, 1])
        pt = c.enter_context(nc.psum_tensor("ex_pt", [P, 2, 512], F32))
        ph = c.enter_context(nc.psum_tensor("ex_ph", [P, 512], F32))
        pg = c.enter_context(nc.psum_tensor("ex_pg", [P, 512], F32))
        pu = c.enter_context(nc.psum_tensor("ex_pu", [P, 512], F32))
        py = c.enter_context(nc.psum_tensor("ex_py", [P, 2, 512], F32))
        spared = sem("spared")
        wg_in, wu_in, wd_in = ([sem(n + str(u)) for u in range(2)] for n in ("wg_in", "wu_in", "wd_in"))
        idx_in, x_in = ([dma_counter(nc, c, f"ex_{n}{u}") for u in range(2)] for n in ("idx_in", "x_in"))
        x_turned, x_copied, gated, upped, silu, hidden, h_turned, h_copied, downed, y_half, y_out = (
            sem(n) for n in ("x_turned", "x_copied", "gated", "upped", "silu", "hidden", "h_turned", "h_copied", "downed", "y_half", "y_out"))
        nc.all_engine_barrier()
        block = c.enter_context(nc.Block())

        def used_blocks(eng):
            return eng.value_load(s.blk[0:1, 31:32], min_val=1, max_val=NBLK)

        def steps(eng, full, tail):
            n = used_blocks(eng)
            full(0, 0, 0)
            with eng.Fori(0, NBLK // 2) as i:
                for b, k, u in ((i * 2 + 1, i, 1), (i * 2 + 2, i + 1, 0)):
                    with eng.If(b < n):
                        full(b, k, u)
                    if tail is not None:
                        with eng.If(b == n):
                            tail(b, k, u)
            if tail is not None:
                with eng.If(n == NBLK):
                    tail(NBLK, NBLK // 2, 1)
            return n

        @block.sync
        def _(sp):
            def load(b, k, u):
                e = sp.value_load(s.blk[0:1, ds(b, 1)], min_val=0, max_val=NE - 1)
                static = isinstance(b, int)
                if not static:
                    sp.wait_ge(gated, b - 1 + ONE)
                sp.dma_start(wg[:, u, :, :], s.inp["moe_w_gate"].rearrange("e (k p) f -> e p k f", p=P)[ds(e, 1)]
                             .rearrange("o p k f -> p (o k) f")).then_inc(wg_in[u], 16)
                if not static:
                    sp.wait_ge(upped, b - 1 + ONE)
                sp.dma_start(wu[:, u, :, :], s.inp["moe_w_up"].rearrange("e (k p) f -> e p k f", p=P)[ds(e, 1)]
                             .rearrange("o p k f -> p (o k) f")).then_inc(wu_in[u], 16)
                if not static:
                    sp.wait_ge(downed, b - 1 + ONE)
                sp.dma_start(wd[:, u, :, :], s.inp["moe_w_down"].rearrange("e (k p) f -> e p k f", p=P)[ds(e, 1)]
                             .rearrange("o p k f -> p (o k) f")).then_inc(wd_in[u], 16)
            steps(sp, load, None)

        @block.gpsimd
        def _(pool):
            tok = s.tok_dram.rearrange("(b p) o -> b p o", p=P)

            def gather(b, k, u):
                if not isinstance(b, int):
                    pool.wait_ge(x_turned, b - 1 + ONE)
                pool.dma_start(idx[:, u:u + 1], tok[ds(b, 1)].rearrange("a p o -> p (a o)")).then_inc(idx_in[u], 16)
                pool.wait_ge(idx_in[u], k * 16 + 16)
                pool.wait_ge(spared, b + ONE)
                pool.tensor_tensor(spare[:, 0:1], s.eps, s.eps, ALU.add).then_inc(spared, 1)
                pool.indirect_dma_start(out=x[:, u, :], out_offset=None, in_=s.h_dram,
                                        in_offset=bass.IndirectOffsetOnAxis(ap=idx[:, u:u + 1], axis=0)).then_inc(x_in[u], 16)
            steps(pool, gather, gather)

        @block.tensor
        def _(pe):
            def turn_x(b, k, u):
                pe.wait_ge(x_in[u], k * 16 + 16)
                pe.wait_ge(x_copied, b + ONE)
                for j in range(KD):
                    mm = pe.transpose(pt[:, j // 4, (j % 4) * P:(j % 4 + 1) * P], x[:, u, j * P:(j + 1) * P], s.ident)
                mm.then_inc(x_turned, 1)

            def turn_h(b):
                pe.wait_ge(hidden, b + 1 + ONE)
                pe.wait_ge(h_copied, b + ONE)
                for j in range(KF):
                    mm = pe.transpose(ph[:, j * P:(j + 1) * P], hid[:, j * P:(j + 1) * P], s.ident)
                mm.then_inc(h_turned, 1)

            def down(b, k, u):
                pe.wait_ge(h_copied, b + 1 + ONE)
                pe.wait_ge(wd_in[u], k * 16 + 16 + ONE)
                pe.wait_ge(y_half, b * 2 + ONE)
                for half in range(2):
                    for j in range(KF):
                        mm = pe.matmul(py[:, half, :], hT[:, j, :], wd[:, u, j, half * 512:(half + 1) * 512],
                                       start=(j == 0), stop=(j == KF - 1))
                mm.then_inc(downed, 1)

            def full(b, k, u):
                first = isinstance(b, int)
                if first:
                    turn_x(0, 0, 0)
                pe.wait_ge(x_copied, b + 1 + ONE)
                pe.wait_ge(wg_in[u], k * 16 + 16 + ONE)
                pe.wait_ge(silu, b + ONE)
                for j in range(KD):
                    mm = pe.matmul(pg[:, :], xT[:, u, j, :], wg[:, u, j, :], start=(j == 0), stop=(j == KD - 1))
                mm.then_inc(gated, 1)
                if not first:
                    turn_h(b - 1)
                pe.wait_ge(wu_in[u], k * 16 + 16 + ONE)
                pe.wait_ge(hidden, b + ONE)
                for j in range(KD):
                    mm = pe.matmul(pu[:, :], xT[:, u, j, :], wu[:, u, j, :], start=(j == 0), stop=(j == KD - 1))
                mm.then_inc(upped, 1)
                turn_x(b + 1, k + u, 1 - u)
                if not first:
                    down(b - 1, k - (1 - u), 1 - u)

            def tail(b, k, u):
                turn_h(b - 1)
                down(b - 1, k - (1 - u), 1 - u)
            steps(pe, full, tail)

        @block.scalar
        def _(act):
            y_rows = s.y_dram.rearrange("(b p) n -> b p n", p=P)

            def tail(b, k, u):
                act.wait_ge(h_turned, b + ONE)
                act.wait_ge(downed, b - 1 + ONE)
                act.activation(hT[:, :, :].rearrange("p a b -> p (a b)"), ph[:, :], ACT.Copy).then_inc(h_copied, 1)
                act.wait_ge(downed, b + ONE)
                act.wait_ge(y_out, (b - 1) * 16 + ONE)
                act.activation(y[:, 0:512], py[:, 0, :], ACT.Copy).then_inc(y_half, 1)
                act.wait_ge(y_half, b * 2 + ONE)
                act.dma_start(y_rows[ds(b - 1, 1)].rearrange("o p n -> p (o n)"), y[:, :]).then_inc(y_out, 16)

            def full(b, k, u):
                act.wait_ge(gated, b + 1 + ONE)
                act.wait_ge(hidden, b + ONE)
                act.activation(sg[:, :], pg[:, :], ACT.Silu).then_inc(silu, 1)
                if not isinstance(b, int):
                    tail(b, k, u)
            n = steps(act, full, tail)
            act.wait_ge(y_out, n * 16 + ONE)
            act.activation(act_spare[:, :], s.eps, ACT.Copy)

        @block.vector
        def _(dve):
            def copy_x(b, u):
                dve.wait_ge(x_turned, b + 1 + ONE)
                if not isinstance(b, int):
                    dve.wait_ge(upped, b - 1 + ONE)
                dve.tensor_copy(xT[:, u, :, :].rearrange("p a b -> p (a b)"), pt[:, :, :].rearrange("p a b -> p (a b)")).then_inc(x_copied, 1)

            def tail(b, k, u):
                dve.wait_ge(downed, b + ONE)
                dve.wait_ge(y_out, (b - 1) * 16 + ONE)
                dve.tensor_copy(y[:, 512:1024], py[:, 1, :]).then_inc(y_half, 1)

            def full(b, k, u):
                first = isinstance(b, int)
                if first:
                    copy_x(0, 0)
                dve.wait_ge(silu, b + 1 + ONE)
                dve.wait_ge(upped, b + 1 + ONE)
                dve.wait_ge(h_turned, b + ONE)
                dve.tensor_tensor(hid[:, :], pu[:, :], sg[:, :], ALU.mult).then_inc(hidden, 1)
                copy_x(b + 1, 1 - u)
                if not first:
                    tail(b, k, u)
            steps(dve, full, tail)


def combine(nc, s, out):
    with ExitStack() as c:
        rows = c.enter_context(nc.sbuf_tensor("cb_rows", [P, 4, 2, D], F32))
        come = [[dma_counter(nc, c, f"cb_in{t}_{k}") for k in range(2)] for t in range(4)]
        added, out_done = (counter(nc, c, "cb_" + n) for n in ("added", "out_done"))
        nc.all_engine_barrier()
        block = c.enter_context(nc.Block())
        out_rows = out.rearrange("o (t p) n -> t p (o n)", p=P)

        @block.gpsimd
        def _(pool):
            for t in range(TT):
                if t >= 4:
                    pool.wait_ge(added, 2 * (t - 4) + 2 + ONE)
                for k in range(2):
                    pool.indirect_dma_start(out=rows[:, t % 4, k, :], out_offset=None, in_=s.y_dram,
                                            in_offset=bass.IndirectOffsetOnAxis(ap=s.slot[:, k, t:t + 1], axis=0)).then_inc(come[t % 4][k], 16)

        @block.vector
        def _(dve):
            for t in range(TT):
                for k in range(2):
                    dve.wait_ge(come[t % 4][k], 16 * (t // 4 + 1))
                    if k:
                        dve.wait_ge(added, 2 * t + 1 + ONE)
                    dve.scalar_tensor_tensor(out=s.x1[:, t, :], in0=rows[:, t % 4, k, :], scalar=s.wt[:, k, t:t + 1], in1=s.x1[:, t, :],
                                             op0=ALU.mult, op1=ALU.add).then_inc(added, 1)

        @block.sync
        def _(sp):
            for t in range(TT):
                sp.wait_ge(added, 2 * t + 2 + ONE)
                sp.dma_start(out_rows[t], s.x1[:, t, :]).then_inc(out_done, 16)
            sp.wait_ge(out_done, 16 * TT + ONE)




def hybrid_layer(nc, inp, consts, params, out):
    def dram(name, shape, dt=F32):
        return nc.dram_tensor(name, shape, dt, kind="Internal").ap()
    s = Shared()
    s.inp = inp
    s.bias_dram = dram("bias_table", (8, GRID_W, 15, GRID_W))
    s.h_dram = dram("ffn_rows", (SEQ, D))
    s.y_dram = dram("expert_rows", (NBLK * P, D))
    s.tok_dram = dram("slot_tokens", (32 * P, 1), I32)
    top = ExitStack()
    cst = top.enter_context(nc.sbuf_tensor("cst", [P, NCC], F32))
    par = top.enter_context(nc.sbuf_tensor("par", [P, NPC], F32))
    s.par = lambda name, n: par[:, PCOL[name]:PCOL[name] + n]

    def const(name):
        return cst[:, CCOL[name]:CCOL[name] + CCOLS[name]]
    s.ident, s.pair_ones, s.ones, s.before, s.fold = (const(n) for n in ("ident", "pair_ones", "ones", "before", "fold"))
    s.eps, s.gn_eps, s.iota, s.blk128, s.token = (const(n) for n in ("eps", "gn_eps", "iota", "blk128", "token"))
    s.l_mask = [const("l_mask_f"), const("l_mask_b")]
    s.x_mask = [const("x_mask_f"), const("x_mask_b")]
    with top:
        params_in = top.enter_context(nc.semaphore("params_in"))
        with nc.Block() as block:
            @block.sync
            def _(sp):
                sp.dma_start(cst[:, :], consts).then_inc(params_in, 16)
                sp.dma_start(par[:, :], params).then_inc(params_in, 16)
                sp.wait_ge(params_in, 32)
        s.mixT = top.enter_context(nc.sbuf_tensor("mixT", [P, KD, SEQ], F32))
        with ExitStack() as c_proj:
            s.proj = c_proj.enter_context(nc.sbuf_tensor("proj", [P, C_ALL, SEQ], F32))
            with ExitStack() as c_mem:
                s.mkT = c_mem.enter_context(nc.sbuf_tensor("mkT", [P, 2, NMEM], F32))
                s.mv = c_mem.enter_context(nc.sbuf_tensor("mv", [P, 2, 256], F32))
                with ExitStack() as c:
                    s.memT = c.enter_context(nc.sbuf_tensor("memT", [P, KD, NMEM], F32))
                    norm_transpose(nc, s, inp["mem"].rearrange("(t p) n -> t p n", p=P), 2, s.memT, "mem_w", "m")
                    memory_kv(nc, s)
                with ExitStack() as c:
                    s.hT = c.enter_context(nc.sbuf_tensor("hT", [P, KD, SEQ], F32))
                    norm_transpose(nc, s, inp["x"].rearrange("(t p) n -> t p n", p=P), TT, s.hT, "attn_w", "x")
                    bias_table(nc, s)
                    projection(nc, s)
                attention(nc, s, memory=True)
                attention(nc, s, memory=False)
            s.extra = c_proj.enter_context(nc.sbuf_tensor("extra", [P, 6, SEQ], F32))
            s.ec = c_proj.enter_context(nc.sbuf_tensor("ec", [P, 4, NCH], F32))
            shift(nc, s)
            gates(nc, s)
            scan(nc, s)
            rwkv_out(nc, s)
        s.x1 = top.enter_context(nc.sbuf_tensor("x1", [P, TT, D], F32))
        out_projection(nc, s)
        with nc.Block() as block:
            @block.gpsimd
            def _(pool):
                pool.sem_clear(range(params_in.num + 1, 256))
        s.logits = top.enter_context(nc.sbuf_tensor("logits", [P, TT, NG + NE], F32))
        s.wt = top.enter_context(nc.sbuf_tensor("wt", [P, 2, TT], F32))
        s.slot = top.enter_context(nc.sbuf_tensor("slot", [P, 2, TT], I32))
        s.blk = top.enter_context(nc.sbuf_tensor("blk", [P, 32], I32))
        ffn_norm_router(nc, s)
        routing(nc, s)
        experts(nc, s)
        combine(nc, s, out)


def constants(np):
    i, j = np.arange(P)[:, None], np.arange(P)[None, :]
    c = np.zeros((P, NCC), np.float32)

    def put(name, v):
        c[:, CCOL[name]:CCOL[name] + CCOLS[name]] = v
    put("ident", i == j)
    put("pair_ones", i // HD == j // HD)
    put("ones", 1)
    put("before", i < j)
    put("fold", i % HD == np.arange(HD)[None, :])
    put("eps", RMS_EPS)
    put("gn_eps", GN_EPS)
    same = i // HD == j // HD
    for name, before in (("f", lambda a, b: a < b), ("b", lambda a, b: a > b)):
        strict, incl = same & before(i, j), same & (before(i, j) | (i == j))
        put("l_mask_" + name, np.concatenate([-1.0 * (strict & (i // 16 == j // 16)), incl, strict, incl], 1))
        strict = same & before(j, i)
        b16, b32 = i // 16 == j // 16, i // 32 == j // 32
        put("x_mask_" + name, -1.0 * np.concatenate([strict & b16, strict & ~b16 & b32, strict & ~b32], 1))
    put("iota", np.arange(32)[None, :])
    put("blk128", P * np.arange(8)[None, :])
    put("token", i + P * np.arange(8)[None, :])
    return c


_INS = ['x', 'mem', 'w_in', 'na_rpb', 'rw_w2', 'rw_a2', 'rw_g2', 'w_mem_kv', 'w_out', 'ffn_norm_w', 'moe_w_group',
        'moe_b_group', 'moe_w_expert', 'moe_b_expert', 'moe_w_gate', 'moe_w_up', 'moe_w_down']


def kernel(**inputs):
    import numpy as _np
    import concourse.bacc as _bacc
    from concourse import mybir as _mybir
    from concourse.bass_utils import run_bass_kernel_spmd as _run

    nc = _bacc.Bacc("TRN2", target_bir_lowering=False, num_devices=1)

    def cols(name, reps=1):
        a = _np.asarray(inputs[name]).reshape(-1)
        return _np.concatenate([a] * reps).reshape(-1, P).T
    params = _np.concatenate([
        cols('attn_norm_w'), cols('mem_norm_w'), cols('na_q_norm_w', 2), cols('na_k_norm_w', 2), cols('mem_q_norm_w', 2),
        cols('mem_k_norm_w', 2), cols('rw_mu_prev'), cols('rw_mu_next'), cols('rw_w0'), cols('rw_a0'), cols('rw_k_k'),
        cols('rw_k_a'), cols('rw_r_k'), cols('rw_ln_w'), cols('rw_ln_b')], axis=1)
    neg_fill = _np.full((GRID_W, 15, GRID_W), NEG, _np.float32)
    arrays, aps = {}, {}

    def give(name, a):
        a = _np.ascontiguousarray(a)
        arrays[f"in_{name}"] = a
        return nc.dram_tensor(f"in_{name}", a.shape, _mybir.dt.from_np(a.dtype), kind="ExternalInput").ap()
    for name in _INS:
        a = _np.asarray(inputs[name])
        aps[name] = give(name, a if a.ndim == 2 else a[0])
    aps['neg_fill'] = give("neg_fill", neg_fill)
    consts, par = give("consts", constants(_np)), give("params", params)
    out = nc.dram_tensor("out", (1, SEQ, D), _mybir.dt.float32, kind="ExternalOutput").ap()
    hybrid_layer(nc, aps, consts, par, out)
    r = _run(nc, [arrays], core_ids=[0])
    return r.results[0]["out"]
```

```python
from contextlib import ExitStack
import math

import concourse.bass as bass
from concourse import mybir

F32 = mybir.dt.float32
I32 = mybir.dt.int32
ALU = mybir.AluOpType
ACT = mybir.ActivationFunctionType
AX = mybir.AxisListType
ds = bass.ds

P = 128
D = 1024
KD = D // P
SEQ = 1024
TT = SEQ // P
NMEM = 256
HD = 64
GRID_W = 64
ROWS = SEQ // GRID_W
KH, KW = 8, 16
NA_PAIRS = 4
RW_PAIRS = 2
MEM_PAIRS = 2
C_Q, C_K, C_V, C_RW, C_MQ, C_ALL = 0, 4, 8, 12, 21, 23
RWC = C_MQ - C_RW
CHUNK = 64
NCH = SEQ // CHUNK
NEG = -1.0e30
NG, NE, FF = 4, 16, 512
KF = FF // P
NBLK = 31
SURE = 2 * SEQ // P
RMS_EPS = 1e-6
GN_EPS = 64e-5
DECAY = math.exp(-0.5)

PCOLS = dict(attn_w=8, mem_w=8, naq_w=1, nak_w=1, mq_w=1, mk_w=1, mu_p=9, mu_n=9, w0=4, a0=4,
             k_k=2, k_a=2, r_k=2, ln_w=2, ln_b=2)
PCOL = {}
_n = 0
for _k, _w in PCOLS.items():
    PCOL[_k] = _n
    _n += _w
NPC = _n

CCOLS = dict(ident=128, pair_ones=128, ones=128, before=128, fold=64, eps=1, gn_eps=1,
             l_mask_f=512, l_mask_b=512, x_mask_f=384, x_mask_b=384, iota=32, blk128=8, token=8)
CCOL = {}
_n = 0
for _k, _w in CCOLS.items():
    CCOL[_k] = _n
    _n += _w
NCC = _n


class Shared:
    pass


ONE = 1


def counter(nc, stack, name):
    sem = stack.enter_context(nc.semaphore(name))
    nc.gpsimd.sem_inc(sem, ONE)
    return sem


def dma_counter(nc, stack, name):
    return stack.enter_context(nc.semaphore(name))


def window_start(r):
    return min(max(r - KH // 2, 0), ROWS - KH)


def norm_transpose(nc, s, src, tiles, dst, w_col, tag):
    with ExitStack() as c:
        xt = c.enter_context(nc.sbuf_tensor("nt_xt" + tag, [P, 2, D], F32))
        xn = c.enter_context(nc.sbuf_tensor("nt_xn" + tag, [P, 2, D], F32))
        sq = c.enter_context(nc.sbuf_tensor("nt_sq" + tag, [P, 2, D], F32))
        st = c.enter_context(nc.sbuf_tensor("nt_st" + tag, [P, 2, 4], F32))
        ps = c.enter_context(nc.psum_tensor("nt_ps" + tag, [P, 2, KD, P], F32))
        loaded = [counter(nc, c, f"nt_loaded{u}{tag}") for u in range(2)]
        std_ready = counter(nc, c, "nt_std" + tag)
        sum_ready = counter(nc, c, "nt_sum" + tag)
        inv_ready = counter(nc, c, "nt_inv" + tag)
        normed = counter(nc, c, "nt_normed" + tag)
        turned = counter(nc, c, "nt_turned" + tag)
        stored = counter(nc, c, "nt_stored" + tag)
        nc.all_engine_barrier()
        block = c.enter_context(nc.Block())

        @block.sync
        def _(sp):
            with sp.Fori(0, tiles // 2) as i:
                for u in range(2):
                    sp.wait_ge(normed, i * 2 + ONE)
                    sp.dma_start(xt[:, u, :], src[ds(i * 2 + u, 1)].rearrange("a p d -> p (a d)")).then_inc(loaded[u], 16)

        @block.scalar
        def _(act):
            with act.Fori(0, tiles // 2) as i:
                for u in range(2):
                    act.wait_ge(loaded[u], i * 16 + 16 + ONE)
                    act.wait_ge(inv_ready, i * 2 + ONE)
                    act.activation(sq[:, u, :], xt[:, u, :], ACT.Square, accum_out=st[:, u, 0:1]).then_inc(sum_ready, 1)
                for u in range(2):
                    act.wait_ge(sum_ready, i * 2 + u + 1 + ONE)
                    act.activation(st[:, u, 1:2], st[:, u, 0:1], ACT.Sqrt, bias=s.eps, scale=1.0 / D).then_inc(std_ready, 1)

        @block.vector
        def _(dve):
            with dve.Fori(0, tiles // 2) as i:
                for u in range(2):
                    dve.wait_ge(std_ready, i * 2 + u + 1 + ONE)
                    dve.reciprocal(st[:, u, 2:3], st[:, u, 1:2]).then_inc(inv_ready, 1)
                for u in range(2):
                    dve.wait_ge(inv_ready, i * 2 + u + 1 + ONE)
                    dve.wait_ge(turned, i * 2 + ONE)
                    dve.tensor_scalar(xn[:, u, :], xt[:, u, :], st[:, u, 2:3], None, ALU.mult).then_inc(normed, 1)
                for u in range(2):
                    dve.wait_ge(turned, i * 2 + u + 1 + ONE)
                    dve.tensor_tensor(dst[:, :, ds((i * 2 + u) * P, P)], ps[:, u, :, :],
                                      s.par(w_col, KD).unsqueeze(2).to_broadcast([P, KD, P]), ALU.mult).then_inc(stored, 1)

        @block.tensor
        def _(pe):
            with pe.Fori(0, tiles // 2) as i:
                for u in range(2):
                    pe.wait_ge(normed, i * 2 + u + 1 + ONE)
                    pe.wait_ge(stored, i * 2 + ONE)
                    for k in range(KD):
                        mm = pe.transpose(ps[:, u, k, :], xn[:, u, k * P:(k + 1) * P], s.ident)
                    mm.then_inc(turned, 1)


def memory_kv(nc, s):
    with ExitStack() as c:
        w = c.enter_context(nc.sbuf_tensor("kv_w", [P, KD, 512], F32))
        ps = c.enter_context(nc.psum_tensor("kv_ps", [P, 4, 512], F32))
        loaded = counter(nc, c, "kv_loaded")
        done = counter(nc, c, "kv_done")
        nc.all_engine_barrier()
        block = c.enter_context(nc.Block())

        @block.sync
        def _(sp):
            sp.dma_start(w[:, :, :], s.inp["w_mem_kv"].rearrange("(k p) n -> p k n", p=P)).then_inc(loaded, 16)

        @block.tensor
        def _(pe):
            pe.wait_ge(loaded, 16 + ONE)
            for j in range(2):
                for k in range(KD):
                    mm = pe.matmul(ps[:, j, 0:NMEM], w[:, k, j * P:(j + 1) * P], s.memT[:, k, :],
                                   start=(k == 0), stop=(k == KD - 1))
                mm.then_inc(done, 1)
            for m in range(2):
                for k in range(KD):
                    mm = pe.matmul(ps[:, 2 + m, 0:256], s.memT[:, k, m * P:(m + 1) * P], w[:, k, 256:512],
                                   start=(k == 0), stop=(k == KD - 1))
                mm.then_inc(done, 1)

        @block.vector
        def _(dve):
            for j in range(2):
                dve.wait_ge(done, j + 1 + ONE)
                dve.tensor_copy(s.mkT[:, j, :], ps[:, j, 0:NMEM])

        @block.scalar
        def _(act):
            for m in range(2):
                act.wait_ge(done, m + 3 + ONE)
                act.activation(s.mv[:, m, :], ps[:, 2 + m, 0:256], ACT.Copy)


def projection(nc, s):
    NORMED = 2 + 2 * NA_PAIRS
    with ExitStack() as c:
        w = c.enter_context(nc.sbuf_tensor("pj_w", [P, 2, KD, P], F32))
        ps = c.enter_context(nc.psum_tensor("pj_ps", [P, 2, 2, 512], F32))
        ps_n = c.enter_context(nc.psum_tensor("pj_ps_n", [P, SEQ], F32))
        qw = c.enter_context(nc.sbuf_tensor("pj_qw", [P, 2], F32))
        spare = c.enter_context(nc.sbuf_tensor("pj_spare", [P, 1], F32))
        loaded = [counter(nc, c, f"pj_loaded{u}") for u in range(2)]
        zeroed, filled = counter(nc, c, "pj_zeroed"), dma_counter(nc, c, "pj_filled")
        done = counter(nc, c, "pj_done")
        out0 = counter(nc, c, "pj_out_act")
        out1 = counter(nc, c, "pj_out_dve")
        squared, sum_ready, std_ready, inv_ready, normed, qscaled = (
            counter(nc, c, "pj_" + n) for n in ("squared", "sum", "std", "inv", "normed", "qscaled"))
        nc.all_engine_barrier()
        block = c.enter_context(nc.Block())
        w_in = s.inp["w_in"].rearrange("(k p) n -> p k n", p=P)
        sq, std, zero = (s.mixT[:, n, :] for n in range(3))

        def steps(eng, step):
            def chunk(t):
                return s.proj[:, ds(t - 2, 1), :]
            memory_k = s.mkT[:, :, :].rearrange("p a n -> p (a n)").unsqueeze(1)
            step(0, 0, 0, C_MQ, memory_k, s.par("mk_w", 1))
            step(1, 0, 1, C_MQ + 1, s.proj[:, C_MQ:C_MQ + 1, :], qw[:, 1:2])
            step(2, 1, 0, 0, s.proj[:, C_MQ + 1:C_MQ + 2, :], qw[:, 1:2])
            for first, weight in ((3, qw[:, 0:1]), (3 + NA_PAIRS, s.par("nak_w", 1))):
                with eng.Fori(0, NA_PAIRS // 2) as i:
                    t = i * 2 + first
                    step(t, i + first // 2, 1, t - 2, chunk(t - 1), weight)
                    step(t + 1, i + (first // 2 + 1), 0, t - 1, chunk(t), weight)
            first = 1 + NORMED
            with eng.Fori(0, (C_ALL - first) // 2) as i:
                t = i * 2 + first
                step(t, i + first // 2, 1, t - 2, None, None)
                step(t + 1, i + (first // 2 + 1), 0, t - 1, None, None)

        @block.gpsimd
        def _(pool):
            pool.memset(zero, 0.0).then_inc(zeroed, 1)
            pool.wait_ge(zeroed, 1 + ONE)
            for b in range(SURE, NBLK):
                pool.dma_start(s.y_dram[b * P:(b + 1) * P, :], zero).then_inc(filled, 16)
            pool.wait_ge(filled, 16 * (NBLK - SURE))

        @block.sync
        def _(sp):
            def step(t, k, u, col, item, weight):
                if not isinstance(t, int) or t >= 2:
                    sp.wait_ge(done, t * 2 - 2 + ONE)
                sp.dma_start(w[:, u, :, :], w_in[:, :, ds(col * P, P)]).then_inc(loaded[u], 16)
            steps(sp, step)

        @block.tensor
        def _(pe):
            def step(t, k, u, col, item, weight):
                pe.wait_ge(loaded[u], k * 16 + 16 + ONE)
                if not isinstance(t, int) or t >= 2:
                    pe.wait_ge(out0, t - 1 + ONE)
                    pe.wait_ge(out1, t - 1 + ONE)
                for half in range(2):
                    for n in range(KD):
                        mm = pe.matmul(ps[:, u, half, :], w[:, u, n, :], s.hT[:, n, half * 512:(half + 1) * 512],
                                       start=(n == 0), stop=(n == KD - 1))
                    mm.then_inc(done, 1)
                    if half == 0 and item is not None:
                        pe.wait_ge(squared, t + 1 + ONE)
                        pe.wait_ge(std_ready, t + ONE)
                        for a in range(item.shape[2] // 512):
                            mm = pe.matmul(ps_n[:, a * 512:(a + 1) * 512], s.pair_ones, sq[:, a * 512:(a + 1) * 512], start=True, stop=True)
                        mm.then_inc(sum_ready, 1)
            steps(pe, step)

        @block.scalar
        def _(act):
            def step(t, k, u, col, item, weight):
                if item is not None:
                    ln = item.shape[2]
                    act.wait_ge(out0, t + ONE)
                    act.wait_ge(out1, t + ONE)
                    act.wait_ge(sum_ready, t + ONE)
                    act.activation(spare[:, :], s.eps, ACT.Copy)
                    act.activation(sq[:, 0:ln].unsqueeze(1), item, ACT.Square).then_inc(squared, 1)
                    act.wait_ge(sum_ready, t + 1 + ONE)
                    act.wait_ge(normed, t + ONE)
                    act.activation(std[:, 0:ln], ps_n[:, 0:ln], ACT.Sqrt, bias=s.eps, scale=1.0 / HD).then_inc(std_ready, 1)
                act.wait_ge(done, t * 2 + 1 + ONE)
                act.activation(s.proj[:, ds(col, 1), 0:512], ps[:, u, 0:1, :], ACT.Copy).then_inc(out0, 1)
            steps(act, step)

        @block.vector
        def _(dve):
            for n, name in enumerate(("naq_w", "mq_w")):
                dve.tensor_scalar(qw[:, n:n + 1], s.par(name, 1), HD ** -0.5, None, ALU.mult).then_inc(qscaled, 1)
            dve.wait_ge(qscaled, 2 + ONE)

            def step(t, k, u, col, item, weight):
                if item is not None:
                    ln = item.shape[2]
                    dve.wait_ge(std_ready, t + 1 + ONE)
                    dve.reciprocal(std[:, 0:ln], std[:, 0:ln]).then_inc(inv_ready, 1)
                    dve.wait_ge(inv_ready, t + 1 + ONE)
                    dve.scalar_tensor_tensor(out=item, in0=item, scalar=weight, in1=std[:, 0:ln].unsqueeze(1),
                                             op0=ALU.mult, op1=ALU.mult).then_inc(normed, 1)
                dve.wait_ge(done, t * 2 + 2 + ONE)
                dve.tensor_copy(s.proj[:, ds(col, 1), 512:1024], ps[:, u, 1:2, :]).then_inc(out1, 1)
            steps(dve, step)


def bias_table(nc, s):
    rpb = s.inp["na_rpb"]
    row = 15 * GRID_W
    H = 8
    with ExitStack() as c:
        filled = counter(nc, c, "bt_filled")
        placed = counter(nc, c, "bt_placed")
        nc.all_engine_barrier()
        block = c.enter_context(nc.Block())
        t = s.bias_dram

        def spot(h, start, dims):
            return bass.AP(t.tensor, h * GRID_W * row + start, dims)

        @block.sync
        def _(sp):
            for h in range(H):
                sp.dma_start(t[h], s.inp["neg_fill"]).then_inc(filled, 16)
            sp.wait_ge(filled, 16 * H + ONE)
            n = 0
            for h in range(H):
                src = bass.AP(rpb.tensor, h * 15 * 31 + KW - 1 - KW // 2, [[0, 49], [31, 15], [1, KW]])
                sp.dma_start(spot(h, 8 * row, [[row + 1, 49], [GRID_W, 15], [1, KW]]), src).then_inc(placed, 16)
                n += 1
            for qc in [*range(8), *range(57, 64)]:
                cs = min(max(qc - KW // 2, 0), GRID_W - KW)
                src = bass.AP(rpb.tensor, cs - qc + KW - 1, [[15 * 31, H], [31, 15], [1, KW]])
                sp.dma_start(spot(0, qc * row + cs, [[GRID_W * row, H], [GRID_W, 15], [1, KW]]), src).then_inc(placed, 16)
                n += 1
            sp.wait_ge(placed, 16 * n + ONE)


def attention(nc, s, memory):
    tag = "m" if memory else "n"
    pairs = MEM_PAIRS if memory else NA_PAIRS
    nk = NMEM if memory else KH * GRID_W
    kt = nk // P
    G = ROWS
    nv = 0 if memory else ROWS - 1
    vb = -(-nv // 4)
    c_q, c_mix = (C_MQ, 6) if memory else (C_Q, 0)
    with ExitStack() as c:
        def sb(name, shape):
            return c.enter_context(nc.sbuf_tensor(f"at{tag}_{name}", shape, F32))

        def sem(name):
            return counter(nc, c, f"at{tag}_{name}")

        qbd = sb("qbd", [P, 2, G, P])
        tb = sb("tb", [P, 2, nk if memory else 15 * GRID_W])
        vst = sb("vst", [P, SEQ])
        v64 = sb("v64", [P, 16, P])
        ssb = sb("ssb", [P, 2, nk])
        pr = sb("pr", [P, 2, nk])
        pn = sb("pn", [P, 2, nk])
        ptb = sb("ptb", [P, 2, nk])
        nm = sb("nm", [P, 2, 4])
        rs = sb("rs", [P, 2, 4])
        ps_s = c.enter_context(nc.psum_tensor(f"at{tag}_ps_s", [P, 2, 512], F32))
        ps_t = c.enter_context(nc.psum_tensor(f"at{tag}_ps_t", [P, 2, 512], F32))
        ps_o = c.enter_context(nc.psum_tensor(f"at{tag}_ps_o", [P, 2, 512], F32))
        ps_v = c.enter_context(nc.psum_tensor(f"at{tag}_ps_v", [P, 2, 512], F32))
        zeroed, q_ready, v_copied, v_turned, v_ready = (sem(n) for n in ("zeroed", "q", "vcopy", "vturn", "vready"))
        bias_in = [sem(f"bias{u}") for u in range(2)]
        scored, biased, exped, inv_sum, normed = (sem(n) for n in ("scored", "biased", "exped", "invsum", "normed"))
        turned, pt_ready, summed, stored = (sem(n) for n in ("turned", "pt", "summed", "stored"))
        nc.all_engine_barrier()
        block = c.enter_context(nc.Block())

        def each_pair(eng, body):
            with eng.Fori(0, pairs // 2) as i:
                for u in range(2):
                    body(i * 2 + u, i, u)

        @block.sync
        def _(sp):
            def body(j, i, u):
                sp.wait_ge(biased, i * 2 * G + ONE)
                sp.dma_start(tb[:, u, :], s.bias_dram.rearrange("(j a) c d k -> j (a c) (d k)", a=2)[ds(j, 1)]
                             .rearrange("o p r -> p (o r)")).then_inc(bias_in[u], 16)
            if not memory:
                each_pair(sp, body)

        @block.gpsimd
        def _(pool):
            if memory:
                pool.memset(tb[:, :, :], 0.0).then_inc(zeroed, 1)
            pool.memset(qbd[:, 1, :, :], 0.0).then_inc(zeroed, 1)
            pool.wait_ge(zeroed, (3 if memory else 2) + ONE)

            def body(j, i, u):
                pool.wait_ge(scored, i * 2 * G + ONE)
                for h in range(2):
                    p0, p1 = h * HD, (h + 1) * HD
                    pool.tensor_copy(qbd[p0:p1, u, :, p0:p1], s.proj[p0:p1, ds(c_q + j, 1), :]
                                     .rearrange("p o (r c) -> p (o r) c", c=HD)).then_inc(q_ready, 1)
            each_pair(pool, body)

        @block.tensor
        def _(pe):
            def body(j, i, u):
                pe.wait_ge(q_ready, j * 2 + 2 + ONE)

                def turn_values():
                    pe.wait_ge(v_copied, j + 1 + ONE)
                    for b in range(vb):
                        pe.wait_ge(v_ready, j * vb + max(b - 1, 0) + ONE)
                        for m in range(4 * b, min(4 * b + 4, nv)):
                            mm = pe.transpose(ps_v[:, b % 2, (m % 4) * P:(m % 4 + 1) * P], vst[:, m * HD:m * HD + P], s.ident)
                        mm.then_inc(v_turned, 1)

                for r in range(G + 3):
                    if r < G:
                        pe.wait_ge(biased, j * G + max(r - 1, 0) + ONE)
                        ks = window_start(r) * GRID_W
                        keys = s.mkT[:, ds(j, 1), :] if memory else s.proj[:, ds(j + C_K, 1), ks:ks + nk]
                        pe.matmul(ps_s[:, r % 2, 0:nk].unsqueeze(1), qbd[:, u, r, :], keys, start=True, stop=True).then_inc(scored, 1)
                    if r == 1 and not memory:
                        turn_values()
                    if 2 <= r < G + 2:
                        q = r - 2
                        pe.wait_ge(normed, j * G + q + 1 + ONE)
                        pe.wait_ge(pt_ready, j * G + max(q - 1, 0) + ONE)
                        for a in range(kt):
                            mm = pe.transpose(ps_t[:, q % 2, a * P:(a + 1) * P], pn[:, q % 2, a * P:(a + 1) * P], s.ident)
                        mm.then_inc(turned, 1)
                    if r >= 3:
                        q = r - 3
                        if q == 0 and not memory:
                            pe.wait_ge(v_ready, j * vb + vb + ONE)
                        pe.wait_ge(pt_ready, j * G + q + 1 + ONE)
                        pe.wait_ge(stored, j * G + max(q - 1, 0) + ONE)
                        for a in range(kt):
                            if memory:
                                v = s.mv[:, a, u * P:(u + 1) * P]
                            else:
                                v = v64[:, window_start(q) + 2 * a, :]
                            mm = pe.matmul(ps_o[:, q % 2, 0:P], v, ptb[:, q % 2, a * P:(a + 1) * P],
                                           start=(a == 0), stop=(a == kt - 1))
                        mm.then_inc(summed, 1)
            each_pair(pe, body)

        @block.vector
        def _(dve):
            dve.memset(qbd[:, 0, :, :], 0.0).then_inc(zeroed, 1)
            if memory:
                dve.wait_ge(zeroed, 3 + ONE)

            def body(j, i, u):
                if not memory:
                    dve.wait_ge(bias_in[u], i * 16 + 16 + ONE)
                for r in range(G + 4):
                    if r < G:
                        t0 = 0 if memory else (window_start(r) - r + KH - 1) * GRID_W
                        dve.wait_ge(scored, j * G + r + 1 + ONE)
                        dve.wait_ge(exped, j * G + max(r - 1, 0) + ONE)
                        dve.memset(nm[:, r % 2, 1:2], 0.0)
                        dve.tensor_tensor_reduce(ssb[:, r % 2, :], ps_s[:, r % 2, 0:nk], tb[:, u, t0:t0 + nk], -1.0, 3.0e38,
                                                 ALU.add, ALU.min, nm[:, r % 2, 0:1]).then_inc(biased, 1)
                    if 1 <= r <= G:
                        q = r - 1
                        dve.wait_ge(exped, j * G + q + 1 + ONE)
                        dve.reciprocal(rs[:, q % 2, 1:2], rs[:, q % 2, 0:1]).then_inc(inv_sum, 1)
                        dve.wait_ge(inv_sum, j * G + q + 1 + ONE)
                        dve.wait_ge(turned, j * G + max(q - 1, 0) + ONE)
                        dve.tensor_scalar(pn[:, q % 2, :], pr[:, q % 2, :], rs[:, q % 2, 1:2], None, ALU.mult).then_inc(normed, 1)
                    if r >= 4:
                        q = r - 4
                        dve.wait_ge(summed, j * G + q + 1 + ONE)
                        for h in range(2):
                            p0, p1 = h * HD, (h + 1) * HD
                            o = dve.tensor_copy(s.mixT[p0:p1, ds(j + c_mix, 1), q * HD:(q + 1) * HD],
                                                ps_o[p0:p1, q % 2, p0:p1].unsqueeze(1))
                        o.then_inc(stored, 1)
            each_pair(dve, body)

        @block.scalar
        def _(act):
            def body(j, i, u):
                if not memory:
                    act.wait_ge(v_turned, j * vb + ONE)
                    act.activation(vst[:, :].unsqueeze(1), s.proj[:, ds(j + C_V, 1), :], ACT.Copy).then_inc(v_copied, 1)
                for r in range(G + 2):
                    if r < G:
                        act.wait_ge(biased, j * G + r + 1 + ONE)
                        act.wait_ge(normed, j * G + max(r - 1, 0) + ONE)
                        act.activation(pr[:, r % 2, :], ssb[:, r % 2, :], ACT.Exp, bias=nm[:, r % 2, 0:1], scale=-1.0,
                                       accum_out=rs[:, r % 2, 0:1]).then_inc(exped, 1)
                    if r < 2:
                        for b in range(r * 2, min(r * 2 + 2, vb)):
                            m = min(4, nv - 4 * b)
                            act.wait_ge(v_turned, j * vb + b + 1 + ONE)
                            act.wait_ge(summed, j * G + ONE)
                            act.activation(v64[:, 4 * b:4 * b + m, :].rearrange("p a b -> p (a b)"), ps_v[:, b % 2, 0:m * P],
                                           ACT.Copy).then_inc(v_ready, 1)
                    if r >= 2:
                        q = r - 2
                        act.wait_ge(turned, j * G + q + 1 + ONE)
                        act.wait_ge(summed, j * G + max(q - 1, 0) + ONE)
                        act.activation(ptb[:, q % 2, :], ps_t[:, q % 2, 0:nk], ACT.Copy).then_inc(pt_ready, 1)
            each_pair(act, body)


def shift(nc, s):
    with ExitStack() as c:
        keep = c.enter_context(nc.sbuf_tensor("sh_keep", [P, RWC], F32))
        summed, kept, scaled, mixed = (counter(nc, c, "sh_" + n) for n in ("sum", "keep", "scaled", "mixed"))
        nc.all_engine_barrier()
        block = c.enter_context(nc.Block())

        @block.vector
        def _(dve):
            dve.tensor_tensor(keep[:, :], s.par("mu_p", RWC), s.par("mu_n", RWC), ALU.add).then_inc(summed, 1)
            dve.wait_ge(summed, 1 + ONE)
            dve.tensor_scalar(keep[:, :], keep[:, :], -1.0, 1.0, ALU.mult, ALU.add).then_inc(kept, 1)
            for j in range(RWC):
                src, dst = s.proj[:, C_RW + j, :], s.proj[:, j, :]
                dve.wait_ge(scaled, j + 1 + ONE)
                dve.scalar_tensor_tensor(out=dst[:, 1:], in0=src[:, :-1], scalar=s.par("mu_p", RWC)[:, j:j + 1], in1=dst[:, 1:],
                                         op0=ALU.mult, op1=ALU.add).then_inc(mixed, 1)
                dve.wait_ge(mixed, 2 * j + 1 + ONE)
                dve.scalar_tensor_tensor(out=dst[:, :-1], in0=src[:, 1:], scalar=s.par("mu_n", RWC)[:, j:j + 1], in1=dst[:, :-1],
                                         op0=ALU.mult, op1=ALU.add).then_inc(mixed, 1)

        @block.scalar
        def _(act):
            act.wait_ge(kept, 1 + ONE)
            for j in range(RWC):
                act.activation(s.proj[:, j, :], s.proj[:, C_RW + j, :], ACT.Copy, scale=keep[:, j:j + 1]).then_inc(scaled, 1)


S_R, S_K, S_V, S_LW, S_LA, S_LG, S_PROD, S_BONUS = 0, 2, 4, 6, 7, 8, 9, 21
UNITS = [(d, p) for d in range(2) for p in range(RW_PAIRS)]


def prod(s, n):
    return s.proj[:, S_PROD + 4 * n:S_PROD + 4 * n + 4, :] if n < 3 else s.extra[:, 0:4, :]


def gates(nc, s):
    with ExitStack() as c:
        def sem(name):
            return counter(nc, c, "ga_" + name)
        tmp = c.enter_context(nc.sbuf_tensor("ga_tmp", [P, 12, SEQ], F32))
        go = s.mixT[:, 4, :]
        w2, a2, g2 = (s.mixT[:, 5, n * 256:(n + 1) * 256] for n in range(3))
        ps = c.enter_context(nc.psum_tensor("ga_ps", [P, 4, SEQ], F32))
        loaded, kk_scaled, act_in, grouped, taken = (sem(n) for n in ("loaded", "kk_scaled", "act_in", "grouped", "taken"))
        kk_steps, kd_steps, b_ready, go_ready, cum_steps = (sem(n) for n in ("kk_steps", "kd_steps", "b_ready", "go_ready", "cum"))
        exps, scaled_v, scaled_g, bonus_steps = (sem(n) for n in ("exps", "scaled_v", "scaled_g", "bonus"))
        nc.all_engine_barrier()
        block = c.enter_context(nc.Block())
        tanh_lw, sig_lg = s.proj[:, S_LW, :], s.proj[:, S_LG, :]

        def lw(n):
            return tmp[:, n, :]

        def a(n):
            return tmp[:, 4 + n, :]

        def kk(p):
            return tmp[:, 8 + p, :]

        def sq(p):
            return tmp[:, 10 + p, :]

        def cum(n):
            return s.proj[:, S_LG if n % 2 else S_LW, :]

        @block.sync
        def _(sp):
            sp.dma_start(w2[:, :], s.inp["rw_w2"].rearrange("d k n -> (d k) n")).then_inc(loaded, 16)
            sp.dma_start(a2[:, :], s.inp["rw_a2"].rearrange("d k n -> (d k) n")).then_inc(loaded, 16)
            sp.dma_start(g2[:, :], s.inp["rw_g2"]).then_inc(loaded, 16)

        @block.tensor
        def _(pe):
            def group(n, lhsT, rhs):
                if n >= 4:
                    pe.wait_ge(taken, n - 3 + ONE)
                for half in range(2):
                    mm = pe.matmul(ps[:, n % 4, half * 512:(half + 1) * 512], lhsT, rhs[:, half * 512:(half + 1) * 512],
                                   start=True, stop=True)
                mm.then_inc(grouped, 1)
            pe.wait_ge(loaded, 48 + ONE)
            pe.wait_ge(act_in, 1 + ONE)
            for n, (d, p) in enumerate(UNITS):
                group(n, w2[d * HD:(d + 1) * HD, p * P:(p + 1) * P], tanh_lw[d * HD:(d + 1) * HD, :])
            for n, (d, p) in enumerate(UNITS):
                group(4 + n, a2[d * HD:(d + 1) * HD, p * P:(p + 1) * P], s.proj[d * HD:(d + 1) * HD, S_LA, :])
            pe.wait_ge(act_in, 2 + ONE)
            for p in range(RW_PAIRS):
                group(8 + p, g2[:, p * P:(p + 1) * P], sig_lg)
            for p in range(RW_PAIRS):
                pe.wait_ge(act_in, 3 + p + ONE)
                group(10 + p, s.pair_ones, sq(p))

        @block.scalar
        def _(act):
            act.activation(tanh_lw, s.proj[:, S_LW, :], ACT.Tanh).then_inc(act_in, 1)
            act.activation(sig_lg, s.proj[:, S_LG, :], ACT.Sigmoid).then_inc(act_in, 1)
            for p in range(RW_PAIRS):
                act.wait_ge(kk_scaled, p + 1 + ONE)
                act.activation(sq(p), kk(p), ACT.Square).then_inc(act_in, 1)
            for n in range(4):
                act.wait_ge(grouped, n + 1 + ONE)
                act.activation(lw(n), ps[:, n % 4, :], ACT.Sigmoid, bias=s.par("w0", 4)[:, n:n + 1]).then_inc(taken, 1)
            for n in range(4):
                act.wait_ge(grouped, n + 5 + ONE)
                act.activation(a(n), ps[:, n % 4, :], ACT.Sigmoid, bias=s.par("a0", 4)[:, n:n + 1]).then_inc(taken, 1)
            for p in range(RW_PAIRS):
                act.wait_ge(grouped, p + 9 + ONE)
                act.activation(s.extra[:, 4 + p, :], ps[:, (8 + p) % 4, :], ACT.Copy).then_inc(taken, 1)
            for p in range(RW_PAIRS):
                act.wait_ge(grouped, p + 11 + ONE)
                act.activation(sq(p), ps[:, (10 + p) % 4, :], ACT.Sqrt).then_inc(taken, 1)
            for n in range(4):
                pr = prod(s, n)
                act.wait_ge(cum_steps, 3 * n + 3 + ONE)
                act.wait_ge(b_ready, 4 + ONE)
                incl = cum(n) if n < 2 else lw(n)
                act.activation(pr[:, 0, :], pr[:, 0, :], ACT.Exp, scale=-DECAY).then_inc(exps, 1)
                act.activation(pr[:, 1, :], incl, ACT.Exp, scale=-DECAY).then_inc(exps, 1)
                act.activation(a(n), incl, ACT.Exp, scale=DECAY).then_inc(exps, 1)
                act.activation(s.ec[:, n, :], cum(n).rearrange("p (c t) -> p c t", t=CHUNK)[:, :, CHUNK - 1], ACT.Exp,
                               scale=-DECAY).then_inc(exps, 1)

        @block.vector
        def _(dve):
            dve.memset(go, 1.0).then_inc(go_ready, 1)
            dve.wait_ge(go_ready, 1 + ONE)
            dve.memset(go.rearrange("p (c t) -> p c t", t=CHUNK)[:, :, 0:1], 0.0).then_inc(go_ready, 1)
            for p in range(RW_PAIRS):
                dve.tensor_scalar(kk(p), s.proj[:, S_K + p, :], s.par("k_k", 2)[:, p:p + 1], None, ALU.mult).then_inc(kk_scaled, 1)
            for n, (d, p) in enumerate(UNITS):
                dve.wait_ge(taken, n + 5 + ONE)
                dve.tensor_scalar(prod(s, n)[:, 3, :], a(n), 1.0, s.par("k_a", 2)[:, p:p + 1], ALU.subtract, ALU.mult).then_inc(kd_steps, 1)
                dve.wait_ge(kd_steps, 2 * n + 1 + ONE)
                dve.scalar_tensor_tensor(out=prod(s, n)[:, 3, :], in0=prod(s, n)[:, 3, :], scalar=1.0, in1=s.proj[:, S_K + p, :],
                                         op0=ALU.add, op1=ALU.mult).then_inc(kd_steps, 1)
            for p in range(RW_PAIRS):
                dve.wait_ge(kd_steps, 2 * (p + 2) + 2 + ONE)
                dve.tensor_tensor(s.proj[:, S_BONUS + p, :], prod(s, p)[:, 3, :], prod(s, p + 2)[:, 3, :], ALU.add).then_inc(bonus_steps, 1)
                dve.wait_ge(bonus_steps, 2 * p + 1 + ONE)
                dve.scalar_tensor_tensor(out=s.proj[:, S_BONUS + p, :], in0=s.proj[:, S_BONUS + p, :], scalar=s.par("r_k", 2)[:, p:p + 1],
                                         in1=s.proj[:, S_R + p, :], op0=ALU.mult, op1=ALU.mult).then_inc(bonus_steps, 1)
            for p in range(RW_PAIRS):
                dve.wait_ge(taken, 11 + p + ONE)
                dve.tensor_scalar(sq(p), sq(p), 1e-12, None, ALU.max).then_inc(kk_steps, 1)
                dve.wait_ge(kk_steps, 3 * p + 1 + ONE)
                dve.reciprocal(sq(p), sq(p)).then_inc(kk_steps, 1)
                dve.wait_ge(kk_steps, 3 * p + 2 + ONE)
                dve.tensor_tensor(kk(p), kk(p), sq(p), ALU.mult).then_inc(kk_steps, 1)
            dve.wait_ge(go_ready, 2 + ONE)

            def scale(n):
                d, p = UNITS[n]
                dve.wait_ge(exps, 4 * n + 4 + ONE)
                dve.tensor_tensor(prod(s, n)[:, 0, :], prod(s, n)[:, 0, :], kk(p), ALU.mult).then_inc(scaled_v, 1)
                dve.tensor_tensor(prod(s, n)[:, 1, :], prod(s, n)[:, 1, :], s.proj[:, S_R + p, :], ALU.mult).then_inc(scaled_v, 1)
            dve.wait_ge(kk_steps, 6 + ONE)
            for n, (d, p) in enumerate(UNITS):
                if n >= 2:
                    scale(n - 2)
                dve.tensor_tensor_scan(cum(n), go, lw(n), 0.0, ALU.mult, ALU.add).then_inc(cum_steps, 1)
                dve.wait_ge(cum_steps, 3 * n + 1 + ONE)
                if d == 0:
                    dve.tensor_tensor(prod(s, n)[:, 0, :], cum(n), lw(n), ALU.subtract).then_inc(cum_steps, 2)
                else:
                    total = cum(n).rearrange("p (c t) -> p c t", t=CHUNK)[:, :, CHUNK - 1:CHUNK].to_broadcast([P, NCH, CHUNK])
                    dve.tensor_tensor(prod(s, n)[:, 0, :].rearrange("p (c t) -> p c t", t=CHUNK), total,
                                      cum(n).rearrange("p (c t) -> p c t", t=CHUNK), ALU.subtract).then_inc(cum_steps, 1)
                    dve.wait_ge(cum_steps, 3 * n + 2 + ONE)
                    dve.tensor_tensor(lw(n), prod(s, n)[:, 0, :], lw(n), ALU.add).then_inc(cum_steps, 1)
            scale(2)
            scale(3)

        @block.gpsimd
        def _(pool):
            pool.wait_ge(kk_steps, 6 + ONE)
            pool.wait_ge(taken, 8 + ONE)
            for n, (d, p) in enumerate(UNITS):
                pool.tensor_tensor(prod(s, n)[:, 2, :], kk(p), a(n), ALU.mult).then_inc(b_ready, 1)
            pool.wait_ge(bonus_steps, 4 + ONE)
            pool.wait_ge(b_ready, 4 + ONE)
            for n in range(4):
                pool.wait_ge(exps, 4 * n + 3 + ONE)
                for j in (2, 3):
                    pool.tensor_tensor(prod(s, n)[:, j, :], prod(s, n)[:, j, :], a(n), ALU.mult).then_inc(scaled_g, 1)


def scan(nc, s):
    NU = len(UNITS)
    with ExitStack() as c:
        def sb(name, shape):
            return c.enter_context(nc.sbuf_tensor("sc_" + name, shape, F32))

        def sem(name):
            return counter(nc, c, "sc_" + name)
        bd_all = [sb("bd", [P, NU, 5, P])[:, :, :, :],
                  s.proj[:, 6:9, :].rearrange("p a t -> p (a t)")[:, 0:NU * 5 * P].rearrange("p (n f c) -> p n f c", n=NU, f=5)]
        lm = sb("lm", [P, NU, 512])
        xm = sb("xm", [P, NU, 3 * P])
        qq = sb("qq", [P, NU, 2, P])
        mm2 = sb("mm2", [P, NU, 2, 2, P])
        y1 = sb("y1", [P, NU, P])
        btv = sb("btv", [P, NU, 320])
        wu = sb("wu", [P, NU, 2, HD])
        st = sb("st", [P, NU, HD])
        ps = c.enter_context(nc.psum_tensor("sc_ps", [P, NU, 2, 512], F32))
        zeroed, packed, unpacked, seeded = (sem(n) for n in ("zeroed", "packed", "unpacked", "seeded"))
        prods, masked, sides = (sem(n) for n in ("products", "masked", "sides"))
        powed, pow_out, improved, inverse = (sem(n) for n in ("powed", "pow_out", "improved", "inverse"))
        crossed, cross_out = sem("crossed"), sem("cross_out")
        w_sum, w_out, u_sum, u_out, y_sum, y_out, s_out = (sem(n) for n in ("w_sum", "w_out", "u_sum", "u_out", "y_sum", "y_out", "s_out"))
        nc.all_engine_barrier()
        block = c.enter_context(nc.Block())
        yb = s.proj[:, 0:4, :].rearrange("p n (c v) -> p n c v", v=HD)

        def chunk_of(i, n):
            return i if UNITS[n][0] == 0 else i * -1 + (NCH - 1)

        def both_chunks(eng, chunk):
            with eng.Fori(0, NCH // 2) as i:
                for u in range(2):
                    chunk(i * 2 + u, bd_all[u])

        @block.gpsimd
        def _(pool):
            for bd in bd_all:
                pool.memset(bd, 0.0).then_inc(zeroed, 1)
            pool.wait_ge(zeroed, 2 + ONE)

            def chunk(i, bd):
                pool.wait_ge(seeded, i * NU * 2 + ONE)
                for n, (d, p) in enumerate(UNITS):
                    tok = chunk_of(i, n) * CHUNK
                    pool.wait_ge(y_sum, i * NU + ONE)
                    for h in range(2):
                        p0, p1 = h * HD, (h + 1) * HD
                        pool.tensor_copy(bd[p0:p1, n, 0:4, p0:p1], prod(s, n)[p0:p1, :, ds(tok, CHUNK)]).then_inc(packed, 1)
                        pool.tensor_copy(bd[p0:p1, n, 4, p0:p1], s.proj[p0:p1, S_V + p, ds(tok, CHUNK)]).then_inc(packed, 1)
                pool.wait_ge(packed, i * NU * 4 + NU * 4 + ONE)
                for n in range(NU):
                    pool.wait_ge(masked, (i * NU + n) * 2 + 2 + ONE)
                    pool.tensor_tensor(qq[:, n, 0, :], lm[:, n, 0:P], s.ident, ALU.add).then_inc(seeded, 1)
                    pool.tensor_tensor(qq[:, n, 1, :], xm[:, n, 0:P], s.ident, ALU.add).then_inc(seeded, 1)
            both_chunks(pool, chunk)

        @block.tensor
        def _(pe):
            pe.sem_inc(y_sum, NU)

            def chunk(i, bd):
                def at(n, per=1):
                    return (i * NU + n) * per
                for n in range(NU):
                    b = bd[:, n, :, :]
                    pe.wait_ge(packed, at(n, 4) + 4 + ONE)
                    pe.wait_ge(y_out, at(n) + 1 + ONE)
                    kr = b[:, 0:2, :].rearrange("p a b -> p (a b)")
                    pe.matmul(ps[:, n, 0, 0:256], b[:, 2, :], kr, start=True, stop=True)
                    pe.matmul(ps[:, n, 0, 256:512], b[:, 3, :], kr, start=True, stop=True)
                    pe.matmul(ps[:, n, 1, 0:P], b[:, 0, :], b[:, 2, :], start=True, stop=True)
                    pe.transpose(ps[:, n, 1, P:2 * P], b[:, 2, :], s.ident)
                    pe.transpose(ps[:, n, 1, 2 * P:3 * P], b[:, 3, :], s.ident)
                    pe.matmul(ps[:, n, 1, 3 * P:3 * P + HD], b[:, 4, :], s.fold, start=True, stop=True).then_inc(prods, 1)
                for n in range(NU):
                    pe.wait_ge(masked, at(n, 2) + 2 + ONE)
                    pe.matmul(ps[:, n, 0, 0:P], lm[:, n, 0:P], xm[:, n, 0:P], start=True, stop=True)
                    pe.matmul(ps[:, n, 0, P:2 * P], xm[:, n, 0:P], lm[:, n, 0:P], start=True, stop=True).then_inc(powed, 1)
                for step in range(3):
                    for n in range(NU):
                        m = mm2[:, n, step % 2, :, :]
                        pe.wait_ge(pow_out, (i * NU * 3) + NU * step + n + 1 + ONE)
                        if step == 0:
                            pe.wait_ge(seeded, at(n, 2) + 2 + ONE)
                            pe.wait_ge(sides, at(n) + 1 + ONE)
                        else:
                            pe.wait_ge(improved, (i * NU * 4) + NU * (step - 1) + n + 1 + ONE)
                        pe.matmul(ps[:, n, 1, 0:P], m[:, 0, :], qq[:, n, 0, :], start=True, stop=True)
                        mm = pe.matmul(ps[:, n, 1, P:2 * P], m[:, 1, :], qq[:, n, 1, :], start=True, stop=True)
                        if step < 2:
                            pe.matmul(ps[:, n, 0, 0:P], m[:, 1, :], m[:, 0, :], start=True, stop=True)
                            mm = pe.matmul(ps[:, n, 0, P:2 * P], m[:, 0, :], m[:, 1, :], start=True, stop=True)
                        mm.then_inc(powed, 1)
                for level in range(2):
                    for n in range(NU):
                        pe.wait_ge(improved, (i * NU * 4) + NU * (2 + level) + n + 1 + ONE)
                        pe.matmul(ps[:, n, 0, 0:P], xm[:, n, (level + 1) * P:(level + 2) * P], qq[:, n, 0, :],
                                  start=True, stop=True).then_inc(crossed, 1)
                    for n in range(NU):
                        pe.wait_ge(cross_out, (i * NU * 2) + NU * level + n + 1 + ONE)
                        mm = pe.matmul(ps[:, n, 1, 0:P], qq[:, n, 1, :], y1[:, n, :], start=True, stop=True)
                        if level == 0:
                            mm = pe.matmul(ps[:, n, 1, P:2 * P], y1[:, n, :], qq[:, n, 1, :], start=True, stop=True)
                        mm.then_inc(crossed, 1)
                for n in range(NU):
                    pe.wait_ge(s_out, at(n) + 1 + ONE)
                    pe.matmul(ps[:, n, 0, 0:HD], bd[:, n, 0, :], st[:, n, :], start=True, stop=False)
                    pe.matmul(ps[:, n, 0, 0:HD], lm[:, n, 256:384], btv[:, n, 256:320], start=False, stop=True).then_inc(w_sum, 1)
                for n in range(NU):
                    pe.wait_ge(w_out, at(n) + 1 + ONE)
                    pe.wait_ge(inverse, at(n) + 1 + ONE)
                    pe.matmul(ps[:, n, 0, HD:2 * HD], qq[:, n, 0, :], wu[:, n, 0, :], start=True, stop=True).then_inc(u_sum, 1)
                for n in range(NU):
                    pe.wait_ge(u_out, at(n) + 1 + ONE)
                    pe.matmul(ps[:, n, 0, 2 * HD:3 * HD], s.ident, st[:, n, :], start=True, stop=False)
                    pe.matmul(ps[:, n, 0, 2 * HD:3 * HD], btv[:, n, 0:P], wu[:, n, 1, :], start=False, stop=False)
                    pe.matmul(ps[:, n, 0, 2 * HD:3 * HD], btv[:, n, P:2 * P], btv[:, n, 256:320], start=False, stop=True)
                    pe.matmul(ps[:, n, 1, 0:HD], bd[:, n, 1, :], st[:, n, :], start=True, stop=False)
                    pe.matmul(ps[:, n, 1, 0:HD], lm[:, n, P:2 * P], wu[:, n, 1, :], start=False, stop=False)
                    pe.matmul(ps[:, n, 1, 0:HD], lm[:, n, 384:512], btv[:, n, 256:320], start=False, stop=True).then_inc(y_sum, 1)
            both_chunks(pe, chunk)

        @block.vector
        def _(dve):
            dve.memset(st[:, :, :], 0.0).then_inc(s_out, NU)
            dve.sem_inc(y_out, NU)
            with dve.Fori(0, NCH) as i:
                def at(n, per=1):
                    return (i * NU + n) * per
                for n, (d, p) in enumerate(UNITS):
                    dve.wait_ge(prods, at(n) + 1 + ONE)
                    dve.wait_ge(u_out, at(0) + ONE)
                    dve.tensor_tensor(xm[:, n, :].rearrange("p (a b) -> p a b", a=3),
                                      ps[:, n, 1:2, 0:P].to_broadcast([P, 3, P]),
                                      s.x_mask[d].rearrange("p (a b) -> p a b", a=3), ALU.mult).then_inc(masked, 1)
                    dve.tensor_tensor(lm[:, n, :], ps[:, n, 0, :], s.l_mask[d], ALU.mult).then_inc(masked, 1)
                for step in range(3):
                    for n in range(NU):
                        dve.wait_ge(powed, (i * NU * 4) + NU * (step + 1) + n + 1 + ONE)
                        dve.tensor_tensor(qq[:, n, :, :], ps[:, n, 1, 0:256].rearrange("p (a b) -> p a b", a=2), qq[:, n, :, :],
                                          ALU.add).then_inc(improved, 1)
                for level in range(2):
                    for n in range(NU):
                        dve.wait_ge(crossed, (i * NU * 4) + NU * (2 * level + 1) + n + 1 + ONE)
                        if level == 0:
                            dve.tensor_tensor(qq[:, n, :, :], ps[:, n, 1, 0:256].rearrange("p (a b) -> p a b", a=2), qq[:, n, :, :],
                                              ALU.add).then_inc(improved, 1)
                        else:
                            dve.tensor_tensor(qq[:, n, 0, :], ps[:, n, 1, 0:P], qq[:, n, 0, :], ALU.add).then_inc(inverse, 1)
                for n in range(NU):
                    ch = chunk_of(i, n)
                    dve.wait_ge(y_sum, at(n) + NU + 1 + ONE)
                    dve.tensor_tensor(st[:, n, :], ps[:, n, 0, 2 * HD:3 * HD],
                                      s.ec[:, n, ds(ch, 1)].to_broadcast([P, HD]), ALU.mult).then_inc(s_out, 1)
                    dve.tensor_copy(yb[:, n, ds(ch, 1), :], ps[:, n, 1:2, 0:HD]).then_inc(y_out, 1)

        @block.scalar
        def _(act):
            with act.Fori(0, NCH) as i:
                def at(n, per=1):
                    return (i * NU + n) * per
                for n in range(NU):
                    act.wait_ge(masked, at(n, 2) + 1 + ONE)
                    act.activation(btv[:, n, :], ps[:, n, 1, P:P + 320], ACT.Copy).then_inc(sides, 1)
                for step in range(3):
                    for n in range(NU):
                        act.wait_ge(powed, (i * NU * 4) + NU * step + n + 1 + ONE)
                        act.activation(mm2[:, n, step % 2, :, :].rearrange("p a b -> p (a b)"), ps[:, n, 0, 0:256],
                                       ACT.Copy).then_inc(pow_out, 1)
                for level in range(2):
                    for n in range(NU):
                        act.wait_ge(crossed, (i * NU * 4) + NU * 2 * level + n + 1 + ONE)
                        act.activation(y1[:, n, :], ps[:, n, 0, 0:P], ACT.Copy).then_inc(cross_out, 1)
                for n in range(NU):
                    act.wait_ge(w_sum, at(n) + 1 + ONE)
                    act.activation(wu[:, n, 0, :], ps[:, n, 0, 0:HD], ACT.Copy).then_inc(w_out, 1)
                for n in range(NU):
                    act.wait_ge(u_sum, at(n) + 1 + ONE)
                    act.activation(wu[:, n, 1, :], ps[:, n, 0, HD:2 * HD], ACT.Copy, scale=-1.0).then_inc(u_out, 1)


def rwkv_out(nc, s):
    with ExitStack() as c:
        def sem(name):
            return counter(nc, c, "ro_" + name)
        ybd = c.enter_context(nc.sbuf_tensor("ro_ybd", [P, RW_PAIRS, P], F32))
        yt = c.enter_context(nc.sbuf_tensor("ro_yt", [P, RW_PAIRS, SEQ], F32))
        ps = c.enter_context(nc.psum_tensor("ro_ps", [P, RW_PAIRS, 512], F32))
        pn = c.enter_context(nc.psum_tensor("ro_pn", [P, SEQ], F32))
        pb = c.enter_context(nc.psum_tensor("ro_pb", [P, SEQ], F32))
        zeroed, packed, turned, stored = (sem(n) for n in ("zeroed", "packed", "turned", "stored"))
        meaned, centred, squared, spread, rooted, bonus, steps = (sem(n) for n in ("mean", "centred", "sq", "var", "root", "bonus", "steps"))
        nc.all_engine_barrier()
        block = c.enter_context(nc.Block())
        yb = s.proj[:, 0:4, :].rearrange("p n (c v) -> p n c v", v=HD)
        root = s.proj[:, 9:11, :]
        sq = s.proj[:, 11:13, :]

        @block.gpsimd
        def _(pool):
            pool.memset(ybd[:, :, :], 0.0).then_inc(zeroed, 1)
            pool.wait_ge(zeroed, 1 + ONE)
            with pool.Fori(0, NCH) as i:
                for p in range(RW_PAIRS):
                    pool.wait_ge(turned, i * RW_PAIRS + ONE)
                    for h in range(2):
                        p0, p1 = h * HD, (h + 1) * HD
                        pool.tensor_tensor(ybd[p0:p1, p:p + 1, p0:p1], yb[p0:p1, p, ds(i, 1), :], yb[p0:p1, p + 2, ds(i, 1), :],
                                           ALU.add).then_inc(packed, 1)

        @block.tensor
        def _(pe):
            with pe.Fori(0, NCH) as i:
                for p in range(RW_PAIRS):
                    pe.wait_ge(packed, (i * RW_PAIRS + p) * 2 + 2 + ONE)
                    pe.wait_ge(stored, i * RW_PAIRS + ONE)
                    pe.matmul(ps[:, p, 0:HD], ybd[:, p, :], s.fold, start=True, stop=True).then_inc(turned, 1)
            for p in range(RW_PAIRS):
                pe.wait_ge(stored, NCH * RW_PAIRS + ONE)
                if p:
                    pe.wait_ge(rooted, p + ONE)
                    pe.wait_ge(steps, 4 * p + ONE)
                for half in range(2):
                    mm = pe.matmul(pn[:, half * 512:(half + 1) * 512], s.pair_ones, yt[:, p, half * 512:(half + 1) * 512], start=True, stop=True)
                mm.then_inc(meaned, 1)
                for half in range(2):
                    mm = pe.matmul(pb[:, half * 512:(half + 1) * 512], s.pair_ones,
                                   s.proj[:, S_BONUS + p, half * 512:(half + 1) * 512], start=True, stop=True)
                mm.then_inc(bonus, 1)
                pe.wait_ge(squared, p + 1 + ONE)
                for half in range(2):
                    mm = pe.matmul(pn[:, half * 512:(half + 1) * 512], s.pair_ones, sq[:, p, half * 512:(half + 1) * 512], start=True, stop=True)
                mm.then_inc(spread, 1)

        @block.scalar
        def _(act):
            with act.Fori(0, NCH) as i:
                for p in range(RW_PAIRS):
                    act.wait_ge(turned, i * RW_PAIRS + p + 1 + ONE)
                    act.activation(yt[:, p, ds(i * CHUNK, CHUNK)], ps[:, p, 0:HD], ACT.Copy).then_inc(stored, 1)
            for p in range(RW_PAIRS):
                act.wait_ge(centred, p + 1 + ONE)
                act.activation(sq[:, p, :], yt[:, p, :], ACT.Square).then_inc(squared, 1)
                act.wait_ge(spread, p + 1 + ONE)
                act.activation(root[:, p, :], pn[:, :], ACT.Sqrt, bias=s.gn_eps, scale=1.0 / HD).then_inc(rooted, 1)

        @block.vector
        def _(dve):
            for p in range(RW_PAIRS):
                dve.wait_ge(meaned, p + 1 + ONE)
                dve.wait_ge(stored, NCH * RW_PAIRS + ONE)
                dve.scalar_tensor_tensor(out=yt[:, p, :], in0=pn[:, :], scalar=-1.0 / HD, in1=yt[:, p, :], op0=ALU.mult, op1=ALU.add)\
                   .then_inc(centred, 1)
                dve.wait_ge(bonus, p + 1 + ONE)
                v = s.proj[:, S_V + p, :]
                dve.tensor_tensor(v, pb[:, :], v, ALU.mult).then_inc(steps, 1)
                dve.wait_ge(rooted, p + 1 + ONE)
                dve.reciprocal(root[:, p, :], root[:, p, :]).then_inc(steps, 1)
                dve.wait_ge(steps, 4 * p + 2 + ONE)
                dve.scalar_tensor_tensor(out=yt[:, p, :], in0=yt[:, p, :], scalar=s.par("ln_w", 2)[:, p:p + 1], in1=root[:, p, :],
                                         op0=ALU.mult, op1=ALU.mult).then_inc(steps, 1)
                dve.wait_ge(steps, 4 * p + 3 + ONE)
                dve.scalar_tensor_tensor(out=yt[:, p, :], in0=yt[:, p, :], scalar=s.par("ln_b", 2)[:, p:p + 1], in1=v,
                                         op0=ALU.add, op1=ALU.add).then_inc(steps, 1)
                dve.wait_ge(steps, 4 * p + 4 + ONE)
                dve.tensor_tensor(s.mixT[:, 4 + p, :], yt[:, p, :], s.extra[:, 4 + p, :], ALU.mult)


def out_projection(nc, s):
    with ExitStack() as c:
        w = c.enter_context(nc.sbuf_tensor("op_w", [P, KD, D], F32))
        ps = c.enter_context(nc.psum_tensor("op_ps", [P, 4, 512], F32))
        loaded, x_in, done, added = (counter(nc, c, "op_" + n) for n in ("loaded", "x_in", "done", "added"))
        nc.all_engine_barrier()
        block = c.enter_context(nc.Block())

        @block.sync
        def _(sp):
            sp.dma_start(w[:, :, :], s.inp["w_out"].rearrange("(k p) n -> p k n", p=P)).then_inc(loaded, 16)
            sp.dma_start(s.x1[:, :, :], s.inp["x"].rearrange("(t p) n -> p t n", p=P)).then_inc(x_in, 16)

        @block.tensor
        def _(pe):
            pe.wait_ge(loaded, 16 + ONE)
            with pe.Fori(0, 2) as half:
                for t in range(TT):
                    pe.wait_ge(added, half * TT + max(t - 3, 0) + ONE)
                    for k in range(KD):
                        mm = pe.matmul(ps[:, t % 4, :], s.mixT[:, k, t * P:(t + 1) * P], w[:, k, ds(half * 512, 512)],
                                       start=(k == 0), stop=(k == KD - 1))
                    mm.then_inc(done, 1)

        @block.vector
        def _(dve):
            dve.wait_ge(x_in, 16 + ONE)
            with dve.Fori(0, 2) as half:
                for t in range(TT):
                    dve.wait_ge(done, half * TT + t + 1 + ONE)
                    x = s.x1[:, t, ds(half * 512, 512)]
                    dve.tensor_tensor(x, ps[:, t % 4, :], x, ALU.add).then_inc(added, 1)


def ffn_norm_router(nc, s):
    with ExitStack() as c:
        def sb(name, shape):
            return c.enter_context(nc.sbuf_tensor("fr_" + name, shape, F32))

        def sem(name):
            return counter(nc, c, "fr_" + name)
        sq = sb("sq", [P, D])
        h = sb("h", [P, 2, D])
        hT = sb("hT", [P, 2, KD, P])
        wf = sb("wf", [P, D])
        wr = sb("wr", [P, KD, NG + NE])
        br = sb("br", [P, NG + NE])
        st = sb("st", [P, 2, 4])
        ps = c.enter_context(nc.psum_tensor("fr_ps", [P, 2, KD, P], F32))
        pl = c.enter_context(nc.psum_tensor("fr_pl", [P, 2, 512], F32))
        loaded, sums, roots, invs, normed, turned, copied, logits, biased = (
            sem(n) for n in ("loaded", "sums", "roots", "invs", "normed", "turned", "copied", "logits", "biased"))
        rows_out = [sem("rows_out0"), sem("rows_out1")]
        nc.all_engine_barrier()
        block = c.enter_context(nc.Block())
        h_rows = s.h_dram.rearrange("(t p) n -> t p n", p=P)

        @block.sync
        def _(sp):
            sp.dma_start(wf[:, :], s.inp["ffn_norm_w"].to_broadcast([P, D])).then_inc(loaded, 16)
            sp.dma_start(wr[:, :, 0:NG], s.inp["moe_w_group"].rearrange("(k p) n -> p k n", p=P)).then_inc(loaded, 16)
            sp.dma_start(wr[:, :, NG:], s.inp["moe_w_expert"].rearrange("(k p) n -> p k n", p=P)).then_inc(loaded, 16)
            sp.dma_start(br[:, 0:NG], s.inp["moe_b_group"].to_broadcast([P, NG])).then_inc(loaded, 16)
            sp.dma_start(br[:, NG:], s.inp["moe_b_expert"].to_broadcast([P, NE])).then_inc(loaded, 16)
            with sp.Fori(0, TT // 2) as i:
                for u in range(2):
                    sp.wait_ge(normed, i * 2 + u + 1 + ONE)
                    sp.dma_start(h_rows[ds(i * 2 + u, 1)].rearrange("o p n -> p (o n)"), h[:, u, :]).then_inc(rows_out[u], 16)
            sp.wait_ge(rows_out[0], 16 * TT // 2 + ONE)
            sp.wait_ge(rows_out[1], 16 * TT // 2 + ONE)

        @block.scalar
        def _(act):
            with act.Fori(0, TT // 2) as i:
                for u in range(2):
                    act.wait_ge(invs, i * 2 + ONE)
                    act.wait_ge(sums, i * 2 + u + ONE)
                    act.activation(sq[:, :].unsqueeze(1), s.x1[:, ds(i * 2 + u, 1), :], ACT.Square, accum_out=st[:, u, 0:1]).then_inc(sums, 1)
                for u in range(2):
                    act.wait_ge(sums, i * 2 + u + 1 + ONE)
                    act.activation(st[:, u, 1:2], st[:, u, 0:1], ACT.Sqrt, bias=s.eps, scale=1.0 / D).then_inc(roots, 1)
                for u in range(2):
                    act.wait_ge(turned, i * 2 + u + 1 + ONE)
                    act.wait_ge(logits, i * 2 + ONE)
                    act.activation(hT[:, u, :, :], ps[:, u, :, :], ACT.Copy).then_inc(copied, 1)

        @block.vector
        def _(dve):
            dve.wait_ge(loaded, 80 + ONE)
            with dve.Fori(0, TT // 2) as i:
                for u in range(2):
                    dve.wait_ge(roots, i * 2 + u + 1 + ONE)
                    dve.reciprocal(st[:, u, 2:3], st[:, u, 1:2]).then_inc(invs, 1)
                for u in range(2):
                    dve.wait_ge(invs, i * 2 + u + 1 + ONE)
                    dve.wait_ge(turned, i * 2 + ONE)
                    dve.wait_ge(rows_out[u], i * 16 + ONE)
                    dve.scalar_tensor_tensor(out=h[:, u:u + 1, :], in0=s.x1[:, ds(i * 2 + u, 1), :], scalar=st[:, u, 2:3],
                                             in1=wf[:, :].unsqueeze(1), op0=ALU.mult, op1=ALU.mult).then_inc(normed, 1)
                for u in range(2):
                    dve.wait_ge(logits, i * 2 + u + 1 + ONE)
                    dve.tensor_tensor(s.logits[:, ds(i * 2 + u, 1), :], pl[:, u:u + 1, 0:NG + NE], br[:, :].unsqueeze(1), ALU.add)\
                       .then_inc(biased, 1)

        @block.tensor
        def _(pe):
            pe.wait_ge(loaded, 80 + ONE)
            with pe.Fori(0, TT // 2) as i:
                for u in range(2):
                    pe.wait_ge(normed, i * 2 + u + 1 + ONE)
                    pe.wait_ge(copied, i * 2 + ONE)
                    for k in range(KD):
                        mm = pe.transpose(ps[:, u, k, :], h[:, u, k * P:(k + 1) * P], s.ident)
                    mm.then_inc(turned, 1)
                for u in range(2):
                    pe.wait_ge(copied, i * 2 + u + 1 + ONE)
                    pe.wait_ge(biased, i * 2 + ONE)
                    for k in range(KD):
                        mm = pe.matmul(pl[:, u, 0:NG + NE], hT[:, u, k, :], wr[:, k, :], start=(k == 0), stop=(k == KD - 1))
                    mm.then_inc(logits, 1)


def routing(nc, s):
    with ExitStack() as c:
        def sb(name, shape, dt=F32):
            return c.enter_context(nc.sbuf_tensor("rt_" + name, shape, dt))

        def sem(name):
            return counter(nc, c, "rt_" + name)
        gmax, gmin, den, m1, m2, e2v = (sb(n, [P, TT]) for n in ("gmax", "gmin", "den", "m1", "m2", "e2"))
        t4, t4b, goh, sel = (sb(n, [P, TT, 4]) for n in ("t4", "t4b", "goh", "sel"))
        t44 = sb("t44", [P, TT, 4, 4])
        eoh = sb("eoh", [P, 2, TT, 4])
        oh = sb("oh", [P, 2, TT, NE])
        both = sb("both", [P, TT, NE])
        off = sb("off", [P, TT + 1, NE])
        rank = sb("rank", [P, TT, NE])
        t16 = sb("t16", [P, 2, TT, NE])
        cnt8 = sb("cnt8", [P, NE, 8])
        nb, ends, starts = (sb(n, [P, NE]) for n in ("nb", "ends", "starts"))
        b32 = sb("b32", [P, 32, NE])
        be = sb("be", [P, 32])
        bei = s.blk
        slotf = sb("slotf", [P, 2, TT])
        zeros = sb("zeros", [P, 32], I32)
        toki = sb("toki", [P, TT], I32)
        ps = c.enter_context(nc.psum_tensor("rt_ps", [P, 2, 512], F32))
        step, expd, stacked, ranked, zeroed, cleared, tok_ready = (
            sem(n) for n in ("step", "exp", "stacked", "ranked", "zeroed", "cleared", "tok"))
        scattered = dma_counter(nc, c, "rt_scattered")
        nc.all_engine_barrier()
        block = c.enter_context(nc.Block())
        gl, el = s.logits[:, :, 0:NG], s.logits[:, :, NG:]
        iota4 = s.iota[:, 0:4]

        def b3(ap, shape):
            return ap.to_broadcast(shape)

        @block.vector
        def _(dve):
            n = 0

            def link(ins):
                nonlocal n
                n += 1
                ins.then_inc(step, 1)
                dve.wait_ge(step, n + ONE)

            def first_max(vals, peak, onehot):
                link(dve.tensor_reduce(peak, vals, AX.X, ALU.max))
                link(dve.tensor_tensor(t4[:, :, :], vals, b3(peak.unsqueeze(2), [P, TT, 4]), ALU.is_equal))
                link(dve.tensor_scalar(t4[:, :, :], t4[:, :, :], -4.0, 4.0, ALU.mult, ALU.add))
                link(dve.tensor_tensor(t4[:, :, :], t4[:, :, :], b3(iota4.unsqueeze(1), [P, TT, 4]), ALU.add))
                link(dve.tensor_reduce(gmin[:, :], t4[:, :, :], AX.X, ALU.min))
                link(dve.tensor_tensor(onehot, b3(gmin[:, :].unsqueeze(2), [P, TT, 4]), b3(iota4.unsqueeze(1), [P, TT, 4]), ALU.is_equal))

            dve.memset(zeros[:, :], 0).then_inc(zeroed, 1)
            dve.tensor_copy(toki[:, :], s.token).then_inc(tok_ready, 1)
            first_max(gl, gmax[:, :], goh[:, :, :])
            link(dve.tensor_tensor(t4b[:, :, :], gl, b3(gmax[:, :].unsqueeze(2), [P, TT, 4]), ALU.subtract))
            dve.wait_ge(expd, 1 + ONE)
            link(dve.tensor_reduce(den[:, :], t4b[:, :, :], AX.X, ALU.add))
            link(dve.tensor_tensor(t44[:, :, :, :], el.rearrange("p t (g e) -> p t e g", g=4),
                                   b3(goh[:, :, :].unsqueeze(2), [P, TT, 4, 4]), ALU.mult))
            link(dve.tensor_reduce(sel[:, :, :], t44[:, :, :, :], AX.X, ALU.add))
            first_max(sel[:, :, :], m1[:, :], eoh[:, 0, :, :])
            link(dve.scalar_tensor_tensor(out=sel[:, :, :], in0=eoh[:, 0, :, :], scalar=NEG, in1=sel[:, :, :], op0=ALU.mult, op1=ALU.add))
            first_max(sel[:, :, :], m2[:, :], eoh[:, 1, :, :])
            link(dve.tensor_tensor(e2v[:, :], m2[:, :], m1[:, :], ALU.subtract))
            dve.wait_ge(expd, 2 + ONE)
            link(dve.tensor_scalar(m1[:, :], e2v[:, :], 1.0, None, ALU.add))
            link(dve.tensor_tensor(m1[:, :], m1[:, :], den[:, :], ALU.mult))
            link(dve.reciprocal(s.wt[:, 0, :], m1[:, :]))
            link(dve.tensor_tensor(s.wt[:, 1, :], s.wt[:, 0, :], e2v[:, :], ALU.mult))
            for k in range(2):
                link(dve.tensor_tensor(oh[:, k, :, :].rearrange("p t (g e) -> p t g e", g=4),
                                       b3(goh[:, :, :].unsqueeze(3), [P, TT, 4, 4]),
                                       b3(eoh[:, k, :, :].unsqueeze(2), [P, TT, 4, 4]), ALU.mult))
            link(dve.tensor_tensor(both[:, :, :], oh[:, 0, :, :], oh[:, 1, :, :], ALU.add))
            dve.sem_inc(stacked, 1)
            link(dve.memset(off[:, 0, :], 0.0))
            dve.wait_ge(ranked, 1 + ONE)
            for t in range(TT):
                link(dve.tensor_tensor(off[:, t + 1, :], ps[:, 1, t * NE:(t + 1) * NE], off[:, t, :], ALU.add))
            link(dve.tensor_tensor(cnt8[:, :, :], b3(off[:, TT, :].unsqueeze(2), [P, NE, 8]), b3(s.blk128.unsqueeze(1), [P, NE, 8]), ALU.is_gt))
            link(dve.tensor_reduce(nb[:, :], cnt8[:, :, :], AX.X, ALU.add))
            link(dve.tensor_tensor_scan(ends[:, :], s.ones[:, 0:NE], nb[:, :], 0.0, ALU.mult, ALU.add))
            link(dve.tensor_tensor(starts[:, :], ends[:, :], nb[:, :], ALU.subtract))
            link(dve.tensor_tensor(b32[:, :, :], b3(ends[:, :].unsqueeze(1), [P, 32, NE]), b3(s.iota.unsqueeze(2), [P, 32, NE]), ALU.is_le))
            link(dve.tensor_reduce(be[:, :], b32[:, :, :], AX.X, ALU.add))
            link(dve.tensor_scalar(bei[:, :], be[:, :], float(NE - 1), None, ALU.min))
            link(dve.tensor_copy(bei[:, 31:32], ends[:, NE - 1:NE]))
            link(dve.tensor_tensor(rank[:, :, :], ps[:, 0, 0:TT * NE].rearrange("p (t e) -> p t e", e=NE), off[:, 0:TT, :], ALU.add))
            link(dve.scalar_tensor_tensor(out=rank[:, :, :], in0=b3(starts[:, :].unsqueeze(1), [P, TT, NE]), scalar=float(P),
                                          in1=rank[:, :, :], op0=ALU.mult, op1=ALU.add))
            link(dve.tensor_tensor(t16[:, :, :, :], oh[:, :, :, :], b3(rank[:, :, :].unsqueeze(1), [P, 2, TT, NE]), ALU.mult))
            link(dve.tensor_reduce(slotf[:, :, :], t16[:, :, :, :], AX.X, ALU.add))
            link(dve.tensor_copy(s.slot[:, :, :], slotf[:, :, :]))
            dve.sem_inc(stacked, 1)

        @block.scalar
        def _(act):
            act.wait_ge(step, 7 + ONE)
            act.activation(t4b[:, :, :], t4b[:, :, :], ACT.Exp).then_inc(expd, 1)
            act.wait_ge(step, 24 + ONE)
            act.activation(e2v[:, :], e2v[:, :], ACT.Exp).then_inc(expd, 1)

        @block.tensor
        def _(pe):
            pe.wait_ge(stacked, 1 + ONE)
            flat = both[:, :, :].rearrange("p t e -> p (t e)")
            pe.matmul(ps[:, 0, 0:TT * NE], s.before, flat, start=True, stop=True)
            pe.matmul(ps[:, 1, 0:TT * NE], s.ones, flat, start=True, stop=True).then_inc(ranked, 1)

        @block.sync
        def _(sp):
            sp.wait_ge(zeroed, 1 + ONE)
            sp.dma_start(s.tok_dram.rearrange("(p n) o -> p (n o)", p=P), zeros[:, :]).then_inc(cleared, 16)
            sp.wait_ge(cleared, 16 + ONE)

        @block.gpsimd
        def _(pool):
            pool.wait_ge(cleared, 16 + ONE)
            pool.wait_ge(tok_ready, 1 + ONE)
            pool.wait_ge(stacked, 2 + ONE)
            for k in range(2):
                for t in range(TT):
                    pool.indirect_dma_start(out=s.tok_dram, out_offset=bass.IndirectOffsetOnAxis(ap=s.slot[:, k, t:t + 1], axis=0),
                                            in_=toki[:, t:t + 1], in_offset=None).then_inc(scattered, 16)
            pool.wait_ge(scattered, 16 * 2 * TT)


def experts(nc, s):
    with ExitStack() as c:
        def sb(name, shape, dt=F32):
            return c.enter_context(nc.sbuf_tensor("ex_" + name, shape, dt))

        def sem(name):
            return counter(nc, c, "ex_" + name)
        wg = sb("wg", [P, 2, KD, FF])
        wu = sb("wu", [P, 2, KD, FF])
        wd = sb("wd", [P, 2, KF, D])
        idx = sb("idx", [P, 2], I32)
        x = sb("x", [P, 2, D])
        xT = sb("xT", [P, 2, KD, P])
        sg = sb("sg", [P, FF])
        hid = sb("hid", [P, FF])
        hT = sb("hT", [P, KF, P])
        y = sb("y", [P, D])
        spare = sb("spare", [P, 1])
        act_spare = sb("act_spare", [P, 1])
        pt = c.enter_context(nc.psum_tensor("ex_pt", [P, 2, 512], F32))
        ph = c.enter_context(nc.psum_tensor("ex_ph", [P, 512], F32))
        pg = c.enter_context(nc.psum_tensor("ex_pg", [P, 512], F32))
        pu = c.enter_context(nc.psum_tensor("ex_pu", [P, 512], F32))
        py = c.enter_context(nc.psum_tensor("ex_py", [P, 2, 512], F32))
        spared = sem("spared")
        wg_in, wu_in, wd_in = ([sem(n + str(u)) for u in range(2)] for n in ("wg_in", "wu_in", "wd_in"))
        idx_in, x_in = ([dma_counter(nc, c, f"ex_{n}{u}") for u in range(2)] for n in ("idx_in", "x_in"))
        x_turned, x_copied, gated, upped, silu, hidden, h_turned, h_copied, downed, y_half, y_out = (
            sem(n) for n in ("x_turned", "x_copied", "gated", "upped", "silu", "hidden", "h_turned", "h_copied", "downed", "y_half", "y_out"))
        nc.all_engine_barrier()
        block = c.enter_context(nc.Block())

        def used_blocks(eng):
            return eng.value_load(s.blk[0:1, 31:32], min_val=1, max_val=NBLK)

        def steps(eng, full, tail):
            n = used_blocks(eng)
            full(0, 0, 0)
            with eng.Fori(0, NBLK // 2) as i:
                for b, k, u in ((i * 2 + 1, i, 1), (i * 2 + 2, i + 1, 0)):
                    with eng.If(b < n):
                        full(b, k, u)
                    if tail is not None:
                        with eng.If(b == n):
                            tail(b, k, u)
            if tail is not None:
                with eng.If(n == NBLK):
                    tail(NBLK, NBLK // 2, 1)
            return n

        @block.sync
        def _(sp):
            def load(b, k, u):
                e = sp.value_load(s.blk[0:1, ds(b, 1)], min_val=0, max_val=NE - 1)
                static = isinstance(b, int)
                if not static:
                    sp.wait_ge(gated, b - 1 + ONE)
                sp.dma_start(wg[:, u, :, :], s.inp["moe_w_gate"].rearrange("e (k p) f -> e p k f", p=P)[ds(e, 1)]
                             .rearrange("o p k f -> p (o k) f")).then_inc(wg_in[u], 16)
                if not static:
                    sp.wait_ge(upped, b - 1 + ONE)
                sp.dma_start(wu[:, u, :, :], s.inp["moe_w_up"].rearrange("e (k p) f -> e p k f", p=P)[ds(e, 1)]
                             .rearrange("o p k f -> p (o k) f")).then_inc(wu_in[u], 16)
                if not static:
                    sp.wait_ge(downed, b - 1 + ONE)
                sp.dma_start(wd[:, u, :, :], s.inp["moe_w_down"].rearrange("e (k p) f -> e p k f", p=P)[ds(e, 1)]
                             .rearrange("o p k f -> p (o k) f")).then_inc(wd_in[u], 16)
            steps(sp, load, None)

        @block.gpsimd
        def _(pool):
            tok = s.tok_dram.rearrange("(b p) o -> b p o", p=P)

            def gather(b, k, u):
                if not isinstance(b, int):
                    pool.wait_ge(x_turned, b - 1 + ONE)
                pool.dma_start(idx[:, u:u + 1], tok[ds(b, 1)].rearrange("a p o -> p (a o)")).then_inc(idx_in[u], 16)
                pool.wait_ge(idx_in[u], k * 16 + 16)
                pool.wait_ge(spared, b + ONE)
                pool.tensor_tensor(spare[:, 0:1], s.eps, s.eps, ALU.add).then_inc(spared, 1)
                pool.indirect_dma_start(out=x[:, u, :], out_offset=None, in_=s.h_dram,
                                        in_offset=bass.IndirectOffsetOnAxis(ap=idx[:, u:u + 1], axis=0)).then_inc(x_in[u], 16)
            steps(pool, gather, gather)

        @block.tensor
        def _(pe):
            def turn_x(b, k, u):
                pe.wait_ge(x_in[u], k * 16 + 16)
                pe.wait_ge(x_copied, b + ONE)
                for j in range(KD):
                    mm = pe.transpose(pt[:, j // 4, (j % 4) * P:(j % 4 + 1) * P], x[:, u, j * P:(j + 1) * P], s.ident)
                mm.then_inc(x_turned, 1)

            def turn_h(b):
                pe.wait_ge(hidden, b + 1 + ONE)
                pe.wait_ge(h_copied, b + ONE)
                for j in range(KF):
                    mm = pe.transpose(ph[:, j * P:(j + 1) * P], hid[:, j * P:(j + 1) * P], s.ident)
                mm.then_inc(h_turned, 1)

            def down(b, k, u):
                pe.wait_ge(h_copied, b + 1 + ONE)
                pe.wait_ge(wd_in[u], k * 16 + 16 + ONE)
                pe.wait_ge(y_half, b * 2 + ONE)
                for half in range(2):
                    for j in range(KF):
                        mm = pe.matmul(py[:, half, :], hT[:, j, :], wd[:, u, j, half * 512:(half + 1) * 512],
                                       start=(j == 0), stop=(j == KF - 1))
                mm.then_inc(downed, 1)

            def full(b, k, u):
                first = isinstance(b, int)
                if first:
                    turn_x(0, 0, 0)
                pe.wait_ge(x_copied, b + 1 + ONE)
                pe.wait_ge(wg_in[u], k * 16 + 16 + ONE)
                pe.wait_ge(silu, b + ONE)
                for j in range(KD):
                    mm = pe.matmul(pg[:, :], xT[:, u, j, :], wg[:, u, j, :], start=(j == 0), stop=(j == KD - 1))
                mm.then_inc(gated, 1)
                if not first:
                    turn_h(b - 1)
                pe.wait_ge(wu_in[u], k * 16 + 16 + ONE)
                pe.wait_ge(hidden, b + ONE)
                for j in range(KD):
                    mm = pe.matmul(pu[:, :], xT[:, u, j, :], wu[:, u, j, :], start=(j == 0), stop=(j == KD - 1))
                mm.then_inc(upped, 1)
                turn_x(b + 1, k + u, 1 - u)
                if not first:
                    down(b - 1, k - (1 - u), 1 - u)

            def tail(b, k, u):
                turn_h(b - 1)
                down(b - 1, k - (1 - u), 1 - u)
            steps(pe, full, tail)

        @block.scalar
        def _(act):
            y_rows = s.y_dram.rearrange("(b p) n -> b p n", p=P)

            def tail(b, k, u):
                act.wait_ge(h_turned, b + ONE)
                act.wait_ge(downed, b - 1 + ONE)
                act.activation(hT[:, :, :].rearrange("p a b -> p (a b)"), ph[:, :], ACT.Copy).then_inc(h_copied, 1)
                act.wait_ge(downed, b + ONE)
                act.wait_ge(y_out, (b - 1) * 16 + ONE)
                act.activation(y[:, 0:512], py[:, 0, :], ACT.Copy).then_inc(y_half, 1)
                act.wait_ge(y_half, b * 2 + ONE)
                act.dma_start(y_rows[ds(b - 1, 1)].rearrange("o p n -> p (o n)"), y[:, :]).then_inc(y_out, 16)

            def full(b, k, u):
                act.wait_ge(gated, b + 1 + ONE)
                act.wait_ge(hidden, b + ONE)
                act.activation(sg[:, :], pg[:, :], ACT.Silu).then_inc(silu, 1)
                if not isinstance(b, int):
                    tail(b, k, u)
            n = steps(act, full, tail)
            act.wait_ge(y_out, n * 16 + ONE)
            act.activation(act_spare[:, :], s.eps, ACT.Copy)

        @block.vector
        def _(dve):
            def copy_x(b, u):
                dve.wait_ge(x_turned, b + 1 + ONE)
                if not isinstance(b, int):
                    dve.wait_ge(upped, b - 1 + ONE)
                dve.tensor_copy(xT[:, u, :, :].rearrange("p a b -> p (a b)"), pt[:, :, :].rearrange("p a b -> p (a b)")).then_inc(x_copied, 1)

            def tail(b, k, u):
                dve.wait_ge(downed, b + ONE)
                dve.wait_ge(y_out, (b - 1) * 16 + ONE)
                dve.tensor_copy(y[:, 512:1024], py[:, 1, :]).then_inc(y_half, 1)

            def full(b, k, u):
                first = isinstance(b, int)
                if first:
                    copy_x(0, 0)
                dve.wait_ge(silu, b + 1 + ONE)
                dve.wait_ge(upped, b + 1 + ONE)
                dve.wait_ge(h_turned, b + ONE)
                dve.tensor_tensor(hid[:, :], pu[:, :], sg[:, :], ALU.mult).then_inc(hidden, 1)
                copy_x(b + 1, 1 - u)
                if not first:
                    tail(b, k, u)
            steps(dve, full, tail)


def combine(nc, s, out):
    with ExitStack() as c:
        rows = c.enter_context(nc.sbuf_tensor("cb_rows", [P, 4, 2, D], F32))
        come = [[dma_counter(nc, c, f"cb_in{t}_{k}") for k in range(2)] for t in range(4)]
        added, out_done = (counter(nc, c, "cb_" + n) for n in ("added", "out_done"))
        nc.all_engine_barrier()
        block = c.enter_context(nc.Block())
        out_rows = out.rearrange("o (t p) n -> t p (o n)", p=P)

        @block.gpsimd
        def _(pool):
            for t in range(TT):
                if t >= 4:
                    pool.wait_ge(added, 2 * (t - 4) + 2 + ONE)
                for k in range(2):
                    pool.indirect_dma_start(out=rows[:, t % 4, k, :], out_offset=None, in_=s.y_dram,
                                            in_offset=bass.IndirectOffsetOnAxis(ap=s.slot[:, k, t:t + 1], axis=0)).then_inc(come[t % 4][k], 16)

        @block.vector
        def _(dve):
            for t in range(TT):
                for k in range(2):
                    dve.wait_ge(come[t % 4][k], 16 * (t // 4 + 1))
                    if k:
                        dve.wait_ge(added, 2 * t + 1 + ONE)
                    dve.scalar_tensor_tensor(out=s.x1[:, t, :], in0=rows[:, t % 4, k, :], scalar=s.wt[:, k, t:t + 1], in1=s.x1[:, t, :],
                                             op0=ALU.mult, op1=ALU.add).then_inc(added, 1)

        @block.sync
        def _(sp):
            for t in range(TT):
                sp.wait_ge(added, 2 * t + 2 + ONE)
                sp.dma_start(out_rows[t], s.x1[:, t, :]).then_inc(out_done, 16)
            sp.wait_ge(out_done, 16 * TT + ONE)




def hybrid_layer(nc, inp, consts, params, out):
    def dram(name, shape, dt=F32):
        return nc.dram_tensor(name, shape, dt, kind="Internal").ap()
    s = Shared()
    s.inp = inp
    s.bias_dram = dram("bias_table", (8, GRID_W, 15, GRID_W))
    s.h_dram = dram("ffn_rows", (SEQ, D))
    s.y_dram = dram("expert_rows", (NBLK * P, D))
    s.tok_dram = dram("slot_tokens", (32 * P, 1), I32)
    top = ExitStack()
    cst = top.enter_context(nc.sbuf_tensor("cst", [P, NCC], F32))
    par = top.enter_context(nc.sbuf_tensor("par", [P, NPC], F32))
    s.par = lambda name, n: par[:, PCOL[name]:PCOL[name] + n]

    def const(name):
        return cst[:, CCOL[name]:CCOL[name] + CCOLS[name]]
    s.ident, s.pair_ones, s.ones, s.before, s.fold = (const(n) for n in ("ident", "pair_ones", "ones", "before", "fold"))
    s.eps, s.gn_eps, s.iota, s.blk128, s.token = (const(n) for n in ("eps", "gn_eps", "iota", "blk128", "token"))
    s.l_mask = [const("l_mask_f"), const("l_mask_b")]
    s.x_mask = [const("x_mask_f"), const("x_mask_b")]
    with top:
        params_in = top.enter_context(nc.semaphore("params_in"))
        with nc.Block() as block:
            @block.sync
            def _(sp):
                sp.dma_start(cst[:, :], consts).then_inc(params_in, 16)
                sp.dma_start(par[:, :], params).then_inc(params_in, 16)
                sp.wait_ge(params_in, 32)
        s.mixT = top.enter_context(nc.sbuf_tensor("mixT", [P, KD, SEQ], F32))
        with ExitStack() as c_proj:
            s.proj = c_proj.enter_context(nc.sbuf_tensor("proj", [P, C_ALL, SEQ], F32))
            with ExitStack() as c_mem:
                s.mkT = c_mem.enter_context(nc.sbuf_tensor("mkT", [P, 2, NMEM], F32))
                s.mv = c_mem.enter_context(nc.sbuf_tensor("mv", [P, 2, 256], F32))
                with ExitStack() as c:
                    s.memT = c.enter_context(nc.sbuf_tensor("memT", [P, KD, NMEM], F32))
                    norm_transpose(nc, s, inp["mem"].rearrange("(t p) n -> t p n", p=P), 2, s.memT, "mem_w", "m")
                    memory_kv(nc, s)
                with ExitStack() as c:
                    s.hT = c.enter_context(nc.sbuf_tensor("hT", [P, KD, SEQ], F32))
                    norm_transpose(nc, s, inp["x"].rearrange("(t p) n -> t p n", p=P), TT, s.hT, "attn_w", "x")
                    bias_table(nc, s)
                    projection(nc, s)
                attention(nc, s, memory=True)
                attention(nc, s, memory=False)
            s.extra = c_proj.enter_context(nc.sbuf_tensor("extra", [P, 6, SEQ], F32))
            s.ec = c_proj.enter_context(nc.sbuf_tensor("ec", [P, 4, NCH], F32))
            shift(nc, s)
            gates(nc, s)
            scan(nc, s)
            rwkv_out(nc, s)
        s.x1 = top.enter_context(nc.sbuf_tensor("x1", [P, TT, D], F32))
        out_projection(nc, s)
        with nc.Block() as block:
            @block.gpsimd
            def _(pool):
                pool.sem_clear(range(params_in.num + 1, 256))
        s.logits = top.enter_context(nc.sbuf_tensor("logits", [P, TT, NG + NE], F32))
        s.wt = top.enter_context(nc.sbuf_tensor("wt", [P, 2, TT], F32))
        s.slot = top.enter_context(nc.sbuf_tensor("slot", [P, 2, TT], I32))
        s.blk = top.enter_context(nc.sbuf_tensor("blk", [P, 32], I32))
        ffn_norm_router(nc, s)
        routing(nc, s)
        experts(nc, s)
        combine(nc, s, out)


def constants(np):
    i, j = np.arange(P)[:, None], np.arange(P)[None, :]
    c = np.zeros((P, NCC), np.float32)

    def put(name, v):
        c[:, CCOL[name]:CCOL[name] + CCOLS[name]] = v
    put("ident", i == j)
    put("pair_ones", i // HD == j // HD)
    put("ones", 1)
    put("before", i < j)
    put("fold", i % HD == np.arange(HD)[None, :])
    put("eps", RMS_EPS)
    put("gn_eps", GN_EPS)
    same = i // HD == j // HD
    for name, before in (("f", lambda a, b: a < b), ("b", lambda a, b: a > b)):
        strict, incl = same & before(i, j), same & (before(i, j) | (i == j))
        put("l_mask_" + name, np.concatenate([-1.0 * (strict & (i // 16 == j // 16)), incl, strict, incl], 1))
        strict = same & before(j, i)
        b16, b32 = i // 16 == j // 16, i // 32 == j // 32
        put("x_mask_" + name, -1.0 * np.concatenate([strict & b16, strict & ~b16 & b32, strict & ~b32], 1))
    put("iota", np.arange(32)[None, :])
    put("blk128", P * np.arange(8)[None, :])
    put("token", i + P * np.arange(8)[None, :])
    return c


_INS = ['x', 'mem', 'w_in', 'na_rpb', 'rw_w2', 'rw_a2', 'rw_g2', 'w_mem_kv', 'w_out', 'ffn_norm_w', 'moe_w_group',
        'moe_b_group', 'moe_w_expert', 'moe_b_expert', 'moe_w_gate', 'moe_w_up', 'moe_w_down']


def kernel(**inputs):
    import numpy as _np
    import concourse.bacc as _bacc
    from concourse import mybir as _mybir
    from concourse.bass_utils import run_bass_kernel_spmd as _run

    nc = _bacc.Bacc("TRN2", target_bir_lowering=False, num_devices=1)

    def cols(name, reps=1):
        a = _np.asarray(inputs[name]).reshape(-1)
        return _np.concatenate([a] * reps).reshape(-1, P).T
    params = _np.concatenate([
        cols('attn_norm_w'), cols('mem_norm_w'), cols('na_q_norm_w', 2), cols('na_k_norm_w', 2), cols('mem_q_norm_w', 2),
        cols('mem_k_norm_w', 2), cols('rw_mu_prev'), cols('rw_mu_next'), cols('rw_w0'), cols('rw_a0'), cols('rw_k_k'),
        cols('rw_k_a'), cols('rw_r_k'), cols('rw_ln_w'), cols('rw_ln_b')], axis=1)
    neg_fill = _np.full((GRID_W, 15, GRID_W), NEG, _np.float32)
    arrays, aps = {}, {}

    def give(name, a):
        a = _np.ascontiguousarray(a)
        arrays[f"in_{name}"] = a
        return nc.dram_tensor(f"in_{name}", a.shape, _mybir.dt.from_np(a.dtype), kind="ExternalInput").ap()
    for name in _INS:
        a = _np.asarray(inputs[name])
        aps[name] = give(name, a if a.ndim == 2 else a[0])
    aps['neg_fill'] = give("neg_fill", neg_fill)
    consts, par = give("consts", constants(_np)), give("params", params)
    out = nc.dram_tensor("out", (1, SEQ, D), _mybir.dt.float32, kind="ExternalOutput").ap()
    hybrid_layer(nc, aps, consts, par, out)
    r = _run(nc, [arrays], core_ids=[0])
    return r.results[0]["out"]
```

```python
from contextlib import ExitStack
import math

import concourse.bass as bass
from concourse import mybir

F32 = mybir.dt.float32
I32 = mybir.dt.int32
ALU = mybir.AluOpType
ACT = mybir.ActivationFunctionType
AX = mybir.AxisListType
ds = bass.ds

P = 128
D = 1024
KD = D // P
SEQ = 1024
TT = SEQ // P
NMEM = 256
HD = 64
GRID_W = 64
ROWS = SEQ // GRID_W
KH, KW = 8, 16
NA_PAIRS = 4
RW_PAIRS = 2
MEM_PAIRS = 2
C_Q, C_K, C_V, C_RW, C_MQ, C_ALL = 0, 4, 8, 12, 21, 23
RWC = C_MQ - C_RW
CHUNK = 64
NCH = SEQ // CHUNK
NEG = -1.0e30
NG, NE, FF = 4, 16, 512
KF = FF // P
NBLK = 31
SURE = 2 * SEQ // P
RMS_EPS = 1e-6
GN_EPS = 64e-5
DECAY = math.exp(-0.5)

PCOLS = dict(attn_w=8, mem_w=8, naq_w=1, nak_w=1, mq_w=1, mk_w=1, mu_p=9, mu_n=9, w0=4, a0=4,
             k_k=2, k_a=2, r_k=2, ln_w=2, ln_b=2)
PCOL = {}
_n = 0
for _k, _w in PCOLS.items():
    PCOL[_k] = _n
    _n += _w
NPC = _n

CCOLS = dict(ident=128, pair_ones=128, ones=128, before=128, fold=64, eps=1, gn_eps=1,
             l_mask_f=512, l_mask_b=512, x_mask_f=384, x_mask_b=384, iota=32, blk128=8, token=8)
CCOL = {}
_n = 0
for _k, _w in CCOLS.items():
    CCOL[_k] = _n
    _n += _w
NCC = _n


class Shared:
    pass


ONE = 1


def counter(nc, stack, name):
    sem = stack.enter_context(nc.semaphore(name))
    nc.gpsimd.sem_inc(sem, ONE)
    return sem


def dma_counter(nc, stack, name):
    return stack.enter_context(nc.semaphore(name))


def window_start(r):
    return min(max(r - KH // 2, 0), ROWS - KH)


S_PROD = 0
S_R, S_K, S_V, S_LW, S_LA, S_LG = (C_RW + n for n in (0, 2, 4, 6, 7, 8))
S_BONUS = (C_MQ, C_MQ + 1)
UNITS = [(d, p) for d in range(2) for p in range(RW_PAIRS)]


def key_direction(s, p):
    return s.mixT[:, 4 + p, :]


def norm_transpose(nc, s, src, tiles, dst, w_col, room, tag):
    with ExitStack() as c:
        xn = c.enter_context(nc.sbuf_tensor("nt_xn" + tag, [P, 2, D], F32))
        sq = c.enter_context(nc.sbuf_tensor("nt_sq" + tag, [P, D], F32))
        st = c.enter_context(nc.sbuf_tensor("nt_st" + tag, [P, 2, 4], F32))
        spare = c.enter_context(nc.sbuf_tensor("nt_spare" + tag, [P, 1], F32))
        ps = c.enter_context(nc.psum_tensor("nt_ps" + tag, [P, 2, KD, P], F32))
        loaded = [counter(nc, c, f"nt_loaded{u}{tag}") for u in range(2)]
        std_ready = counter(nc, c, "nt_std" + tag)
        sum_ready = counter(nc, c, "nt_sum" + tag)
        inv_ready = counter(nc, c, "nt_inv" + tag)
        normed = counter(nc, c, "nt_normed" + tag)
        turned = counter(nc, c, "nt_turned" + tag)
        stored = counter(nc, c, "nt_stored" + tag)
        nc.all_engine_barrier()
        block = c.enter_context(nc.Block())

        def rows(t):
            return s.mixT[:, ds(t + room, 1), :]

        def each_tile(eng, body):
            with eng.Fori(0, tiles // 2) as i:
                for u in range(2):
                    body(i * 2 + u, i, u)

        @block.sync
        def _(sp):
            def body(t, i, u):
                sp.wait_ge(loaded[u], i * 16 + ONE)
                sp.dma_start(rows(t), src[ds(t, 1)].rearrange("a p d -> p a d")).then_inc(loaded[u], 16)
            each_tile(sp, body)

        @block.scalar
        def _(act):
            def body(t, i, u):
                act.wait_ge(loaded[u], i * 16 + 16 + ONE)
                act.wait_ge(inv_ready, i * 2 + ONE)
                act.wait_ge(sum_ready, t + ONE)
                act.activation(spare[:, :], s.eps, ACT.Copy)
                act.activation(sq[:, :].unsqueeze(1), rows(t), ACT.Square, accum_out=st[:, u, 0:1]).then_inc(sum_ready, 1)
                act.wait_ge(sum_ready, t + 1 + ONE)
                act.activation(st[:, u, 1:2], st[:, u, 0:1], ACT.Sqrt, bias=s.eps, scale=1.0 / D).then_inc(std_ready, 1)
            each_tile(act, body)

        @block.vector
        def _(dve):
            def norm(t, i, u):
                dve.wait_ge(std_ready, t + 1 + ONE)
                dve.reciprocal(st[:, u, 2:3], st[:, u, 1:2]).then_inc(inv_ready, 1)
                dve.wait_ge(inv_ready, t + 1 + ONE)
                dve.wait_ge(turned, i * 2 + ONE)
                dve.tensor_scalar(xn[:, u:u + 1, :], rows(t), st[:, u, 2:3], None, ALU.mult).then_inc(normed, 1)

            def store(t, u):
                dve.wait_ge(turned, t + 1 + ONE)
                dve.tensor_tensor(dst[:, :, ds(t * P, P)], ps[:, u, :, :],
                                  s.par(w_col, KD).unsqueeze(2).to_broadcast([P, KD, P]), ALU.mult).then_inc(stored, 1)
            norm(0, 0, 0)
            if tiles > 2:
                with dve.Fori(0, tiles // 2 - 1) as i:
                    norm(i * 2 + 1, i, 1)
                    store(i * 2, 0)
                    norm(i * 2 + 2, i + 1, 0)
                    store(i * 2 + 1, 1)
            norm(tiles - 1, tiles // 2 - 1, 1)
            store(tiles - 2, 0)
            store(tiles - 1, 1)

        @block.tensor
        def _(pe):
            def body(t, i, u):
                pe.wait_ge(normed, t + 1 + ONE)
                pe.wait_ge(stored, i * 2 + ONE)
                for k in range(KD):
                    mm = pe.transpose(ps[:, u, k, :], xn[:, u, k * P:(k + 1) * P], s.ident)
                mm.then_inc(turned, 1)
            each_tile(pe, body)


def memory_kv(nc, s):
    with ExitStack() as c:
        w = s.kv_w
        ps = c.enter_context(nc.psum_tensor("kv_ps", [P, 4, 512], F32))
        done = counter(nc, c, "kv_done")
        nc.all_engine_barrier()
        block = c.enter_context(nc.Block())

        @block.tensor
        def _(pe):
            pe.wait_ge(s.kv_loaded, 16)
            for j in range(2):
                for k in range(KD):
                    mm = pe.matmul(ps[:, j, 0:NMEM], w[:, k, j * P:(j + 1) * P], s.memT[:, k, :],
                                   start=(k == 0), stop=(k == KD - 1))
                mm.then_inc(done, 1)
            for m in range(2):
                for k in range(KD):
                    mm = pe.matmul(ps[:, 2 + m, 0:256], s.memT[:, k, m * P:(m + 1) * P], w[:, k, 256:512],
                                   start=(k == 0), stop=(k == KD - 1))
                mm.then_inc(done, 1)

        @block.vector
        def _(dve):
            for j in range(2):
                dve.wait_ge(done, j + 1 + ONE)
                dve.tensor_copy(s.mkT[:, j, :], ps[:, j, 0:NMEM])

        @block.scalar
        def _(act):
            for m in range(2):
                act.wait_ge(done, m + 3 + ONE)
                act.activation(s.mv[:, m, :], ps[:, 2 + m, 0:256], ACT.Copy)


def bias_table(pool, s, filled, placed):
    rpb = s.inp["na_rpb"]
    row = 15 * GRID_W
    H = 2 * NA_PAIRS
    t = s.bias_dram

    def spot(h, start, dims):
        return bass.AP(t.tensor, h * GRID_W * row + start, dims)
    for h in range(H):
        pool.dma_start(t[h], s.inp["neg_fill"]).then_inc(filled, 16)
    pool.wait_ge(filled, 16 * H)
    n = 0
    for h in range(H):
        src = bass.AP(rpb.tensor, h * 15 * 31 + KW - 1 - KW // 2, [[0, 49], [31, 15], [1, KW]])
        pool.dma_start(spot(h, 8 * row, [[row + 1, 49], [GRID_W, 15], [1, KW]]), src).then_inc(placed, 16)
        n += 1
    for qc in [*range(8), *range(57, 64)]:
        cs = min(max(qc - KW // 2, 0), GRID_W - KW)
        src = bass.AP(rpb.tensor, cs - qc + KW - 1, [[15 * 31, H], [31, 15], [1, KW]])
        pool.dma_start(spot(0, qc * row + cs, [[GRID_W * row, H], [GRID_W, 15], [1, KW]]), src).then_inc(placed, 16)
        n += 1
    pool.wait_ge(placed, 16 * n)


def projection(nc, s):
    NORMED = 2 + 2 * NA_PAIRS
    with ExitStack() as c:
        w = c.enter_context(nc.sbuf_tensor("pj_w", [P, 2, KD, P], F32))
        ps = c.enter_context(nc.psum_tensor("pj_ps", [P, 2, 2, 512], F32))
        ps_n = c.enter_context(nc.psum_tensor("pj_ps_n", [P, SEQ], F32))
        ps_k = c.enter_context(nc.psum_tensor("pj_ps_k", [P, SEQ], F32))
        qw = c.enter_context(nc.sbuf_tensor("pj_qw", [P, 2], F32))
        spare = c.enter_context(nc.sbuf_tensor("pj_spare", [P, 1], F32))
        keep = c.enter_context(nc.sbuf_tensor("pj_keep", [P, RWC], F32))
        loaded = [counter(nc, c, f"pj_loaded{u}") for u in range(2)]
        zeroed, filled = counter(nc, c, "pj_zeroed"), dma_counter(nc, c, "pj_filled")
        bias_filled, bias_placed = dma_counter(nc, c, "pj_bias_filled"), dma_counter(nc, c, "pj_bias_placed")
        done = counter(nc, c, "pj_done")
        out0 = counter(nc, c, "pj_out_act")
        out1 = counter(nc, c, "pj_out_dve")
        kk_scaled, kk_squared, kk_summed, kk_rooted, kk_steps = (
            counter(nc, c, "pj_kk_" + n) for n in ("scaled", "squared", "summed", "rooted", "steps"))
        squared, sum_ready, std_ready, inv_ready, normed, qscaled, kept, shift_half = (
            counter(nc, c, "pj_" + n) for n in ("squared", "sum", "std", "inv", "normed", "qscaled", "kept", "shift_half"))
        nc.all_engine_barrier()
        block = c.enter_context(nc.Block())
        w_in = s.inp["w_in"].rearrange("(k p) n -> p k n", p=P)
        sq, std, zero = (s.mixT[:, n, :] for n in range(3))
        kk_sq = [s.mixT[:, n, :] for n in (6, 7)]

        def both(u):
            return ps[:, u, :, :].rearrange("p a b -> p (a b)")

        def steps(eng, step, shifted=None, directions=None):
            def chunk(t):
                return s.proj[:, ds(t - 2, 1), :]
            memory_k = s.mkT[:, :, :].rearrange("p a n -> p (a n)").unsqueeze(1)
            step(0, 0, 0, C_MQ, memory_k, s.par("mk_w", 1))
            step(1, 0, 1, C_MQ + 1, s.proj[:, C_MQ:C_MQ + 1, :], qw[:, 1:2])
            step(2, 1, 0, 0, s.proj[:, C_MQ + 1:C_MQ + 2, :], qw[:, 1:2])
            for first, weight in ((3, qw[:, 0:1]), (3 + NA_PAIRS, s.par("nak_w", 1))):
                with eng.Fori(0, NA_PAIRS // 2) as i:
                    t = i * 2 + first
                    step(t, i + first // 2, 1, t - 2, chunk(t - 1), weight)
                    step(t + 1, i + (first // 2 + 1), 0, t - 1, chunk(t), weight)
            first = 1 + NORMED
            last_key = 2 + C_RW + 3
            if shifted is not None:
                for t in range(first, 2 + C_RW):
                    step(t, t // 2, t % 2, t - 2, None, None)
                for t in range(2 + C_RW, C_ALL):
                    shifted(t, t % 2, t - 2, t - 2 - C_RW)
                    directions(t - last_key)
                return
            for first, end in ((first, last_key + 2), (last_key + 2, C_ALL)):
                with eng.Fori(0, (end - first) // 2) as i:
                    t = i * 2 + first
                    step(t, i + first // 2, 1, t - 2, None, None)
                    step(t + 1, i + (first // 2 + 1), 0, t - 1, None, None)
                if directions is not None and end < C_ALL:
                    directions()

        @block.gpsimd
        def _(pool):
            pool.memset(zero, 0.0).then_inc(zeroed, 1)
            pool.wait_ge(zeroed, 1 + ONE)
            for b in range(SURE, NBLK):
                pool.dma_start(s.y_dram[b * P:(b + 1) * P, :], zero).then_inc(filled, 16)
            bias_table(pool, s, bias_filled, bias_placed)
            pool.wait_ge(filled, 16 * (NBLK - SURE))

        @block.sync
        def _(sp):
            def step(t, k, u, col, item, weight):
                if not isinstance(t, int) or t >= 2:
                    sp.wait_ge(done, t * 2 - 2 + ONE)
                sp.dma_start(w[:, u, :, :], w_in[:, :, ds(col * P, P)]).then_inc(loaded[u], 16)
            steps(sp, step)

        @block.tensor
        def _(pe):
            def step(t, k, u, col, item, weight):
                pe.wait_ge(loaded[u], k * 16 + 16 + ONE)
                if not isinstance(t, int) or t >= 2:
                    pe.wait_ge(out0, t - 1 + ONE)
                    pe.wait_ge(out1, t - 1 + ONE)
                for half in range(2):
                    for n in range(KD):
                        mm = pe.matmul(ps[:, u, half, :], w[:, u, n, :], s.hT[:, n, half * 512:(half + 1) * 512],
                                       start=(n == 0), stop=(n == KD - 1))
                    mm.then_inc(done, 1)
                    if half == 0 and item is not None:
                        pe.wait_ge(squared, t + 1 + ONE)
                        pe.wait_ge(std_ready, t + ONE)
                        for a in range(item.shape[2] // 512):
                            mm = pe.matmul(ps_n[:, a * 512:(a + 1) * 512], s.pair_ones, sq[:, a * 512:(a + 1) * 512], start=True, stop=True)
                        mm.then_inc(sum_ready, 1)

            def directions():
                for p, dst in enumerate((ps_n, ps_k)):
                    pe.wait_ge(kk_squared, p + 1 + ONE)
                    for a in range(2):
                        mm = pe.matmul(dst[:, a * 512:(a + 1) * 512], s.pair_ones, kk_sq[p][:, a * 512:(a + 1) * 512], start=True, stop=True)
                    mm.then_inc(kk_summed, 1)
            steps(pe, step, None, directions)

        @block.scalar
        def _(act):
            def step(t, k, u, col, item, weight):
                if item is not None:
                    ln = item.shape[2]
                    act.wait_ge(out0, t + ONE)
                    act.wait_ge(out1, t + ONE)
                    act.wait_ge(sum_ready, t + ONE)
                    act.activation(spare[:, :], s.eps, ACT.Copy)
                    act.activation(sq[:, 0:ln].unsqueeze(1), item, ACT.Square).then_inc(squared, 1)
                    act.wait_ge(sum_ready, t + 1 + ONE)
                    act.wait_ge(normed, t + ONE)
                    act.activation(std[:, 0:ln], ps_n[:, 0:ln], ACT.Sqrt, bias=s.eps, scale=1.0 / HD).then_inc(std_ready, 1)
                act.wait_ge(done, t * 2 + 1 + ONE)
                act.activation(s.proj[:, ds(col, 1), 0:512], ps[:, u, 0:1, :], ACT.Copy).then_inc(out0, 1)

            def shifted(t, u, col, n):
                act.wait_ge(kept, 1 + ONE)
                act.wait_ge(done, t * 2 + 2 + ONE)
                act.activation(s.proj[:, col, :], both(u), ACT.Copy, scale=keep[:, n:n + 1]).then_inc(out0, 1)

            def directions(n):
                for p in range(RW_PAIRS):
                    if n == 0:
                        act.wait_ge(kk_scaled, p + 1 + ONE)
                        act.activation(kk_sq[p], key_direction(s, p), ACT.Square).then_inc(kk_squared, 1)
                    if n == 2:
                        act.wait_ge(kk_summed, p + 1 + ONE)
                        act.activation(kk_sq[p], (ps_n, ps_k)[p][:, :], ACT.Sqrt).then_inc(kk_rooted, 1)
            steps(act, step, shifted, directions)

        @block.vector
        def _(dve):
            for n, name in enumerate(("naq_w", "mq_w")):
                dve.tensor_scalar(qw[:, n:n + 1], s.par(name, 1), HD ** -0.5, None, ALU.mult).then_inc(qscaled, 1)
            dve.wait_ge(qscaled, 2 + ONE)
            dve.tensor_tensor(keep[:, :], s.par("mu_p", RWC), s.par("mu_n", RWC), ALU.add).then_inc(qscaled, 1)
            dve.wait_ge(qscaled, 3 + ONE)
            dve.tensor_scalar(keep[:, :], keep[:, :], -1.0, 1.0, ALU.mult, ALU.add).then_inc(kept, 1)

            def step(t, k, u, col, item, weight):
                if item is not None:
                    ln = item.shape[2]
                    dve.wait_ge(std_ready, t + 1 + ONE)
                    dve.reciprocal(std[:, 0:ln], std[:, 0:ln]).then_inc(inv_ready, 1)
                    dve.wait_ge(inv_ready, t + 1 + ONE)
                    dve.scalar_tensor_tensor(out=item, in0=item, scalar=weight, in1=std[:, 0:ln].unsqueeze(1),
                                             op0=ALU.mult, op1=ALU.mult).then_inc(normed, 1)
                dve.wait_ge(done, t * 2 + 2 + ONE)
                dve.tensor_copy(s.proj[:, ds(col, 1), 512:1024], ps[:, u, 1:2, :]).then_inc(out1, 1)

            def shifted(t, u, col, n):
                src, dst = both(u), s.proj[:, col, :]
                dve.wait_ge(out0, t + 1 + ONE)
                dve.scalar_tensor_tensor(out=dst[:, 1:], in0=src[:, :-1], scalar=s.par("mu_p", RWC)[:, n:n + 1], in1=dst[:, 1:],
                                         op0=ALU.mult, op1=ALU.add).then_inc(shift_half, 1)
                dve.wait_ge(shift_half, n + 1 + ONE)
                dve.scalar_tensor_tensor(out=dst[:, :-1], in0=src[:, 1:], scalar=s.par("mu_n", RWC)[:, n:n + 1], in1=dst[:, :-1],
                                         op0=ALU.mult, op1=ALU.add).then_inc(out1, 1)

            def directions(n):
                if n == 0:
                    dve.wait_ge(out1, 2 + C_RW + 3 + 1 + ONE)
                    for p in range(RW_PAIRS):
                        dve.tensor_scalar(key_direction(s, p), s.proj[:, S_K + p, :], s.par("k_k", 2)[:, p:p + 1], None, ALU.mult)\
                           .then_inc(kk_scaled, 1)
                if n in (3, 4):
                    p = n - 3
                    dve.wait_ge(kk_rooted, p + 1 + ONE)
                    dve.tensor_scalar(kk_sq[p], kk_sq[p], 1e-12, None, ALU.max).then_inc(kk_steps, 1)
                    dve.wait_ge(kk_steps, 2 * p + 1 + ONE)
                    dve.reciprocal(kk_sq[p], kk_sq[p]).then_inc(kk_steps, 1)
                    dve.wait_ge(kk_steps, 2 * p + 2 + ONE)
                    dve.tensor_tensor(key_direction(s, p), key_direction(s, p), kk_sq[p], ALU.mult)
            steps(dve, step, shifted, directions)


def attention(nc, s, memory):
    tag = "m" if memory else "n"
    pairs = MEM_PAIRS if memory else NA_PAIRS
    nk = NMEM if memory else KH * GRID_W
    kt = nk // P
    G = ROWS
    nv = 0 if memory else ROWS - 1
    vb = -(-nv // 4)
    c_q, c_mix = (C_MQ, 6) if memory else (C_Q, 0)
    with ExitStack() as c:
        def sb(name, shape):
            return c.enter_context(nc.sbuf_tensor(f"at{tag}_{name}", shape, F32))

        def sem(name):
            return counter(nc, c, f"at{tag}_{name}")

        qbd = sb("qbd", [P, 2, G, P])
        tb = sb("tb", [P, 2, nk if memory else 15 * GRID_W])
        vst = sb("vst", [P, SEQ])
        v64 = sb("v64", [P, 16, P])
        ssb = sb("ssb", [P, 2, nk])
        pr = sb("pr", [P, 2, nk])
        pn = sb("pn", [P, 2, nk])
        ptb = sb("ptb", [P, 2, nk])
        nm = sb("nm", [P, 2, 4])
        rs = sb("rs", [P, 2, 4])
        ps_s = c.enter_context(nc.psum_tensor(f"at{tag}_ps_s", [P, 2, 512], F32))
        ps_t = c.enter_context(nc.psum_tensor(f"at{tag}_ps_t", [P, 2, 512], F32))
        ps_o = c.enter_context(nc.psum_tensor(f"at{tag}_ps_o", [P, 2, 512], F32))
        ps_v = c.enter_context(nc.psum_tensor(f"at{tag}_ps_v", [P, 2, 512], F32))
        zeroed, q_ready, v_copied, v_turned, v_ready = (sem(n) for n in ("zeroed", "q", "vcopy", "vturn", "vready"))
        bias_in = [sem(f"bias{u}") for u in range(2)]
        scored, biased, exped, inv_sum, normed = (sem(n) for n in ("scored", "biased", "exped", "invsum", "normed"))
        turned, pt_ready, summed, stored = (sem(n) for n in ("turned", "pt", "summed", "stored"))
        nc.all_engine_barrier()
        block = c.enter_context(nc.Block())

        def each_pair(eng, body):
            with eng.Fori(0, pairs // 2) as i:
                for u in range(2):
                    body(i * 2 + u, i, u)

        def lay_out(eng, j):
            for h in range(2):
                p0, p1 = h * HD, (h + 1) * HD
                eng.tensor_copy(qbd[p0:p1, j % 2, :, p0:p1], s.proj[p0:p1, c_q + j, :]
                                .rearrange("p (r c) -> p r c", c=HD)).then_inc(q_ready, 1)

        @block.sync
        def _(sp):
            def body(j, i, u):
                sp.wait_ge(biased, i * 2 * G + ONE)
                sp.dma_start(tb[:, u, :], s.bias_dram.rearrange("(j a) c d k -> j (a c) (d k)", a=2)[ds(j, 1)]
                             .rearrange("o p r -> p (o r)")).then_inc(bias_in[u], 16)
            if not memory:
                each_pair(sp, body)

        @block.gpsimd
        def _(pool):
            for j in range(1, pairs):
                if j == 1:
                    pool.wait_ge(q_ready, 2 + ONE)
                    pool.wait_ge(zeroed, 2 + ONE)
                if j >= 2:
                    pool.wait_ge(scored, (j - 1) * G + ONE)
                lay_out(pool, j)

        @block.tensor
        def _(pe):
            def body(j, i, u):
                pe.wait_ge(q_ready, j * 2 + 2 + ONE)

                def turn_values():
                    pe.wait_ge(v_copied, j + 1 + ONE)
                    for b in range(vb):
                        pe.wait_ge(v_ready, j * vb + max(b - 1, 0) + ONE)
                        for m in range(4 * b, min(4 * b + 4, nv)):
                            mm = pe.transpose(ps_v[:, b % 2, (m % 4) * P:(m % 4 + 1) * P], vst[:, m * HD:m * HD + P], s.ident)
                        mm.then_inc(v_turned, 1)

                for r in range(G + 3):
                    if r < G:
                        pe.wait_ge(biased, j * G + max(r - 1, 0) + ONE)
                        ks = window_start(r) * GRID_W
                        keys = s.mkT[:, ds(j, 1), :] if memory else s.proj[:, ds(j + C_K, 1), ks:ks + nk]
                        pe.matmul(ps_s[:, r % 2, 0:nk].unsqueeze(1), qbd[:, u, r, :], keys, start=True, stop=True).then_inc(scored, 1)
                    if r == 1 and not memory:
                        turn_values()
                    if 2 <= r < G + 2:
                        q = r - 2
                        pe.wait_ge(normed, j * G + q + 1 + ONE)
                        pe.wait_ge(pt_ready, j * G + max(q - 1, 0) + ONE)
                        for a in range(kt):
                            mm = pe.transpose(ps_t[:, q % 2, a * P:(a + 1) * P], pn[:, q % 2, a * P:(a + 1) * P], s.ident)
                        mm.then_inc(turned, 1)
                    if r >= 3:
                        q = r - 3
                        if q == 0 and not memory:
                            pe.wait_ge(v_ready, j * vb + vb + ONE)
                        pe.wait_ge(pt_ready, j * G + q + 1 + ONE)
                        pe.wait_ge(stored, j * G + max(q - 1, 0) + ONE)
                        for a in range(kt):
                            if memory:
                                v = s.mv[:, a, u * P:(u + 1) * P]
                            else:
                                v = v64[:, window_start(q) + 2 * a, :]
                            mm = pe.matmul(ps_o[:, q % 2, 0:P], v, ptb[:, q % 2, a * P:(a + 1) * P],
                                           start=(a == 0), stop=(a == kt - 1))
                        mm.then_inc(summed, 1)
            each_pair(pe, body)

        @block.vector
        def _(dve):
            dve.memset(qbd[:, 0, :, :], 0.0).then_inc(zeroed, 1)
            dve.wait_ge(zeroed, 1 + ONE)
            lay_out(dve, 0)
            dve.memset(qbd[:, 1, :, :], 0.0).then_inc(zeroed, 1)
            if memory:
                dve.memset(tb[:, :, :], 0.0).then_inc(zeroed, 1)
                dve.wait_ge(zeroed, 3 + ONE)

            def body(j, i, u):
                if not memory:
                    dve.wait_ge(bias_in[u], i * 16 + 16 + ONE)
                for r in range(G + 4):
                    if r < G:
                        t0 = 0 if memory else (window_start(r) - r + KH - 1) * GRID_W
                        dve.wait_ge(scored, j * G + r + 1 + ONE)
                        dve.wait_ge(exped, j * G + max(r - 1, 0) + ONE)
                        dve.memset(nm[:, r % 2, 1:2], 0.0)
                        dve.tensor_tensor_reduce(ssb[:, r % 2, :], ps_s[:, r % 2, 0:nk], tb[:, u, t0:t0 + nk], -1.0, 3.0e38,
                                                 ALU.add, ALU.min, nm[:, r % 2, 0:1]).then_inc(biased, 1)
                    if 1 <= r <= G:
                        q = r - 1
                        dve.wait_ge(exped, j * G + q + 1 + ONE)
                        dve.reciprocal(rs[:, q % 2, 1:2], rs[:, q % 2, 0:1]).then_inc(inv_sum, 1)
                        dve.wait_ge(inv_sum, j * G + q + 1 + ONE)
                        dve.wait_ge(turned, j * G + max(q - 1, 0) + ONE)
                        dve.tensor_scalar(pn[:, q % 2, :], pr[:, q % 2, :], rs[:, q % 2, 1:2], None, ALU.mult).then_inc(normed, 1)
                    if r >= 4:
                        q = r - 4
                        dve.wait_ge(summed, j * G + q + 1 + ONE)
                        for h in range(2):
                            p0, p1 = h * HD, (h + 1) * HD
                            o = dve.tensor_copy(s.mixT[p0:p1, ds(j + c_mix, 1), q * HD:(q + 1) * HD],
                                                ps_o[p0:p1, q % 2, p0:p1].unsqueeze(1))
                        o.then_inc(stored, 1)
            each_pair(dve, body)

        @block.scalar
        def _(act):
            def body(j, i, u):
                if not memory:
                    act.wait_ge(v_turned, j * vb + ONE)
                    act.activation(vst[:, :].unsqueeze(1), s.proj[:, ds(j + C_V, 1), :], ACT.Copy).then_inc(v_copied, 1)
                for r in range(G + 2):
                    if r < G:
                        act.wait_ge(biased, j * G + r + 1 + ONE)
                        act.wait_ge(normed, j * G + max(r - 1, 0) + ONE)
                        act.activation(pr[:, r % 2, :], ssb[:, r % 2, :], ACT.Exp, bias=nm[:, r % 2, 0:1], scale=-1.0,
                                       accum_out=rs[:, r % 2, 0:1]).then_inc(exped, 1)
                    if r < 2:
                        for b in range(r * 2, min(r * 2 + 2, vb)):
                            m = min(4, nv - 4 * b)
                            act.wait_ge(v_turned, j * vb + b + 1 + ONE)
                            act.wait_ge(summed, j * G + ONE)
                            act.activation(v64[:, 4 * b:4 * b + m, :].rearrange("p a b -> p (a b)"), ps_v[:, b % 2, 0:m * P],
                                           ACT.Copy).then_inc(v_ready, 1)
                    if r >= 2:
                        q = r - 2
                        act.wait_ge(turned, j * G + q + 1 + ONE)
                        act.wait_ge(summed, j * G + max(q - 1, 0) + ONE)
                        act.activation(ptb[:, q % 2, :], ps_t[:, q % 2, 0:nk], ACT.Copy).then_inc(pt_ready, 1)
            each_pair(act, body)


def prod(s, n):
    return s.proj[:, S_PROD + 4 * n:S_PROD + 4 * n + 4, :] if n < 3 else s.extra[:, 0:4, :]


def gates(nc, s):
    with ExitStack() as c:
        def sem(name):
            return counter(nc, c, "ga_" + name)
        tmp = c.enter_context(nc.sbuf_tensor("ga_tmp", [P, 12, SEQ], F32))
        go = tmp[:, 8, :]
        w2, a2, g2 = (tmp[:, 9, n * 256:(n + 1) * 256] for n in range(3))
        ps = c.enter_context(nc.psum_tensor("ga_ps", [P, 4, SEQ], F32))
        loaded, act_in, grouped, taken = (sem(n) for n in ("loaded", "act_in", "grouped", "taken"))
        kd_steps, b_ready, go_ready, cum_steps = (sem(n) for n in ("kd_steps", "b_ready", "go_ready", "cum"))
        exps, inverses, bonus_steps = (sem(n) for n in ("exps", "inverses", "bonus"))
        nc.all_engine_barrier()
        block = c.enter_context(nc.Block())
        tanh_lw, sig_lg = s.proj[:, S_LW, :], s.proj[:, S_LG, :]

        def lw(n):
            return tmp[:, n, :]

        def a(n):
            return tmp[:, 4 + n, :]

        def kk(p):
            return key_direction(s, p)

        def cum(n):
            return tmp[:, 10 + n, :] if n < 2 else s.proj[:, S_LG if n % 2 else S_LW, :]

        def decay_updates(eng, units):
            for n in units:
                eng.wait_ge(b_ready, n + 1 + ONE)
                eng.wait_ge(inverses, n + 1 + ONE)
                for j in (2, 3):
                    eng.tensor_tensor(prod(s, n)[:, j, :], prod(s, n)[:, j, :], a(n), ALU.mult)

        @block.sync
        def _(sp):
            sp.dma_start(w2[:, :], s.inp["rw_w2"].rearrange("d k n -> (d k) n")).then_inc(loaded, 16)
            sp.dma_start(a2[:, :], s.inp["rw_a2"].rearrange("d k n -> (d k) n")).then_inc(loaded, 16)
            sp.dma_start(g2[:, :], s.inp["rw_g2"]).then_inc(loaded, 16)

        @block.tensor
        def _(pe):
            def group(n, lhsT, rhs):
                if n >= 4:
                    pe.wait_ge(taken, n - 3 + ONE)
                for half in range(2):
                    mm = pe.matmul(ps[:, n % 4, half * 512:(half + 1) * 512], lhsT, rhs[:, half * 512:(half + 1) * 512],
                                   start=True, stop=True)
                mm.then_inc(grouped, 1)
            pe.wait_ge(loaded, 48 + ONE)
            pe.wait_ge(act_in, 1 + ONE)
            for n, (d, p) in enumerate(UNITS):
                group(n, w2[d * HD:(d + 1) * HD, p * P:(p + 1) * P], tanh_lw[d * HD:(d + 1) * HD, :])
            pe.wait_ge(act_in, 2 + ONE)
            for p in range(RW_PAIRS):
                group(4 + p, g2[:, p * P:(p + 1) * P], sig_lg)
            for n, (d, p) in enumerate(UNITS):
                group(6 + n, a2[d * HD:(d + 1) * HD, p * P:(p + 1) * P], s.proj[d * HD:(d + 1) * HD, S_LA, :])

        @block.scalar
        def _(act):
            act.activation(tanh_lw, s.proj[:, S_LW, :], ACT.Tanh).then_inc(act_in, 1)
            act.activation(sig_lg, s.proj[:, S_LG, :], ACT.Sigmoid).then_inc(act_in, 1)
            for n in range(4):
                act.wait_ge(grouped, n + 1 + ONE)
                act.activation(lw(n), ps[:, n % 4, :], ACT.Sigmoid, bias=s.par("w0", 4)[:, n:n + 1]).then_inc(taken, 1)
            for p in range(RW_PAIRS):
                act.wait_ge(grouped, 4 + p + 1 + ONE)
                act.activation(s.extra[:, 4 + p, :], ps[:, (4 + p) % 4, :], ACT.Copy).then_inc(taken, 1)
            def incl(n):
                return cum(n) if n < 2 else lw(n)
            for n in range(4):
                pr = prod(s, n)
                act.wait_ge(cum_steps, 3 * n + 3 + ONE)
                act.activation(pr[:, 0, :], pr[:, 0, :], ACT.Exp, scale=-DECAY).then_inc(exps, 1)
                act.activation(pr[:, 1, :], incl(n), ACT.Exp, scale=-DECAY).then_inc(exps, 1)
                act.activation(s.ec[:, n, :], cum(n).rearrange("p (c t) -> p c t", t=CHUNK)[:, :, CHUNK - 1], ACT.Exp,
                               scale=-DECAY)
            for n in range(4):
                act.wait_ge(grouped, 6 + n + 1 + ONE)
                act.activation(a(n), ps[:, (6 + n) % 4, :], ACT.Sigmoid, bias=s.par("a0", 4)[:, n:n + 1]).then_inc(taken, 1)
            for n in range(4):
                act.wait_ge(b_ready, n + 1 + ONE)
                act.wait_ge(kd_steps, 2 * n + 1 + ONE)
                act.activation(a(n), incl(n), ACT.Exp, scale=DECAY).then_inc(inverses, 1)

        @block.vector
        def _(dve):
            dve.memset(go, 1.0).then_inc(go_ready, 1)
            dve.wait_ge(go_ready, 1 + ONE)
            dve.memset(go.rearrange("p (c t) -> p c t", t=CHUNK)[:, :, 0:1], 0.0).then_inc(go_ready, 1)

            def cumulate(n):
                dve.wait_ge(taken, 1 + n + ONE)
                if n >= 2:
                    dve.wait_ge(grouped, 2 * n + ONE)
                dve.tensor_tensor_scan(cum(n), go, lw(n), 0.0, ALU.mult, ALU.add).then_inc(cum_steps, 1)
                dve.wait_ge(cum_steps, 3 * n + 1 + ONE)
                if UNITS[n][0] == 0:
                    dve.tensor_tensor(prod(s, n)[:, 0, :], cum(n), lw(n), ALU.subtract).then_inc(cum_steps, 2)
                else:
                    total = cum(n).rearrange("p (c t) -> p c t", t=CHUNK)[:, :, CHUNK - 1:CHUNK].to_broadcast([P, NCH, CHUNK])
                    dve.tensor_tensor(prod(s, n)[:, 0, :].rearrange("p (c t) -> p c t", t=CHUNK), total,
                                      cum(n).rearrange("p (c t) -> p c t", t=CHUNK), ALU.subtract).then_inc(cum_steps, 1)
                    dve.wait_ge(cum_steps, 3 * n + 2 + ONE)
                    dve.tensor_tensor(lw(n), prod(s, n)[:, 0, :], lw(n), ALU.add).then_inc(cum_steps, 1)

            def update_key(n):
                p = UNITS[n][1]
                dve.wait_ge(taken, n + 7 + ONE)
                dve.tensor_scalar(prod(s, n)[:, 3, :], a(n), 1.0, s.par("k_a", 2)[:, p:p + 1], ALU.subtract, ALU.mult).then_inc(kd_steps, 1)
                dve.wait_ge(kd_steps, 2 * n + 1 + ONE)
                dve.scalar_tensor_tensor(out=prod(s, n)[:, 3, :], in0=prod(s, n)[:, 3, :], scalar=1.0, in1=s.proj[:, S_K + p, :],
                                         op0=ALU.add, op1=ALU.mult).then_inc(kd_steps, 1)

            def sum_keys(p):
                dve.wait_ge(kd_steps, 2 * (p + 2) + 2 + ONE)
                dve.tensor_tensor(s.proj[:, S_BONUS[p], :], prod(s, p)[:, 3, :], prod(s, p + 2)[:, 3, :], ALU.add).then_inc(bonus_steps, 1)
                dve.wait_ge(bonus_steps, 2 * p + 1 + ONE)
                dve.scalar_tensor_tensor(out=s.proj[:, S_BONUS[p], :], in0=s.proj[:, S_BONUS[p], :], scalar=s.par("r_k", 2)[:, p:p + 1],
                                         in1=s.proj[:, S_R + p, :], op0=ALU.mult, op1=ALU.mult).then_inc(bonus_steps, 1)

            def scale(n):
                p = UNITS[n][1]
                dve.wait_ge(exps, 2 * n + 2 + ONE)
                dve.tensor_tensor(prod(s, n)[:, 0, :], prod(s, n)[:, 0, :], kk(p), ALU.mult)
                dve.tensor_tensor(prod(s, n)[:, 1, :], prod(s, n)[:, 1, :], s.proj[:, S_R + p, :], ALU.mult)
            dve.wait_ge(go_ready, 2 + ONE)
            for n in range(4):
                cumulate(n)
            for n in range(4):
                scale(n)
            for n in range(4):
                update_key(n)
            for p in range(RW_PAIRS):
                sum_keys(p)
            dve.wait_ge(bonus_steps, 4 + ONE)
            decay_updates(dve, range(2))

        @block.gpsimd
        def _(pool):
            for n, (d, p) in enumerate(UNITS):
                pool.wait_ge(taken, 7 + n + ONE)
                pool.tensor_tensor(prod(s, n)[:, 2, :], kk(p), a(n), ALU.mult).then_inc(b_ready, 1)
            pool.wait_ge(bonus_steps, 4 + ONE)
            pool.wait_ge(b_ready, 4 + ONE)
            decay_updates(pool, range(2, 4))


def scan(nc, s):
    NU = len(UNITS)
    with ExitStack() as c:
        def sb(name, shape):
            return c.enter_context(nc.sbuf_tensor("sc_" + name, shape, F32))

        def sem(name):
            return counter(nc, c, "sc_" + name)
        bd_all = [sb("bd", [P, NU, 5, P])[:, :, :, :],
                  s.proj[:, S_LW:S_LG + 1, :].rearrange("p a t -> p (a t)")[:, 0:NU * 5 * P].rearrange("p (n f c) -> p n f c", n=NU, f=5)]
        lm = sb("lm", [P, NU, 512])
        xm = sb("xm", [P, NU, 3 * P])
        qq = sb("qq", [P, NU, 2, P])
        mm2 = sb("mm2", [P, NU, 2, 2, P])
        y1 = sb("y1", [P, NU, P])
        btv = sb("btv", [P, NU, 320])
        wu = sb("wu", [P, NU, 2, HD])
        st = sb("st", [P, NU, HD])
        ps = c.enter_context(nc.psum_tensor("sc_ps", [P, NU, 2, 512], F32))
        zeroed, packed, unpacked, seeded = (sem(n) for n in ("zeroed", "packed", "unpacked", "seeded"))
        prods, masked, sides = (sem(n) for n in ("products", "masked", "sides"))
        powed, pow_out, improved, inverse = (sem(n) for n in ("powed", "pow_out", "improved", "inverse"))
        crossed, cross_out, flipped, flip_out = (sem(n) for n in ("crossed", "cross_out", "flipped", "flip_out"))
        w_sum, w_out, u_sum, u_out, y_sum, y_out, s_out = (sem(n) for n in ("w_sum", "w_out", "u_sum", "u_out", "y_sum", "y_out", "s_out"))
        nc.all_engine_barrier()
        block = c.enter_context(nc.Block())
        yb = s.proj[:, S_R:S_R + 4, :].rearrange("p n (c v) -> p n c v", v=HD)

        def chunk_of(i, n):
            return i if UNITS[n][0] == 0 else i * -1 + (NCH - 1)

        def both_chunks(eng, chunk):
            with eng.Fori(0, NCH // 2) as i:
                for u in range(2):
                    chunk(i * 2 + u, bd_all[u])

        @block.gpsimd
        def _(pool):
            for bd in bd_all:
                pool.memset(bd, 0.0).then_inc(zeroed, 1)
            pool.wait_ge(zeroed, 2 + ONE)

            def chunk(i, bd):
                pool.wait_ge(seeded, i * NU + ONE)
                for n, (d, p) in enumerate(UNITS):
                    tok = chunk_of(i, n) * CHUNK
                    pool.wait_ge(y_sum, i * NU + ONE)
                    for h in range(2):
                        p0, p1 = h * HD, (h + 1) * HD
                        pool.tensor_copy(bd[p0:p1, n, 0:4, p0:p1], prod(s, n)[p0:p1, :, ds(tok, CHUNK)]).then_inc(packed, 1)
                        pool.tensor_copy(bd[p0:p1, n, 4, p0:p1], s.proj[p0:p1, S_V + p, ds(tok, CHUNK)]).then_inc(packed, 1)
                pool.wait_ge(packed, i * NU * 4 + NU * 4 + ONE)
                for n in range(NU):
                    pool.wait_ge(masked, (i * NU + n) * 2 + 2 + ONE)
                    pool.tensor_tensor(qq[:, n, 0, :], lm[:, n, 0:P], s.ident, ALU.add).then_inc(seeded, 1)
            both_chunks(pool, chunk)
            pool.memset(both_directions(s), 0.0)

        @block.tensor
        def _(pe):
            pe.sem_inc(y_sum, NU)

            def chunk(i, bd):
                def at(n, per=1):
                    return (i * NU + n) * per
                for n in range(NU):
                    b = bd[:, n, :, :]
                    pe.wait_ge(packed, at(n, 4) + 4 + ONE)
                    pe.wait_ge(y_out, at(n) + 1 + ONE)
                    kr = b[:, 0:2, :].rearrange("p a b -> p (a b)")
                    pe.matmul(ps[:, n, 0, 0:256], b[:, 2, :], kr, start=True, stop=True)
                    pe.matmul(ps[:, n, 0, 256:512], b[:, 3, :], kr, start=True, stop=True)
                    pe.matmul(ps[:, n, 1, 0:P], b[:, 0, :], b[:, 2, :], start=True, stop=True)
                    pe.transpose(ps[:, n, 1, P:2 * P], b[:, 2, :], s.ident)
                    pe.transpose(ps[:, n, 1, 2 * P:3 * P], b[:, 3, :], s.ident)
                    pe.matmul(ps[:, n, 1, 3 * P:3 * P + HD], b[:, 4, :], s.fold, start=True, stop=True).then_inc(prods, 1)
                for n in range(NU):
                    pe.wait_ge(masked, at(n, 2) + 2 + ONE)
                    pe.matmul(ps[:, n, 0, 0:P], lm[:, n, 0:P], xm[:, n, 0:P], start=True, stop=True)
                    pe.matmul(ps[:, n, 0, P:2 * P], xm[:, n, 0:P], lm[:, n, 0:P], start=True, stop=True).then_inc(powed, 1)
                for step in range(3):
                    for n in range(NU):
                        m = mm2[:, n, step % 2, :, :]
                        pe.wait_ge(pow_out, (i * NU * 3) + NU * step + n + 1 + ONE)
                        if step == 0:
                            pe.wait_ge(seeded, at(n) + 1 + ONE)
                            pe.wait_ge(sides, at(n) + 1 + ONE)
                        else:
                            pe.wait_ge(improved, (i * NU * 4) + NU * (step - 1) + n + 1 + ONE)
                        mm = pe.matmul(ps[:, n, 1, 0:P], m[:, 0, :], qq[:, n, 0, :], start=True, stop=True)
                        if step < 2:
                            mm = pe.matmul(ps[:, n, 0, 0:P], m[:, 1, :], m[:, 0, :], start=True, stop=True)
                        if step < 1:
                            mm = pe.matmul(ps[:, n, 0, P:2 * P], m[:, 0, :], m[:, 1, :], start=True, stop=True)
                        mm.then_inc(powed, 1)
                for level in range(2):
                    for n in range(NU):
                        pe.wait_ge(improved, (i * NU * 4) + NU * (2 + level) + n + 1 + ONE)
                        pe.matmul(ps[:, n, 0, 0:P], xm[:, n, (level + 1) * P:(level + 2) * P], qq[:, n, 0, :],
                                  start=True, stop=True).then_inc(crossed, 1)
                        if level == 0:
                            pe.transpose(ps[:, n, 1, P:2 * P], qq[:, n, 0, :], s.ident).then_inc(flipped, 1)
                    for n in range(NU):
                        if level == 0:
                            pe.wait_ge(flip_out, at(n) + 1 + ONE)
                        pe.wait_ge(cross_out, (i * NU * 2) + NU * level + n + 1 + ONE)
                        mm = pe.matmul(ps[:, n, 1, 0:P], qq[:, n, 1, :], y1[:, n, :], start=True, stop=True)
                        if level == 0:
                            mm = pe.matmul(ps[:, n, 1, P:2 * P], y1[:, n, :], qq[:, n, 1, :], start=True, stop=True)
                        mm.then_inc(crossed, 1)
                for n in range(NU):
                    pe.wait_ge(s_out, at(n) + 1 + ONE)
                    pe.matmul(ps[:, n, 0, 0:HD], bd[:, n, 0, :], st[:, n, :], start=True, stop=False)
                    pe.matmul(ps[:, n, 0, 0:HD], lm[:, n, 256:384], btv[:, n, 256:320], start=False, stop=True).then_inc(w_sum, 1)
                for n in range(NU):
                    pe.wait_ge(w_out, at(n) + 1 + ONE)
                    pe.wait_ge(inverse, at(n) + 1 + ONE)
                    pe.matmul(ps[:, n, 0, HD:2 * HD], qq[:, n, 0, :], wu[:, n, 0, :], start=True, stop=True).then_inc(u_sum, 1)
                for n in range(NU):
                    pe.wait_ge(u_out, at(n) + 1 + ONE)
                    pe.matmul(ps[:, n, 0, 2 * HD:3 * HD], s.ident, st[:, n, :], start=True, stop=False)
                    pe.matmul(ps[:, n, 0, 2 * HD:3 * HD], btv[:, n, 0:P], wu[:, n, 1, :], start=False, stop=False)
                    pe.matmul(ps[:, n, 0, 2 * HD:3 * HD], btv[:, n, P:2 * P], btv[:, n, 256:320], start=False, stop=True)
                    pe.matmul(ps[:, n, 1, 0:HD], bd[:, n, 1, :], st[:, n, :], start=True, stop=False)
                    pe.matmul(ps[:, n, 1, 0:HD], lm[:, n, P:2 * P], wu[:, n, 1, :], start=False, stop=False)
                    pe.matmul(ps[:, n, 1, 0:HD], lm[:, n, 384:512], btv[:, n, 256:320], start=False, stop=True).then_inc(y_sum, 1)
            both_chunks(pe, chunk)

        @block.vector
        def _(dve):
            dve.memset(st[:, :, :], 0.0).then_inc(s_out, NU)
            dve.sem_inc(y_out, NU)
            with dve.Fori(0, NCH) as i:
                def at(n, per=1):
                    return (i * NU + n) * per
                for n, (d, p) in enumerate(UNITS):
                    dve.wait_ge(prods, at(n) + 1 + ONE)
                    dve.wait_ge(u_out, at(0) + ONE)
                    dve.tensor_tensor(xm[:, n, :].rearrange("p (a b) -> p a b", a=3),
                                      ps[:, n, 1:2, 0:P].to_broadcast([P, 3, P]),
                                      s.x_mask[d].rearrange("p (a b) -> p a b", a=3), ALU.mult).then_inc(masked, 1)
                    dve.tensor_tensor(lm[:, n, :], ps[:, n, 0, :], s.l_mask[d], ALU.mult).then_inc(masked, 1)
                for step in range(3):
                    for n in range(NU):
                        dve.wait_ge(powed, (i * NU * 4) + NU * (step + 1) + n + 1 + ONE)
                        dve.tensor_tensor(qq[:, n, 0, :], ps[:, n, 1, 0:P], qq[:, n, 0, :], ALU.add).then_inc(improved, 1)
                for n in range(NU):
                    dve.wait_ge(flipped, at(n) + 1 + ONE)
                    dve.tensor_copy(qq[:, n, 1, :], ps[:, n, 1, P:2 * P]).then_inc(flip_out, 1)
                for level in range(2):
                    for n in range(NU):
                        dve.wait_ge(crossed, (i * NU * 4) + NU * (2 * level + 1) + n + 1 + ONE)
                        if level == 0:
                            dve.tensor_tensor(qq[:, n, :, :], ps[:, n, 1, 0:256].rearrange("p (a b) -> p a b", a=2), qq[:, n, :, :],
                                              ALU.add).then_inc(improved, 1)
                        else:
                            dve.tensor_tensor(qq[:, n, 0, :], ps[:, n, 1, 0:P], qq[:, n, 0, :], ALU.add).then_inc(inverse, 1)
                for n in range(NU):
                    ch = chunk_of(i, n)
                    dve.wait_ge(y_sum, at(n) + NU + 1 + ONE)
                    dve.tensor_tensor(st[:, n, :], ps[:, n, 0, 2 * HD:3 * HD],
                                      s.ec[:, n, ds(ch, 1)].to_broadcast([P, HD]), ALU.mult).then_inc(s_out, 1)
                    dve.tensor_copy(yb[:, n, ds(ch, 1), :], ps[:, n, 1:2, 0:HD]).then_inc(y_out, 1)

        @block.scalar
        def _(act):
            with act.Fori(0, NCH) as i:
                def at(n, per=1):
                    return (i * NU + n) * per
                for n in range(NU):
                    act.wait_ge(masked, at(n, 2) + 1 + ONE)
                    act.activation(btv[:, n, :], ps[:, n, 1, P:P + 320], ACT.Copy).then_inc(sides, 1)
                for step in range(3):
                    for n in range(NU):
                        act.wait_ge(powed, (i * NU * 4) + NU * step + n + 1 + ONE)
                        ln = 2 * P if step < 2 else P
                        act.activation(mm2[:, n, step % 2, :, :].rearrange("p a b -> p (a b)")[:, 0:ln], ps[:, n, 0, 0:ln],
                                       ACT.Copy).then_inc(pow_out, 1)
                for level in range(2):
                    for n in range(NU):
                        act.wait_ge(crossed, (i * NU * 4) + NU * 2 * level + n + 1 + ONE)
                        act.activation(y1[:, n, :], ps[:, n, 0, 0:P], ACT.Copy).then_inc(cross_out, 1)
                for n in range(NU):
                    act.wait_ge(w_sum, at(n) + 1 + ONE)
                    act.activation(wu[:, n, 0, :], ps[:, n, 0, 0:HD], ACT.Copy).then_inc(w_out, 1)
                for n in range(NU):
                    act.wait_ge(u_sum, at(n) + 1 + ONE)
                    act.activation(wu[:, n, 1, :], ps[:, n, 0, HD:2 * HD], ACT.Copy, scale=-1.0).then_inc(u_out, 1)


def both_directions(s):
    return s.proj[:, S_PROD:S_PROD + 4, :].rearrange("p a t -> p (a t)").rearrange("p (n c k) -> p n c k", n=RW_PAIRS, c=NCH)


ATTENTION, RWKV = (0, 1, 2, 3, 6, 7), (4, 5)
EARLY = 2


def out_products(pe, s, t, half, chunks):
    for k in chunks:
        mm = pe.matmul(s.ps_out[:, t % 2, half * 512:(half + 1) * 512], s.mixT[:, k, t * P:(t + 1) * P],
                       s.w_out[:, k, half * 512:(half + 1) * 512], start=(k == ATTENTION[0]), stop=(k == RWKV[-1]))
    return mm


def rwkv_out(nc, s):
    with ExitStack() as c:
        def sem(name):
            return c.enter_context(nc.semaphore("ro_" + name))
        yt = c.enter_context(nc.sbuf_tensor("ro_yt", [P, RW_PAIRS, SEQ], F32))
        py = s.ps_out
        pn = c.enter_context(nc.psum_tensor("ro_pn", [P, SEQ], F32))
        pb = c.enter_context(nc.psum_tensor("ro_pb", [P, SEQ], F32))
        packed = [sem("packed0"), sem("packed1")]
        turned, stored, meaned, centred, squared, spread, rooted, bonus, with_v, steps = (
            sem(n) for n in ("turned", "stored", "mean", "centred", "sq", "var", "root", "bonus", "with_v", "steps"))
        block = c.enter_context(nc.Block())
        yb = s.proj[:, S_R:S_R + 4, :].rearrange("p n (c v) -> p n c v", v=HD)
        ybd = both_directions(s)
        root = s.proj[:, S_PROD + 4:S_PROD + 6, :]
        sq = s.proj[:, S_PROD + 6:S_PROD + 8, :]

        def pack(eng, p):
            for h in range(2):
                p0, p1 = h * HD, (h + 1) * HD
                eng.tensor_tensor(ybd[p0:p1, p, :, p0:p1], yb[p0:p1, p, :, :], yb[p0:p1, p + 2, :, :], ALU.add).then_inc(packed[p], 1)

        @block.sync
        def _(sp):
            for a in range(2):
                ks = slice(a * KD // 2, (a + 1) * KD // 2)
                sp.dma_start(s.w_out[:, ks, :], s.inp["w_out"].rearrange("(k p) n -> p k n", p=P)[:, ks, :]).then_inc(s.w_out_in[a], 16)

        @block.gpsimd
        def _(pool):
            pack(pool, 1)

        @block.tensor
        def _(pe):
            def sums(dst, src, done):
                for half in range(2):
                    mm = pe.matmul(dst[:, half * 512:(half + 1) * 512], s.pair_ones, src[:, half * 512:(half + 1) * 512], start=True, stop=True)
                mm.then_inc(done, 1)
            sums(pb, s.proj[:, S_BONUS[0], :], bonus)
            for p in range(RW_PAIRS):
                pe.wait_ge(packed[p], 2)
                for i in range(NCH):
                    mm = pe.matmul(py[:, p, i * CHUNK:(i + 1) * CHUNK], ybd[:, p, i, :], s.fold, start=True, stop=True)
                mm.then_inc(turned, 1)
            for p in range(RW_PAIRS):
                pe.wait_ge(stored, p + 1)
                if p:
                    pe.wait_ge(rooted, p)
                sums(pn, yt[:, p, :], meaned)
                if p:
                    pe.wait_ge(with_v, p)
                    sums(pb, s.proj[:, S_BONUS[p], :], bonus)
                pe.wait_ge(squared, p + 1)
                pe.wait_ge(centred, p + 1)
                sums(pn, sq[:, p, :], spread)
            for a in range(2):
                pe.wait_ge(s.w_out_in[a], 16)
            for t in range(EARLY):
                for half in range(2):
                    out_products(pe, s, t, half, ATTENTION)

        @block.scalar
        def _(act):
            for p in range(RW_PAIRS):
                act.wait_ge(turned, p + 1)
                act.activation(yt[:, p, :], py[:, p, :], ACT.Copy).then_inc(stored, 1)
            for p in range(RW_PAIRS):
                act.wait_ge(centred, p + 1)
                act.activation(sq[:, p, :], yt[:, p, :], ACT.Square).then_inc(squared, 1)
                act.wait_ge(spread, p + 1)
                act.activation(root[:, p, :], pn[:, :], ACT.Sqrt, bias=s.gn_eps, scale=1.0 / HD).then_inc(rooted, 1)

        @block.vector
        def _(dve):
            def centre(p):
                dve.wait_ge(meaned, p + 1)
                dve.wait_ge(stored, p + 1)
                dve.scalar_tensor_tensor(out=yt[:, p, :], in0=pn[:, :], scalar=-1.0 / HD, in1=yt[:, p, :], op0=ALU.mult, op1=ALU.add)\
                   .then_inc(centred, 1)

            def gate_v(p):
                v = s.proj[:, S_V + p, :]
                dve.wait_ge(bonus, p + 1)
                dve.tensor_tensor(v, pb[:, :], v, ALU.mult).then_inc(with_v, 1)

            def finish(p, half):
                cols = slice(half * 512, (half + 1) * 512)
                n = (2 * p + half) * 3
                dve.wait_ge(rooted, p + 1)
                dve.reciprocal(root[:, p, cols], root[:, p, cols]).then_inc(steps, 1)
                dve.wait_ge(steps, n + 1)
                dve.scalar_tensor_tensor(out=yt[:, p, cols], in0=yt[:, p, cols], scalar=s.par("ln_w", 2)[:, p:p + 1],
                                         in1=root[:, p, cols], op0=ALU.mult, op1=ALU.mult).then_inc(steps, 1)
                dve.wait_ge(steps, n + 2)
                dve.wait_ge(with_v, p + 1)
                dve.scalar_tensor_tensor(out=yt[:, p, cols], in0=yt[:, p, cols], scalar=s.par("ln_b", 2)[:, p:p + 1],
                                         in1=s.proj[:, S_V + p, cols], op0=ALU.add, op1=ALU.add).then_inc(steps, 1)
                dve.wait_ge(steps, n + 3)
                dve.tensor_tensor(s.mixT[:, 4 + p, cols], yt[:, p, cols], s.extra[:, 4 + p, cols], ALU.mult)
            pack(dve, 0)
            gate_v(0)
            centre(0)
            finish(0, 0)
            centre(1)
            finish(0, 1)
            gate_v(1)
            finish(1, 0)
            finish(1, 1)


def out_projection_router(nc, s):
    with ExitStack() as c:
        def sb(name, shape):
            return c.enter_context(nc.sbuf_tensor("op_" + name, shape, F32))

        def sem(name):
            return c.enter_context(nc.semaphore("op_" + name))
        sq, wf = s.proj[:, 8, :], s.proj[:, 9, :]
        h = s.proj[:, 10:12, :]
        hT = s.proj[:, 12:14, :].rearrange("p a (k t) -> p a k t", k=KD)
        wr = sb("wr", [P, KD, NG + NE])
        br = sb("br", [P, NG + NE])
        st = sb("st", [P, 2, 4])
        pt = c.enter_context(nc.psum_tensor("op_pt", [P, KD, P], F32))
        pl = c.enter_context(nc.psum_tensor("op_pl", [P, 2, 512], F32))
        x_in = [sem(f"x_in{n}") for n in range(TT // 2)]
        router_in, done, added = (sem(n) for n in ("router_in", "done", "added"))
        summed, rooted, inverted, normed, turned, copied, logits, biased = (
            sem(n) for n in ("summed", "rooted", "inverted", "normed", "turned", "copied", "logits", "biased"))
        rows_out = [sem("rows_out0"), sem("rows_out1")]
        block = c.enter_context(nc.Block())

        @block.sync
        def _(sp):
            sp.dma_start(wf[:, :], s.inp["ffn_norm_w"].to_broadcast([P, D])).then_inc(router_in, 16)
            sp.dma_start(wr[:, :, 0:NG], s.inp["moe_w_group"].rearrange("(k p) n -> p k n", p=P)).then_inc(router_in, 16)
            sp.dma_start(wr[:, :, NG:], s.inp["moe_w_expert"].rearrange("(k p) n -> p k n", p=P)).then_inc(router_in, 16)
            sp.dma_start(br[:, 0:NG], s.inp["moe_b_group"].to_broadcast([P, NG])).then_inc(router_in, 16)
            sp.dma_start(br[:, NG:], s.inp["moe_b_expert"].to_broadcast([P, NE])).then_inc(router_in, 16)
            for t in range(0, TT, 2):
                sp.dma_start(s.x1[:, t:t + 2, :], s.inp["x"].rearrange("(t p) n -> p t n", p=P)[:, t:t + 2, :]).then_inc(x_in[t // 2], 16)
            for t in range(TT):
                sp.wait_ge(normed, t + 1)
                sp.dma_start(s.h_dram[t * P:(t + 1) * P, :], h[:, t % 2, :]).then_inc(rows_out[t % 2], 16)
            for u in range(2):
                sp.wait_ge(rows_out[u], 16 * TT // 2)

        @block.tensor
        def _(pe):
            for t in range(TT + 2):
                if t < TT:
                    if t >= 2:
                        pe.wait_ge(added, 2 * (t - 1))
                    for half in range(2):
                        out_products(pe, s, t, half, RWKV if t < EARLY else ATTENTION + RWKV).then_inc(done, 1)
                if t >= 2:
                    q = t - 2
                    if q == 0:
                        pe.wait_ge(router_in, 80)
                    pe.wait_ge(copied, q + 1)
                    if q >= 2:
                        pe.wait_ge(biased, q - 1)
                    for k in range(KD):
                        mm = pe.matmul(pl[:, q % 2, 0:NG + NE], hT[:, q % 2, k, :], wr[:, k, :], start=(k == 0), stop=(k == KD - 1))
                    mm.then_inc(logits, 1)
                if 1 <= t <= TT:
                    q = t - 1
                    pe.wait_ge(normed, q + 1)
                    if q:
                        pe.wait_ge(copied, q)
                    for k in range(KD):
                        mm = pe.transpose(pt[:, k, :], h[:, q % 2, k * P:(k + 1) * P], s.ident)
                    mm.then_inc(turned, 1)

        @block.vector
        def _(dve):
            dve.wait_ge(router_in, 80)
            for t in range(TT + 2):
                if t < TT:
                    if t % 2 == 0:
                        dve.wait_ge(x_in[t // 2], 16)
                    for half in range(2):
                        dve.wait_ge(done, 2 * t + half + 1)
                        x = s.x1[:, t, half * 512:(half + 1) * 512]
                        dve.tensor_tensor(x, s.ps_out[:, t % 2, half * 512:(half + 1) * 512], x, ALU.add).then_inc(added, 1)
                    dve.wait_ge(rooted, t + 1)
                    dve.reciprocal(st[:, t % 2, 2:3], st[:, t % 2, 1:2]).then_inc(inverted, 1)
                    dve.wait_ge(inverted, t + 1)
                    if t >= 2:
                        dve.wait_ge(turned, t - 1)
                        dve.wait_ge(rows_out[t % 2], 16 * (t // 2))
                    dve.scalar_tensor_tensor(out=h[:, t % 2, :], in0=s.x1[:, t, :], scalar=st[:, t % 2, 2:3], in1=wf[:, :],
                                             op0=ALU.mult, op1=ALU.mult).then_inc(normed, 1)
                if t >= 2:
                    q = t - 2
                    dve.wait_ge(logits, q + 1)
                    dve.tensor_tensor(s.logits[:, q, :], pl[:, q % 2, 0:NG + NE], br[:, :], ALU.add).then_inc(biased, 1)

        @block.scalar
        def _(act):
            for t in range(TT + 1):
                if t < TT:
                    act.wait_ge(added, 2 * t + 2)
                    if t >= 2:
                        act.wait_ge(inverted, t - 1)
                    if t:
                        act.wait_ge(summed, t)
                    act.activation(sq[:, :], s.x1[:, t, :], ACT.Square, accum_out=st[:, t % 2, 0:1]).then_inc(summed, 1)
                    act.wait_ge(summed, t + 1)
                    act.activation(st[:, t % 2, 1:2], st[:, t % 2, 0:1], ACT.Sqrt, bias=s.eps, scale=1.0 / D).then_inc(rooted, 1)
                if t:
                    q = t - 1
                    act.wait_ge(turned, q + 1)
                    if q >= 2:
                        act.wait_ge(logits, q - 1)
                    act.activation(hT[:, q % 2, :, :].rearrange("p a b -> p (a b)"), pt[:, :, :].rearrange("p a b -> p (a b)"),
                                   ACT.Copy).then_inc(copied, 1)


def routing(nc, s):
    with ExitStack() as c:
        def sb(name, shape, dt=F32):
            return c.enter_context(nc.sbuf_tensor("rt_" + name, shape, dt))

        def sem(name):
            return counter(nc, c, "rt_" + name)
        gmax, gmin, den, m1, m2, e2v = (sb(n, [P, TT]) for n in ("gmax", "gmin", "den", "m1", "m2", "e2"))
        t4, t4b, goh, sel = (sb(n, [P, TT, 4]) for n in ("t4", "t4b", "goh", "sel"))
        t44 = sb("t44", [P, TT, 4, 4])
        eoh = sb("eoh", [P, 2, TT, 4])
        oh = sb("oh", [P, 2, TT, NE])
        both = sb("both", [P, TT, NE])
        off = sb("off", [P, TT + 1, NE])
        rank = sb("rank", [P, TT, NE])
        t16 = sb("t16", [P, 2, TT, NE])
        cnt8 = sb("cnt8", [P, NE, 8])
        nb, ends, starts = (sb(n, [P, NE]) for n in ("nb", "ends", "starts"))
        b32 = sb("b32", [P, 32, NE])
        be = sb("be", [P, 32])
        bei = s.blk
        slotf = sb("slotf", [P, 2, TT])
        zeros = sb("zeros", [P, 32], I32)
        toki = sb("toki", [P, TT], I32)
        ps = c.enter_context(nc.psum_tensor("rt_ps", [P, 2, 512], F32))
        step, expd, stacked, ranked, zeroed, cleared, tok_ready = (
            sem(n) for n in ("step", "exp", "stacked", "ranked", "zeroed", "cleared", "tok"))
        scattered = dma_counter(nc, c, "rt_scattered")
        nc.all_engine_barrier()
        block = c.enter_context(nc.Block())
        gl, el = s.logits[:, :, 0:NG], s.logits[:, :, NG:]
        iota4 = s.iota[:, 0:4]

        def b3(ap, shape):
            return ap.to_broadcast(shape)

        @block.vector
        def _(dve):
            n = 0

            def link(ins):
                nonlocal n
                n += 1
                ins.then_inc(step, 1)
                dve.wait_ge(step, n + ONE)

            def first_max(vals, peak, onehot):
                link(dve.tensor_reduce(peak, vals, AX.X, ALU.max))
                link(dve.tensor_tensor(t4[:, :, :], vals, b3(peak.unsqueeze(2), [P, TT, 4]), ALU.is_equal))
                link(dve.tensor_scalar(t4[:, :, :], t4[:, :, :], -4.0, 4.0, ALU.mult, ALU.add))
                link(dve.tensor_tensor(t4[:, :, :], t4[:, :, :], b3(iota4.unsqueeze(1), [P, TT, 4]), ALU.add))
                link(dve.tensor_reduce(gmin[:, :], t4[:, :, :], AX.X, ALU.min))
                link(dve.tensor_tensor(onehot, b3(gmin[:, :].unsqueeze(2), [P, TT, 4]), b3(iota4.unsqueeze(1), [P, TT, 4]), ALU.is_equal))

            dve.memset(zeros[:, :], 0).then_inc(zeroed, 1)
            dve.tensor_copy(toki[:, :], s.token).then_inc(tok_ready, 1)
            first_max(gl, gmax[:, :], goh[:, :, :])
            link(dve.tensor_tensor(t4b[:, :, :], gl, b3(gmax[:, :].unsqueeze(2), [P, TT, 4]), ALU.subtract))
            dve.wait_ge(expd, 1 + ONE)
            link(dve.tensor_reduce(den[:, :], t4b[:, :, :], AX.X, ALU.add))
            link(dve.tensor_tensor(t44[:, :, :, :], el.rearrange("p t (g e) -> p t e g", g=4),
                                   b3(goh[:, :, :].unsqueeze(2), [P, TT, 4, 4]), ALU.mult))
            link(dve.tensor_reduce(sel[:, :, :], t44[:, :, :, :], AX.X, ALU.add))
            first_max(sel[:, :, :], m1[:, :], eoh[:, 0, :, :])
            link(dve.scalar_tensor_tensor(out=sel[:, :, :], in0=eoh[:, 0, :, :], scalar=NEG, in1=sel[:, :, :], op0=ALU.mult, op1=ALU.add))
            first_max(sel[:, :, :], m2[:, :], eoh[:, 1, :, :])
            link(dve.tensor_tensor(e2v[:, :], m2[:, :], m1[:, :], ALU.subtract))
            dve.wait_ge(expd, 2 + ONE)
            link(dve.tensor_scalar(m1[:, :], e2v[:, :], 1.0, None, ALU.add))
            link(dve.tensor_tensor(m1[:, :], m1[:, :], den[:, :], ALU.mult))
            link(dve.reciprocal(s.wt[:, 0, :], m1[:, :]))
            link(dve.tensor_tensor(s.wt[:, 1, :], s.wt[:, 0, :], e2v[:, :], ALU.mult))
            for k in range(2):
                link(dve.tensor_tensor(oh[:, k, :, :].rearrange("p t (g e) -> p t g e", g=4),
                                       b3(goh[:, :, :].unsqueeze(3), [P, TT, 4, 4]),
                                       b3(eoh[:, k, :, :].unsqueeze(2), [P, TT, 4, 4]), ALU.mult))
            link(dve.tensor_tensor(both[:, :, :], oh[:, 0, :, :], oh[:, 1, :, :], ALU.add))
            dve.sem_inc(stacked, 1)
            link(dve.memset(off[:, 0, :], 0.0))
            dve.wait_ge(ranked, 1 + ONE)
            for t in range(TT):
                link(dve.tensor_tensor(off[:, t + 1, :], ps[:, 1, t * NE:(t + 1) * NE], off[:, t, :], ALU.add))
            link(dve.tensor_tensor(cnt8[:, :, :], b3(off[:, TT, :].unsqueeze(2), [P, NE, 8]), b3(s.blk128.unsqueeze(1), [P, NE, 8]), ALU.is_gt))
            link(dve.tensor_reduce(nb[:, :], cnt8[:, :, :], AX.X, ALU.add))
            link(dve.tensor_tensor_scan(ends[:, :], s.ones[:, 0:NE], nb[:, :], 0.0, ALU.mult, ALU.add))
            link(dve.tensor_tensor(starts[:, :], ends[:, :], nb[:, :], ALU.subtract))
            link(dve.tensor_tensor(b32[:, :, :], b3(ends[:, :].unsqueeze(1), [P, 32, NE]), b3(s.iota.unsqueeze(2), [P, 32, NE]), ALU.is_le))
            link(dve.tensor_reduce(be[:, :], b32[:, :, :], AX.X, ALU.add))
            link(dve.tensor_scalar(bei[:, :], be[:, :], float(NE - 1), None, ALU.min))
            link(dve.tensor_copy(bei[:, 31:32], ends[:, NE - 1:NE]))
            link(dve.tensor_tensor(rank[:, :, :], ps[:, 0, 0:TT * NE].rearrange("p (t e) -> p t e", e=NE), off[:, 0:TT, :], ALU.add))
            link(dve.scalar_tensor_tensor(out=rank[:, :, :], in0=b3(starts[:, :].unsqueeze(1), [P, TT, NE]), scalar=float(P),
                                          in1=rank[:, :, :], op0=ALU.mult, op1=ALU.add))
            link(dve.tensor_tensor(t16[:, :, :, :], oh[:, :, :, :], b3(rank[:, :, :].unsqueeze(1), [P, 2, TT, NE]), ALU.mult))
            link(dve.tensor_reduce(slotf[:, :, :], t16[:, :, :, :], AX.X, ALU.add))
            link(dve.tensor_copy(s.slot[:, :, :], slotf[:, :, :]))
            dve.sem_inc(stacked, 1)

        @block.scalar
        def _(act):
            act.wait_ge(step, 7 + ONE)
            act.activation(t4b[:, :, :], t4b[:, :, :], ACT.Exp).then_inc(expd, 1)
            act.wait_ge(step, 24 + ONE)
            act.activation(e2v[:, :], e2v[:, :], ACT.Exp).then_inc(expd, 1)

        @block.tensor
        def _(pe):
            pe.wait_ge(stacked, 1 + ONE)
            flat = both[:, :, :].rearrange("p t e -> p (t e)")
            pe.matmul(ps[:, 0, 0:TT * NE], s.before, flat, start=True, stop=True)
            pe.matmul(ps[:, 1, 0:TT * NE], s.ones, flat, start=True, stop=True).then_inc(ranked, 1)

        @block.sync
        def _(sp):
            sp.wait_ge(zeroed, 1 + ONE)
            sp.dma_start(s.tok_dram.rearrange("(p n) o -> p (n o)", p=P), zeros[:, :]).then_inc(cleared, 16)
            sp.wait_ge(cleared, 16 + ONE)
            sp.wait_ge(stacked, 2 + ONE)
            e = sp.value_load(s.blk[0:1, 0:1], min_val=0, max_val=NE - 1)
            for load in expert_loads(s, e, 0):
                load(sp)

        @block.gpsimd
        def _(pool):
            pool.wait_ge(cleared, 16 + ONE)
            pool.wait_ge(tok_ready, 1 + ONE)
            pool.wait_ge(stacked, 2 + ONE)
            for k in range(2):
                for t in range(TT):
                    pool.indirect_dma_start(out=s.tok_dram, out_offset=bass.IndirectOffsetOnAxis(ap=s.slot[:, k, t:t + 1], axis=0),
                                            in_=toki[:, t:t + 1], in_offset=None).then_inc(scattered, 16)
            pool.wait_ge(scattered, 16 * 2 * TT)


def expert_loads(s, e, u):
    def load(dst, name, done):
        return lambda eng: eng.dma_start(dst, s.inp[name].rearrange("e (k p) f -> e p k f", p=P)[ds(e, 1)]
                                         .rearrange("o p k f -> p (o k) f")).then_inc(done, 16)
    return (load(s.wg[:, u, :, :], "moe_w_gate", s.wg_in[u]), load(s.wu[:, u, :, :], "moe_w_up", s.wu_in[u]),
            load(s.wd[:, u, :, :], "moe_w_down", s.wd_in[u]))


def experts(nc, s):
    with ExitStack() as c:
        def sb(name, shape, dt=F32):
            return c.enter_context(nc.sbuf_tensor("ex_" + name, shape, dt))

        def sem(name):
            return counter(nc, c, "ex_" + name)
        wg, wu, wd = s.wg, s.wu, s.wd
        idx = sb("idx", [P, 2], I32)
        x = s.proj[:, 16:18, :]
        xT = s.proj[:, 18:20, :].rearrange("p a (k t) -> p a k t", k=KD)
        sg = sb("sg", [P, FF])
        hid = sb("hid", [P, FF])
        hT = sb("hT", [P, KF, P])
        y = sb("y", [P, D])
        spare = sb("spare", [P, 1])
        act_spare = sb("act_spare", [P, 1])
        pt = c.enter_context(nc.psum_tensor("ex_pt", [P, 2, 512], F32))
        ph = c.enter_context(nc.psum_tensor("ex_ph", [P, 512], F32))
        pg = c.enter_context(nc.psum_tensor("ex_pg", [P, 512], F32))
        pu = c.enter_context(nc.psum_tensor("ex_pu", [P, 512], F32))
        py = c.enter_context(nc.psum_tensor("ex_py", [P, 2, 512], F32))
        spared = sem("spared")
        wg_in, wu_in, wd_in = s.wg_in, s.wu_in, s.wd_in
        idx_in, x_in = ([dma_counter(nc, c, f"ex_{n}{u}") for u in range(2)] for n in ("idx_in", "x_in"))
        x_turned, x_copied, gated, upped, silu, hidden, h_turned, h_copied, downed, y_half, y_out = (
            sem(n) for n in ("x_turned", "x_copied", "gated", "upped", "silu", "hidden", "h_turned", "h_copied", "downed", "y_half", "y_out"))
        nc.all_engine_barrier()
        block = c.enter_context(nc.Block())

        def used_blocks(eng):
            return eng.value_load(s.blk[0:1, 31:32], min_val=1, max_val=NBLK)

        def steps(eng, full, tail):
            n = used_blocks(eng)
            full(0, 0, 0)
            with eng.Fori(0, NBLK // 2) as i:
                for b, k, u in ((i * 2 + 1, i, 1), (i * 2 + 2, i + 1, 0)):
                    with eng.If(b < n):
                        full(b, k, u)
                    if tail is not None:
                        with eng.If(b == n):
                            tail(b, k, u)
            if tail is not None:
                with eng.If(n == NBLK):
                    tail(NBLK, NBLK // 2, 1)
            return n

        @block.sync
        def _(sp):
            sp.wait_ge(x_in[0], 16)
            e = sp.value_load(s.blk[0:1, 1:2], min_val=0, max_val=NE - 1)
            for load in expert_loads(s, e, 1):
                load(sp)
            n = used_blocks(sp)
            with sp.Fori(1, (NBLK + 1) // 2) as i:
                for u in range(2):
                    b = i * 2 + u
                    with sp.If(b < n):
                        e = sp.value_load(s.blk[0:1, ds(b, 1)], min_val=0, max_val=NE - 1)
                        for load, used in zip(expert_loads(s, e, u), (gated, upped, downed)):
                            sp.wait_ge(used, b - 1 + ONE)
                            load(sp)

        @block.gpsimd
        def _(pool):
            tok = s.tok_dram.rearrange("(b p) o -> b p o", p=P)

            def gather(b, k, u):
                if not isinstance(b, int):
                    pool.wait_ge(x_turned, b - 1 + ONE)
                pool.dma_start(idx[:, u:u + 1], tok[ds(b, 1)].rearrange("a p o -> p (a o)")).then_inc(idx_in[u], 16)
                pool.wait_ge(idx_in[u], k * 16 + 16)
                pool.wait_ge(spared, b + ONE)
                pool.tensor_tensor(spare[:, 0:1], s.eps, s.eps, ALU.add).then_inc(spared, 1)
                pool.indirect_dma_start(out=x[:, u, :], out_offset=None, in_=s.h_dram,
                                        in_offset=bass.IndirectOffsetOnAxis(ap=idx[:, u:u + 1], axis=0)).then_inc(x_in[u], 16)
            steps(pool, gather, gather)

        @block.tensor
        def _(pe):
            def turn_x(b, k, u):
                pe.wait_ge(x_in[u], k * 16 + 16)
                pe.wait_ge(x_copied, b + ONE)
                for j in range(KD):
                    mm = pe.transpose(pt[:, j // 4, (j % 4) * P:(j % 4 + 1) * P], x[:, u, j * P:(j + 1) * P], s.ident)
                mm.then_inc(x_turned, 1)

            def turn_h(b):
                pe.wait_ge(hidden, b + 1 + ONE)
                pe.wait_ge(h_copied, b + ONE)
                for j in range(KF):
                    mm = pe.transpose(ph[:, j * P:(j + 1) * P], hid[:, j * P:(j + 1) * P], s.ident)
                mm.then_inc(h_turned, 1)

            def down(b, k, u):
                pe.wait_ge(h_copied, b + 1 + ONE)
                pe.wait_ge(wd_in[u], k * 16 + 16 + ONE)
                pe.wait_ge(y_half, b * 2 + ONE)
                for half in range(2):
                    for j in range(KF):
                        mm = pe.matmul(py[:, half, :], hT[:, j, :], wd[:, u, j, half * 512:(half + 1) * 512],
                                       start=(j == 0), stop=(j == KF - 1))
                mm.then_inc(downed, 1)

            def full(b, k, u):
                first = isinstance(b, int)
                if first:
                    turn_x(0, 0, 0)
                pe.wait_ge(x_copied, b + 1 + ONE)
                pe.wait_ge(wg_in[u], k * 16 + 16 + ONE)
                pe.wait_ge(silu, b + ONE)
                for j in range(KD):
                    mm = pe.matmul(pg[:, :], xT[:, u, j, :], wg[:, u, j, :], start=(j == 0), stop=(j == KD - 1))
                mm.then_inc(gated, 1)
                if not first:
                    turn_h(b - 1)
                pe.wait_ge(wu_in[u], k * 16 + 16 + ONE)
                pe.wait_ge(hidden, b + ONE)
                for j in range(KD):
                    mm = pe.matmul(pu[:, :], xT[:, u, j, :], wu[:, u, j, :], start=(j == 0), stop=(j == KD - 1))
                mm.then_inc(upped, 1)
                turn_x(b + 1, k + u, 1 - u)
                if not first:
                    down(b - 1, k - (1 - u), 1 - u)

            def tail(b, k, u):
                turn_h(b - 1)
                down(b - 1, k - (1 - u), 1 - u)
            steps(pe, full, tail)

        @block.scalar
        def _(act):
            y_rows = s.y_dram.rearrange("(b p) n -> b p n", p=P)

            def tail(b, k, u):
                act.wait_ge(h_turned, b + ONE)
                act.wait_ge(downed, b - 1 + ONE)
                act.activation(hT[:, :, :].rearrange("p a b -> p (a b)"), ph[:, :], ACT.Copy).then_inc(h_copied, 1)
                act.wait_ge(downed, b + ONE)
                act.wait_ge(y_out, (b - 1) * 16 + ONE)
                act.activation(y[:, 0:512], py[:, 0, :], ACT.Copy).then_inc(y_half, 1)
                act.wait_ge(y_half, b * 2 + ONE)
                act.dma_start(y_rows[ds(b - 1, 1)].rearrange("o p n -> p (o n)"), y[:, :]).then_inc(y_out, 16)

            def full(b, k, u):
                act.wait_ge(gated, b + 1 + ONE)
                act.wait_ge(hidden, b + ONE)
                act.activation(sg[:, :], pg[:, :], ACT.Silu).then_inc(silu, 1)
                if not isinstance(b, int):
                    tail(b, k, u)
            n = steps(act, full, tail)
            act.wait_ge(y_out, n * 16 + ONE)
            act.activation(act_spare[:, :], s.eps, ACT.Copy)

        @block.vector
        def _(dve):
            def copy_x(b, u):
                dve.wait_ge(x_turned, b + 1 + ONE)
                if not isinstance(b, int):
                    dve.wait_ge(upped, b - 1 + ONE)
                dve.tensor_copy(xT[:, u, :, :].rearrange("p a b -> p (a b)"), pt[:, :, :].rearrange("p a b -> p (a b)")).then_inc(x_copied, 1)

            def tail(b, k, u):
                dve.wait_ge(downed, b + ONE)
                dve.wait_ge(y_out, (b - 1) * 16 + ONE)
                dve.tensor_copy(y[:, 512:1024], py[:, 1, :]).then_inc(y_half, 1)

            def full(b, k, u):
                first = isinstance(b, int)
                if first:
                    copy_x(0, 0)
                dve.wait_ge(silu, b + 1 + ONE)
                dve.wait_ge(upped, b + 1 + ONE)
                dve.wait_ge(h_turned, b + ONE)
                dve.tensor_tensor(hid[:, :], pu[:, :], sg[:, :], ALU.mult).then_inc(hidden, 1)
                copy_x(b + 1, 1 - u)
                if not first:
                    tail(b, k, u)
            steps(dve, full, tail)


def combine(nc, s, out):
    with ExitStack() as c:
        rows = s.proj[:, 8:16, :].rearrange("p (t k) n -> p t k n", k=2)
        come = [[dma_counter(nc, c, f"cb_in{t}_{k}") for k in range(2)] for t in range(4)]
        added, out_done = (counter(nc, c, "cb_" + n) for n in ("added", "out_done"))
        nc.all_engine_barrier()
        block = c.enter_context(nc.Block())
        out_rows = out.rearrange("o (t p) n -> t p (o n)", p=P)

        @block.gpsimd
        def _(pool):
            for t in range(TT):
                if t >= 4:
                    pool.wait_ge(added, 2 * (t - 4) + 2 + ONE)
                for k in range(2):
                    pool.indirect_dma_start(out=rows[:, t % 4, k, :], out_offset=None, in_=s.y_dram,
                                            in_offset=bass.IndirectOffsetOnAxis(ap=s.slot[:, k, t:t + 1], axis=0)).then_inc(come[t % 4][k], 16)

        @block.vector
        def _(dve):
            for t in range(TT):
                for k in range(2):
                    dve.wait_ge(come[t % 4][k], 16 * (t // 4 + 1))
                    if k:
                        dve.wait_ge(added, 2 * t + 1 + ONE)
                    dve.scalar_tensor_tensor(out=s.x1[:, t, :], in0=rows[:, t % 4, k, :], scalar=s.wt[:, k, t:t + 1], in1=s.x1[:, t, :],
                                             op0=ALU.mult, op1=ALU.add).then_inc(added, 1)

        @block.sync
        def _(sp):
            for t in range(TT):
                sp.wait_ge(added, 2 * t + 2 + ONE)
                sp.dma_start(out_rows[t], s.x1[:, t, :]).then_inc(out_done, 16)
            sp.wait_ge(out_done, 16 * TT + ONE)




def hybrid_layer(nc, inp, consts, params, out):
    def dram(name, shape, dt=F32):
        return nc.dram_tensor(name, shape, dt, kind="Internal").ap()
    s = Shared()
    s.inp = inp
    s.bias_dram = dram("bias_table", (8, GRID_W, 15, GRID_W))
    s.h_dram = dram("ffn_rows", (SEQ, D))
    s.y_dram = dram("expert_rows", (NBLK * P, D))
    s.tok_dram = dram("slot_tokens", (32 * P, 1), I32)
    top = ExitStack()
    cst = top.enter_context(nc.sbuf_tensor("cst", [P, NCC], F32))
    par = top.enter_context(nc.sbuf_tensor("par", [P, NPC], F32))
    s.par = lambda name, n: par[:, PCOL[name]:PCOL[name] + n]

    def const(name):
        return cst[:, CCOL[name]:CCOL[name] + CCOLS[name]]
    s.ident, s.pair_ones, s.ones, s.before, s.fold = (const(n) for n in ("ident", "pair_ones", "ones", "before", "fold"))
    s.eps, s.gn_eps, s.iota, s.blk128, s.token = (const(n) for n in ("eps", "gn_eps", "iota", "blk128", "token"))
    s.l_mask = [const("l_mask_f"), const("l_mask_b")]
    s.x_mask = [const("x_mask_f"), const("x_mask_b")]
    with top:
        params_in = top.enter_context(nc.semaphore("params_in"))
        s.kv_loaded = top.enter_context(nc.semaphore("kv_loaded"))
        s.mixT = top.enter_context(nc.sbuf_tensor("mixT", [P, KD, SEQ], F32))
        s.kv_w = s.mixT[:, 0:4, :].rearrange("p a n -> p (a n)").rearrange("p (k n) -> p k n", k=KD)
        with nc.Block() as block:
            @block.sync
            def _(sp):
                sp.dma_start(cst[:, :], consts).then_inc(params_in, 16)
                sp.dma_start(par[:, :], params).then_inc(params_in, 16)
                sp.dma_start(s.kv_w, s.inp["w_mem_kv"].rearrange("(k p) n -> p k n", p=P)).then_inc(s.kv_loaded, 16)
                sp.wait_ge(params_in, 32)
        s.proj = top.enter_context(nc.sbuf_tensor("proj", [P, C_ALL, SEQ], F32))
        with ExitStack() as c_mem:
            s.mkT = c_mem.enter_context(nc.sbuf_tensor("mkT", [P, 2, NMEM], F32))
            s.mv = c_mem.enter_context(nc.sbuf_tensor("mv", [P, 2, 256], F32))
            with ExitStack() as c:
                s.memT = c.enter_context(nc.sbuf_tensor("memT", [P, KD, NMEM], F32))
                norm_transpose(nc, s, inp["mem"].rearrange("(t p) n -> t p n", p=P), 2, s.memT, "mem_w", 4, "m")
                memory_kv(nc, s)
            with ExitStack() as c:
                s.hT = c.enter_context(nc.sbuf_tensor("hT", [P, KD, SEQ], F32))
                norm_transpose(nc, s, inp["x"].rearrange("(t p) n -> t p n", p=P), TT, s.hT, "attn_w", 0, "x")
                projection(nc, s)
            attention(nc, s, memory=True)
            attention(nc, s, memory=False)
        s.x1 = s.proj[:, 0:TT, :]
        s.logits = top.enter_context(nc.sbuf_tensor("logits", [P, TT, NG + NE], F32))
        with ExitStack() as c_mix:
            s.extra = c_mix.enter_context(nc.sbuf_tensor("extra", [P, 6, SEQ], F32))
            s.ec = c_mix.enter_context(nc.sbuf_tensor("ec", [P, 4, NCH], F32))
            gates(nc, s)
            scan(nc, s)
            s.w_out = c_mix.enter_context(nc.sbuf_tensor("w_out", [P, KD, D], F32))
            s.w_out_in = [c_mix.enter_context(nc.semaphore(f"w_out_in{a}")) for a in range(2)]
            s.ps_out = c_mix.enter_context(nc.psum_tensor("ps_out", [P, 2, D], F32))
            rwkv_out(nc, s)
            out_projection_router(nc, s)
        with nc.Block() as block:
            @block.gpsimd
            def _(pool):
                pool.sem_clear(range(params_in.num + 1, 256))
        s.wt = top.enter_context(nc.sbuf_tensor("wt", [P, 2, TT], F32))
        s.slot = top.enter_context(nc.sbuf_tensor("slot", [P, 2, TT], I32))
        s.blk = top.enter_context(nc.sbuf_tensor("blk", [P, 32], I32))
        s.wg = s.mixT[:, :, :].rearrange("p (u a) n -> p u (a n)", u=2).rearrange("p u (k f) -> p u k f", k=KD)
        s.wu = s.proj[:, TT:TT + KD, :].rearrange("p (u a) n -> p u (a n)", u=2).rearrange("p u (k f) -> p u k f", k=KD)
        s.wd = top.enter_context(nc.sbuf_tensor("wd", [P, 2, KF, D], F32))
        s.wg_in, s.wu_in, s.wd_in = ([counter(nc, top, f"{name}{u}") for u in range(2)] for name in ("wg_in", "wu_in", "wd_in"))
        routing(nc, s)
        experts(nc, s)
        combine(nc, s, out)


def constants(np):
    i, j = np.arange(P)[:, None], np.arange(P)[None, :]
    c = np.zeros((P, NCC), np.float32)

    def put(name, v):
        c[:, CCOL[name]:CCOL[name] + CCOLS[name]] = v
    put("ident", i == j)
    put("pair_ones", i // HD == j // HD)
    put("ones", 1)
    put("before", i < j)
    put("fold", i % HD == np.arange(HD)[None, :])
    put("eps", RMS_EPS)
    put("gn_eps", GN_EPS)
    same = i // HD == j // HD
    for name, before in (("f", lambda a, b: a < b), ("b", lambda a, b: a > b)):
        strict, incl = same & before(i, j), same & (before(i, j) | (i == j))
        put("l_mask_" + name, np.concatenate([-1.0 * (strict & (i // 16 == j // 16)), incl, strict, incl], 1))
        strict = same & before(j, i)
        b16, b32 = i // 16 == j // 16, i // 32 == j // 32
        put("x_mask_" + name, -1.0 * np.concatenate([strict & b16, strict & ~b16 & b32, strict & ~b32], 1))
    put("iota", np.arange(32)[None, :])
    put("blk128", P * np.arange(8)[None, :])
    put("token", i + P * np.arange(8)[None, :])
    return c


_INS = ['x', 'mem', 'w_in', 'na_rpb', 'rw_w2', 'rw_a2', 'rw_g2', 'w_mem_kv', 'w_out', 'ffn_norm_w', 'moe_w_group',
        'moe_b_group', 'moe_w_expert', 'moe_b_expert', 'moe_w_gate', 'moe_w_up', 'moe_w_down']


def kernel(**inputs):
    import numpy as _np
    import concourse.bacc as _bacc
    from concourse import mybir as _mybir
    from concourse.bass_utils import run_bass_kernel_spmd as _run

    nc = _bacc.Bacc("TRN2", target_bir_lowering=False, num_devices=1)

    def cols(name, reps=1):
        a = _np.asarray(inputs[name]).reshape(-1)
        return _np.concatenate([a] * reps).reshape(-1, P).T
    params = _np.concatenate([
        cols('attn_norm_w'), cols('mem_norm_w'), cols('na_q_norm_w', 2), cols('na_k_norm_w', 2), cols('mem_q_norm_w', 2),
        cols('mem_k_norm_w', 2), cols('rw_mu_prev'), cols('rw_mu_next'), cols('rw_w0'), cols('rw_a0'), cols('rw_k_k'),
        cols('rw_k_a'), cols('rw_r_k'), cols('rw_ln_w'), cols('rw_ln_b')], axis=1)
    neg_fill = _np.full((GRID_W, 15, GRID_W), NEG, _np.float32)
    arrays, aps = {}, {}

    def give(name, a):
        a = _np.ascontiguousarray(a)
        arrays[f"in_{name}"] = a
        return nc.dram_tensor(f"in_{name}", a.shape, _mybir.dt.from_np(a.dtype), kind="ExternalInput").ap()
    for name in _INS:
        a = _np.asarray(inputs[name])
        aps[name] = give(name, a if a.ndim == 2 else a[0])
    aps['neg_fill'] = give("neg_fill", neg_fill)
    consts, par = give("consts", constants(_np)), give("params", params)
    out = nc.dram_tensor("out", (1, SEQ, D), _mybir.dt.float32, kind="ExternalOutput").ap()
    hybrid_layer(nc, aps, consts, par, out)
    r = _run(nc, [arrays], core_ids=[0])
    return r.results[0]["out"]
```
